# Optimizing a Trainium2 kernel written in Bass

```python
import jax, jax.numpy as jnp
from jax import lax
import numpy as np
import math

D_MODEL = 1024
BATCH = 1
SEQ = 256
DEPTH = 2

N_META = 16
BLOCK = 128
SSD_HEADS = 8
SSD_HEAD_DIM = 64
SSD_D = SSD_HEADS * SSD_HEAD_DIM
SSD_GROUPS = 2
SSD_STATE = 64
SSD_CONV = 4
SSD_CONV_DIM = SSD_D + 2 * SSD_GROUPS * SSD_STATE
FOX_HEADS = 4
FOX_HEAD_DIM = 64
FOX_D = FOX_HEADS * FOX_HEAD_DIM
MLA_HEADS = 4
MLA_Q_LORA = 256
MLA_KV_LORA = 128
MLA_NOPE = 64
MLA_ROPE = 32
MLA_V = 64
MLA_D = MLA_HEADS * MLA_V
ROPE_THETA = 10000.0
D_MIX = SSD_D + FOX_D + MLA_D
IN_SIZES = [SSD_D, SSD_CONV_DIM, SSD_HEADS,
            FOX_D, FOX_D, FOX_D, FOX_HEADS,
            MLA_Q_LORA, MLA_KV_LORA, MLA_ROPE]
N_IN = sum(IN_SIZES)
IN_SPLITS = [int(s) for s in np.cumsum(IN_SIZES)[:-1]]
D_FF = 2816
ALPHA = (2 * DEPTH) ** 0.25
BETA = (8 * DEPTH) ** -0.25
EPS = 1e-5


def layer_norm(x, g, b):
    xf = x.astype(jnp.float32)
    mu = jnp.mean(xf, -1, keepdims=True)
    var = jnp.mean(jnp.square(xf - mu), -1, keepdims=True)
    return ((xf - mu) * lax.rsqrt(var + EPS) * g + b).astype(x.dtype)

def rms_norm(x, g):
    xf = x.astype(jnp.float32)
    y = xf * lax.rsqrt(jnp.mean(jnp.square(xf), -1, keepdims=True) + EPS)
    return (y * g).astype(x.dtype)

def swiglu(x, w_gate, w_up, w_down):
    return (jax.nn.silu(x @ w_gate) * (x @ w_up)) @ w_down

def rope(x, cos, sin):
    x1, x2 = jnp.split(x.astype(jnp.float32), 2, axis=-1)
    return jnp.concatenate([x1 * cos - x2 * sin, x2 * cos + x1 * sin], -1).astype(x.dtype)

def block_edges(total):
    return sorted(set([0] + list(range(N_META, total, BLOCK)) + [total]))

def blocked_causal_attention(logits_fn, v):
    total = v.shape[1]
    outs = []
    edges = block_edges(total)
    for q0, q1 in zip(edges[:-1], edges[1:]):
        s = logits_fn(q0, q1).astype(jnp.float32)
        causal = jnp.arange(q1)[None, :] <= jnp.arange(q0, q1)[:, None]
        s = jnp.where(causal, s, -jnp.inf)
        p = jax.nn.softmax(s, axis=-1).astype(v.dtype)
        outs.append(jnp.einsum('bhqk,bkhd->bqhd', p, v[:, :q1]))
    return jnp.concatenate(outs, axis=1)

def causal_depthwise_conv(x, w, bias):
    out = lax.conv_general_dilated(
        x, w[:, None, :], window_strides=(1,), padding=[(SSD_CONV - 1, 0)],
        dimension_numbers=('NWC', 'WIO', 'NWC'), feature_group_count=x.shape[-1])
    return out + bias

def ssd_chunked(x, dt, A, Bm, Cm):
    b, l, h, p = x.shape
    n = Bm.shape[-1]
    nc = l // BLOCK
    x = x.reshape(b, nc, BLOCK, h, p)
    dt = dt.reshape(b, nc, BLOCK, h)
    Bm = Bm.reshape(b, nc, BLOCK, h, n)
    Cm = Cm.reshape(b, nc, BLOCK, h, n)
    a = jnp.moveaxis(dt * A, -1, 1)
    a_cum = jnp.cumsum(a, axis=-1)
    xdt = x * dt[..., None]
    idx = jnp.arange(BLOCK)
    causal = idx[:, None] >= idx[None, :]
    seg = jnp.exp(jnp.where(causal, a_cum[..., :, None] - a_cum[..., None, :], -jnp.inf))
    cb = jnp.einsum('bclhn,bcshn->bhcls', Cm, Bm)
    y_diag = jnp.einsum('bhcls,bcshp->bclhp', cb * seg, xdt)
    decay_states = jnp.exp(a_cum[..., -1:] - a_cum)
    states = jnp.einsum('bclhn,bhcl,bclhp->bchpn', Bm, decay_states, xdt)
    chunk_decay = jnp.exp(a_cum[..., -1])

    def step(s, inp):
        st, dec = inp
        return s * dec[..., None, None] + st, s

    init = jnp.zeros((b, h, p, n), x.dtype)
    _, prev = lax.scan(step, init, (jnp.moveaxis(states, 1, 0), jnp.moveaxis(chunk_decay, 2, 0)))
    prev = jnp.moveaxis(prev, 0, 1)
    y_off = jnp.einsum('bclhn,bchpn,bhcl->bclhp', Cm, prev, jnp.exp(a_cum))
    return (y_diag + y_off).reshape(b, l, h, p)

def ssd_mixer(z, xbc, dt_raw, conv_w, conv_b, dt_bias, a_log, d_skip, norm_g):
    b, L, _ = xbc.shape
    f32 = jnp.float32
    xbc = jax.nn.silu(causal_depthwise_conv(xbc, conv_w, conv_b)).astype(f32)
    xs, Bm, Cm = jnp.split(xbc, [SSD_D, SSD_D + SSD_GROUPS * SSD_STATE], axis=-1)
    xs = xs.reshape(b, L, SSD_HEADS, SSD_HEAD_DIM)
    rep = SSD_HEADS // SSD_GROUPS
    Bm = jnp.repeat(Bm.reshape(b, L, SSD_GROUPS, SSD_STATE), rep, axis=2)
    Cm = jnp.repeat(Cm.reshape(b, L, SSD_GROUPS, SSD_STATE), rep, axis=2)
    dt = jax.nn.softplus(dt_raw.astype(f32) + dt_bias.astype(f32))
    A = -jnp.exp(a_log.astype(f32))
    pad = (-L) % BLOCK
    padf = lambda t: jnp.pad(t, ((0, 0), (pad, 0)) + ((0, 0),) * (t.ndim - 2))
    y = ssd_chunked(padf(xs), padf(dt), A, padf(Bm), padf(Cm))[:, pad:]
    y = y + d_skip.astype(f32)[:, None] * xs
    y = y.reshape(b, L, SSD_D) * jax.nn.silu(z.astype(f32))
    y = rms_norm(y.reshape(b, L, SSD_GROUPS, SSD_D // SSD_GROUPS), 1.0).reshape(b, L, SSD_D) * norm_g
    return y.astype(z.dtype)

def fox_mixer(q, k, v, f_raw, f_b):
    b, L, _ = q.shape
    q = q.reshape(b, L, FOX_HEADS, FOX_HEAD_DIM)
    k = k.reshape(b, L, FOX_HEADS, FOX_HEAD_DIM)
    v = v.reshape(b, L, FOX_HEADS, FOX_HEAD_DIM)
    log_f = jax.nn.log_sigmoid(f_raw.astype(jnp.float32) + f_b.astype(jnp.float32))
    c = jnp.cumsum(log_f, axis=1).transpose(0, 2, 1)
    scale = FOX_HEAD_DIM ** -0.5

    def logits(q0, q1):
        s = jnp.einsum('bqhd,bkhd->bhqk', q[:, q0:q1], k[:, :q1]).astype(jnp.float32) * scale
        return s + (c[:, :, q0:q1, None] - c[:, :, None, :q1])

    return blocked_causal_attention(logits, v).reshape(b, L, FOX_D)

def mla_mixer(cq, ckv, k_rope, q_norm_g, w_uq, kv_norm_g, w_ukv, cos, sin):
    b, L, _ = cq.shape
    qh = (rms_norm(cq, q_norm_g) @ w_uq).reshape(b, L, MLA_HEADS, MLA_NOPE + MLA_ROPE)
    q_nope, q_rope = qh[..., :MLA_NOPE], qh[..., MLA_NOPE:]
    q_rope = rope(q_rope, cos[None, :, None, :], sin[None, :, None, :])
    kv = (rms_norm(ckv, kv_norm_g) @ w_ukv).reshape(b, L, MLA_HEADS, MLA_NOPE + MLA_V)
    k_nope, v = kv[..., :MLA_NOPE], kv[..., MLA_NOPE:]
    k_rope = rope(k_rope, cos[None], sin[None])
    scale = (MLA_NOPE + MLA_ROPE) ** -0.5

    def logits(q0, q1):
        s = jnp.einsum('bqhd,bkhd->bhqk', q_nope[:, q0:q1], k_nope[:, :q1])
        s = s + jnp.einsum('bqhr,bkr->bhqk', q_rope[:, q0:q1], k_rope[:, :q1])
        return s * scale

    return blocked_causal_attention(logits, v).reshape(b, L, MLA_D)

def first_inputs(seed: int = 0) -> dict:
    key = jax.random.key(seed)
    ks = iter(jax.random.split(key, 48))
    f32 = jnp.float32
    Dm, F, NL = D_MODEL, D_FF, DEPTH

    def nrm(shape, scale):
        return jax.random.normal(next(ks), shape, f32) * scale

    def gain(shape):
        return 1.0 + nrm(shape, 0.02)

    u = jax.random.uniform(next(ks), (NL, SSD_HEADS), f32)
    dt0 = jnp.exp(u * (np.log(0.1) - np.log(0.001)) + np.log(0.001))
    dt_bias = dt0 + jnp.log(-jnp.expm1(-dt0))
    a_log = jnp.log(jax.random.uniform(next(ks), (NL, SSD_HEADS), f32, 1.0, 16.0))
    return {
        "x": nrm((BATCH, SEQ, Dm), 1.0),
        "meta": nrm((N_META, Dm), 1.0),
        "ffn1_w_gate": nrm((NL, Dm, F), Dm ** -0.5),
        "ffn1_w_up": nrm((NL, Dm, F), Dm ** -0.5),
        "ffn1_w_down": nrm((NL, F, Dm), F ** -0.5 * BETA),
        "ln1_g": gain((NL, Dm)),
        "ln1_b": nrm((NL, Dm), 0.02),
        "w_in": nrm((NL, Dm, N_IN), Dm ** -0.5),
        "conv_w": nrm((NL, SSD_CONV, SSD_CONV_DIM), SSD_CONV ** -0.5),
        "conv_b": nrm((NL, SSD_CONV_DIM), 0.02),
        "dt_bias": dt_bias,
        "a_log": a_log,
        "d_skip": gain((NL, SSD_HEADS)),
        "ssd_norm_g": gain((NL, SSD_D)),
        "fox_f_b": 3.0 + nrm((NL, FOX_HEADS), 0.5),
        "mla_q_norm_g": gain((NL, MLA_Q_LORA)),
        "mla_w_uq": nrm((NL, MLA_Q_LORA, MLA_HEADS * (MLA_NOPE + MLA_ROPE)), MLA_Q_LORA ** -0.5),
        "mla_kv_norm_g": gain((NL, MLA_KV_LORA)),
        "mla_w_ukv": nrm((NL, MLA_KV_LORA, MLA_HEADS * (MLA_NOPE + MLA_V)), MLA_KV_LORA ** -0.5),
        "w_out": nrm((NL, D_MIX, Dm), D_MIX ** -0.5 * BETA),
        "ln2_g": gain((NL, Dm)),
        "ln2_b": nrm((NL, Dm), 0.02),
        "ffn2_w_gate": nrm((NL, Dm, F), Dm ** -0.5),
        "ffn2_w_up": nrm((NL, Dm, F), Dm ** -0.5),
        "ffn2_w_down": nrm((NL, F, Dm), F ** -0.5 * BETA),
        "ln3_g": gain((NL, Dm)),
        "ln3_b": nrm((NL, Dm), 0.02),
    }

def first_block(x, meta, ffn1_w_gate, ffn1_w_up, ffn1_w_down, ln1_g, ln1_b, w_in,
              conv_w, conv_b, dt_bias, a_log, d_skip, ssd_norm_g, fox_f_b,
              mla_q_norm_g, mla_w_uq, mla_kv_norm_g, mla_w_ukv, w_out, ln2_g, ln2_b,
              ffn2_w_gate, ffn2_w_up, ffn2_w_down, ln3_g, ln3_b):
    b = x.shape[0]
    h = jnp.concatenate([jnp.broadcast_to(meta[None].astype(x.dtype), (b, N_META, D_MODEL)), x], axis=1)
    total = h.shape[1]
    pos = jnp.arange(total, dtype=jnp.float32)
    inv_freq = 1.0 / (ROPE_THETA ** (jnp.arange(0, MLA_ROPE, 2, dtype=jnp.float32) / MLA_ROPE))
    ang = pos[:, None] * inv_freq[None, :]
    cos, sin = jnp.cos(ang), jnp.sin(ang)

    for l in range(DEPTH):
        h = layer_norm(ALPHA * h + 0.5 * swiglu(h, ffn1_w_gate[l], ffn1_w_up[l], ffn1_w_down[l]),
                       ln1_g[l], ln1_b[l])
        proj = h @ w_in[l]
        (z, xbc, dt_raw, fq, fk, fv, f_raw, cq, ckv, k_rope) = jnp.split(proj, IN_SPLITS, axis=-1)
        y_ssd = ssd_mixer(z, xbc, dt_raw, conv_w[l], conv_b[l], dt_bias[l], a_log[l],
                          d_skip[l], ssd_norm_g[l])
        y_fox = fox_mixer(fq, fk, fv, f_raw, fox_f_b[l])
        y_mla = mla_mixer(cq, ckv, k_rope, mla_q_norm_g[l], mla_w_uq[l], mla_kv_norm_g[l],
                          mla_w_ukv[l], cos, sin)
        mix = jnp.concatenate([y_ssd, y_fox.astype(h.dtype), y_mla.astype(h.dtype)], axis=-1) @ w_out[l]
        h = layer_norm(ALPHA * h + mix, ln2_g[l], ln2_b[l])
        h = layer_norm(ALPHA * h + 0.5 * swiglu(h, ffn2_w_gate[l], ffn2_w_up[l], ffn2_w_down[l]),
                       ln3_g[l], ln3_b[l])
    return h[:, N_META:]


POOL_WIDTH = D_MODEL // 4
FOURIER_WIDTH = D_MODEL // 4
ATTN_WIDTH = D_MODEL // 2
POOL_WINDOWS = (2, 4, 8, 16)
N_POOL_GROUPS = len(POOL_WINDOWS)
POOL_GROUP_DIM = POOL_WIDTH // N_POOL_GROUPS
N_FOURIER_GROUPS = 4
FOURIER_GROUP_DIM = FOURIER_WIDTH // N_FOURIER_GROUPS
ATTN_HEADS = 4
ATTN_HEAD_DIM = ATTN_WIDTH // (2 * ATTN_HEADS)
ATTN_V_DIM = 2 * ATTN_HEAD_DIM
Q_BLOCK = 128
IN_COLS = POOL_WIDTH + FOURIER_WIDTH + 3 * ATTN_WIDTH
NORM_EPS = 1e-6


def alibi_slopes(n_heads):
    return jnp.array([2.0 ** (-8.0 * (i + 1) / n_heads) for i in range(n_heads)], dtype=jnp.float32)

def lambda_init_fn(layer_idx):
    return 0.8 - 0.6 * math.exp(-0.3 * layer_idx)

def rmsnorm(x, g):
    xf = x.astype(jnp.float32)
    y = xf * lax.rsqrt(jnp.mean(xf * xf, axis=-1, keepdims=True) + NORM_EPS)
    return (y * g.astype(jnp.float32)).astype(x.dtype)

def swiglu_2(x, w_gate, w_up, w_down):
    return (jax.nn.silu(x @ w_gate) * (x @ w_up)) @ w_down

def pool_mixer(a, pool_w, pool_scale):
    B, S, _ = a.shape
    af = a.reshape(B, S, N_POOL_GROUPS, POOL_GROUP_DIM).astype(jnp.float32)
    prefix = jnp.concatenate(
        [jnp.zeros((B, 1, N_POOL_GROUPS, POOL_GROUP_DIM), jnp.float32), jnp.cumsum(af, axis=1)], axis=1)
    t = jnp.arange(S)
    outs = []
    for g, w in enumerate(POOL_WINDOWS):
        left = w // 2
        right = w - 1 - left
        hi = jnp.minimum(t + right + 1, S)
        lo = jnp.maximum(t - left, 0)
        pg = prefix[:, :, g]
        win_sum = jnp.take(pg, hi, axis=1) - jnp.take(pg, lo, axis=1)
        cnt = (hi - lo).astype(jnp.float32)[None, :, None]
        outs.append(win_sum / cnt - af[:, :, g])
    m = jnp.stack(outs, axis=2).astype(a.dtype)
    y = jnp.einsum('bsgc,gcd->bsgd', m, pool_w).reshape(B, S, POOL_WIDTH)
    return y * pool_scale

def fourier_mixer(f, fourier_w):
    B, S, _ = f.shape
    f4 = f.reshape(B, S, N_FOURIER_GROUPS, FOURIER_GROUP_DIM).astype(jnp.float32)
    y = jnp.real(jnp.fft.fft2(f4, axes=(1, 3), norm='ortho'))
    y = y.astype(f.dtype).reshape(B, S, FOURIER_WIDTH)
    return y @ fourier_w

def diff_attention(q, k, v, lam, lam_init, head_norm):
    B, S = q.shape[0], q.shape[1]
    n_blk = S // Q_BLOCK
    scale = ATTN_HEAD_DIM ** -0.5
    slopes = alibi_slopes(ATTN_HEADS)
    kpos = jnp.arange(S, dtype=jnp.float32)
    qb = q.reshape(B, n_blk, Q_BLOCK, ATTN_HEADS, 2, ATTN_HEAD_DIM).transpose(1, 0, 2, 3, 4, 5)

    def one_block(args):
        q_blk, i = args
        qpos = (i * Q_BLOCK + jnp.arange(Q_BLOCK)).astype(jnp.float32)
        bias = -slopes[:, None, None] * jnp.abs(qpos[:, None] - kpos[None, :])
        s = jnp.einsum('bqhjd,bkhjd->bhjqk', q_blk, k).astype(jnp.float32) * scale + bias[None, :, None]
        p = jax.nn.softmax(s, axis=-1)
        attn = p[:, :, 0] - lam.astype(jnp.float32) * p[:, :, 1]
        return jnp.einsum('bhqk,bkhe->bqhe', attn.astype(v.dtype), v)

    o = lax.map(one_block, (qb, jnp.arange(n_blk)))
    o = o.transpose(1, 0, 2, 3, 4).reshape(B, S, ATTN_HEADS, ATTN_V_DIM)
    o = rmsnorm(o, head_norm.reshape(ATTN_HEADS, ATTN_V_DIM)) * (1.0 - lam_init)
    return o.reshape(B, S, ATTN_WIDTH)

def second_inputs(seed: int = 0) -> dict:
    key = jax.random.key(seed)
    ks = jax.random.split(key, 24)
    f32 = jnp.float32

    def nrm(k, shape, fan_in):
        return jax.random.normal(k, shape, f32) * (fan_in ** -0.5)

    def gain(k, shape):
        return 1.0 + 0.05 * jax.random.normal(k, shape, f32)

    return {
        "x": jax.random.normal(ks[0], (BATCH, SEQ, D_MODEL), f32),
        "ffn1_norm": gain(ks[1], (DEPTH, D_MODEL)),
        "ffn1_w_gate": nrm(ks[2], (DEPTH, D_MODEL, D_FF), D_MODEL),
        "ffn1_w_up": nrm(ks[3], (DEPTH, D_MODEL, D_FF), D_MODEL),
        "ffn1_w_down": nrm(ks[4], (DEPTH, D_FF, D_MODEL), D_FF),
        "mix_norm": gain(ks[5], (DEPTH, D_MODEL)),
        "w_in": nrm(ks[6], (DEPTH, D_MODEL, IN_COLS), D_MODEL),
        "pool_w": nrm(ks[7], (DEPTH, N_POOL_GROUPS, POOL_GROUP_DIM, POOL_GROUP_DIM), POOL_GROUP_DIM),
        "pool_scale": gain(ks[8], (DEPTH, POOL_WIDTH)),
        "fourier_w": nrm(ks[9], (DEPTH, FOURIER_WIDTH, FOURIER_WIDTH), FOURIER_WIDTH),
        "lam_q1": 0.1 * jax.random.normal(ks[10], (DEPTH, ATTN_HEAD_DIM), f32),
        "lam_k1": 0.1 * jax.random.normal(ks[11], (DEPTH, ATTN_HEAD_DIM), f32),
        "lam_q2": 0.1 * jax.random.normal(ks[12], (DEPTH, ATTN_HEAD_DIM), f32),
        "lam_k2": 0.1 * jax.random.normal(ks[13], (DEPTH, ATTN_HEAD_DIM), f32),
        "attn_head_norm": gain(ks[14], (DEPTH, ATTN_WIDTH)),
        "w_out": nrm(ks[15], (DEPTH, D_MODEL, D_MODEL), D_MODEL),
        "ffn2_norm": gain(ks[16], (DEPTH, D_MODEL)),
        "ffn2_w_gate": nrm(ks[17], (DEPTH, D_MODEL, D_FF), D_MODEL),
        "ffn2_w_up": nrm(ks[18], (DEPTH, D_MODEL, D_FF), D_MODEL),
        "ffn2_w_down": nrm(ks[19], (DEPTH, D_FF, D_MODEL), D_FF),
        "final_norm": gain(ks[20], (D_MODEL,)),
    }

def second_block(x, ffn1_norm, ffn1_w_gate, ffn1_w_up, ffn1_w_down, mix_norm, w_in, pool_w, pool_scale,
              fourier_w, lam_q1, lam_k1, lam_q2, lam_k2, attn_head_norm, w_out,
              ffn2_norm, ffn2_w_gate, ffn2_w_up, ffn2_w_down, final_norm):
    B, S, _ = x.shape
    c0 = POOL_WIDTH
    c1 = c0 + FOURIER_WIDTH
    c2 = c1 + ATTN_WIDTH
    c3 = c2 + ATTN_WIDTH
    for l in range(DEPTH):
        h = rmsnorm(x, ffn1_norm[l])
        x = x + 0.5 * swiglu_2(h, ffn1_w_gate[l], ffn1_w_up[l], ffn1_w_down[l])

        h = rmsnorm(x, mix_norm[l])
        p = h @ w_in[l]
        a = p[..., :c0]
        f = p[..., c0:c1]
        q = p[..., c1:c2].reshape(B, S, ATTN_HEADS, 2, ATTN_HEAD_DIM)
        k = p[..., c2:c3].reshape(B, S, ATTN_HEADS, 2, ATTN_HEAD_DIM)
        v = p[..., c3:].reshape(B, S, ATTN_HEADS, ATTN_V_DIM)

        lam_init = lambda_init_fn(l)
        lam = (jnp.exp(jnp.sum(lam_q1[l].astype(jnp.float32) * lam_k1[l].astype(jnp.float32)))
               - jnp.exp(jnp.sum(lam_q2[l].astype(jnp.float32) * lam_k2[l].astype(jnp.float32)))
               + lam_init)

        y_pool = pool_mixer(a, pool_w[l], pool_scale[l])
        y_four = fourier_mixer(f, fourier_w[l])
        y_attn = diff_attention(q, k, v, lam, lam_init, attn_head_norm[l]).astype(x.dtype)
        y = jnp.concatenate([y_pool, y_four, y_attn], axis=-1) @ w_out[l]
        x = x + y

        h = rmsnorm(x, ffn2_norm[l])
        x = x + 0.5 * swiglu_2(h, ffn2_w_gate[l], ffn2_w_up[l], ffn2_w_down[l])
    return rmsnorm(x, final_norm)


def setup_inputs(seed=0):
    out = dict(first_inputs(seed))
    for name, value in second_inputs(seed + 1).items():
        if name != "x":
            out[name + "_2"] = value
    return out


def reference(
    x, meta, ffn1_w_gate, ffn1_w_up, ffn1_w_down, ln1_g, ln1_b, w_in, conv_w, conv_b, dt_bias,
    a_log, d_skip, ssd_norm_g, fox_f_b, mla_q_norm_g, mla_w_uq, mla_kv_norm_g, mla_w_ukv, w_out,
    ln2_g, ln2_b, ffn2_w_gate, ffn2_w_up, ffn2_w_down, ln3_g, ln3_b, ffn1_norm_2, ffn1_w_gate_2,
    ffn1_w_up_2, ffn1_w_down_2, mix_norm_2, w_in_2, pool_w_2, pool_scale_2, fourier_w_2,
    lam_q1_2, lam_k1_2, lam_q2_2, lam_k2_2, attn_head_norm_2, w_out_2, ffn2_norm_2,
    ffn2_w_gate_2, ffn2_w_up_2, ffn2_w_down_2, final_norm_2,
):
    x = first_block(
        x, meta, ffn1_w_gate, ffn1_w_up, ffn1_w_down, ln1_g, ln1_b, w_in, conv_w, conv_b,
        dt_bias, a_log, d_skip, ssd_norm_g, fox_f_b, mla_q_norm_g, mla_w_uq, mla_kv_norm_g,
        mla_w_ukv, w_out, ln2_g, ln2_b, ffn2_w_gate, ffn2_w_up, ffn2_w_down, ln3_g, ln3_b,
    )
    return second_block(
        x, ffn1_norm_2, ffn1_w_gate_2, ffn1_w_up_2, ffn1_w_down_2, mix_norm_2, w_in_2, pool_w_2,
        pool_scale_2, fourier_w_2, lam_q1_2, lam_k1_2, lam_q2_2, lam_k2_2, attn_head_norm_2,
        w_out_2, ffn2_norm_2, ffn2_w_gate_2, ffn2_w_up_2, ffn2_w_down_2, final_norm_2,
    )


_drawn_inputs = setup_inputs


def setup_inputs(seed=0):
    import zlib

    import numpy as np

    out = dict(_drawn_inputs(seed))
    spreads = {}
    factors = {'conv_b': 3.887,
     'd_skip': 8.0,
     'ssd_norm_g': 5.646,
     'mla_q_norm_g': 8.0,
     'mla_kv_norm_g': 8.0,
     'lam_k1_2': 5.152,
     'lam_k2_2': 8.0}
    for name, (base, spread) in spreads.items():
        noise = np.random.default_rng([zlib.crc32(name.encode()), seed]).standard_normal(out[name].shape)
        drawn = base * np.exp(spread * noise) if base else spread * noise
        out[name] = __import__('jax').numpy.asarray(drawn.astype(out[name].dtype))
    for name, factor in factors.items():
        out[name] = (out[name] * factor).astype(out[name].dtype)
    return out
```

```python
from contextlib import ExitStack

import numpy as np

import concourse.bass as bass
from concourse import mybir

F32 = mybir.dt.float32
F32R = mybir.dt.float32r
ALU = mybir.AluOpType
ACT = mybir.ActivationFunctionType
AX_X = mybir.AxisListType.X

P = 128
D = 1024
KD = D // P
DEPTH = 2
SEQ = 256
N_META = 16
T1 = SEQ + N_META
T2 = SEQ
D_FF = 2816
NF = D_FF // P
HALF_F = NF // 2
ALPHA = (2 * DEPTH) ** 0.25
EPS1, EPS2 = 1e-5, 1e-6

W_NARROW = KD * P
W_WIDE = HALF_F * P
IN1, IN2, OUTB = 20, 16, 8
UP_PAIRS, DOWN_PAIRS = NF, KD
FFN_PAIRS = UP_PAIRS + DOWN_PAIRS
LAYER1_PAIRS = 2 * FFN_PAIRS + IN1 // 2 + OUTB // 2
LAYER2_PAIRS = 2 * FFN_PAIRS + IN2 // 2 + OUTB // 2
BLOCK2_PAIR0 = DEPTH * LAYER1_PAIRS
PAD_PAIRS = 2

Z0, XBC0, B_BLK, C_BLK, FQ0, FK0, FV0, CQ0, CKV, MISC = 0, 4, 8, 9, 10, 12, 14, 16, 18, 19
SSD_HEADS, FOX_HEADS, MLA_HEADS, HD, ROPE = 8, 4, 4, 64, 32
CONV = 4
ROW0 = 64
FROW0 = 96
MLA_SCALE = float(np.float32((HD + ROPE) ** -0.5))
FOX_SCALE = HD ** -0.5
MASK = -1e30
TILES = [(0, 128), (128, 128), (256, 16)]
TRI = [0, 272, 416]
TRI_W = [T1 - t for t, _ in TILES]
S_BANK = [(0, 0, 128), (0, 128, 256), (1, 0, T1)]

P1 = {}
_n = 0
for _name, _w in (("ln1g", 8), ("ln1b", 8), ("ln2g", 8), ("ln2b", 8), ("ln3g", 8), ("ln3b", 8), ("convw", 24),
                  ("convb", 6), ("dskip", 4), ("ssdg", 4), ("qg", 2), ("kvg", 1), ("rowbias", 1), ("rowsign", 1),
                  ("alog", 1), ("uq", 2 * 384), ("ukv", 512)):
    P1[_name] = _n
    _n += _w
P1_W = _n
P2 = {}
_n = 0
for _name, _w in (("mixg", 8), ("ffn2g", 8), ("nextg", 8), ("firstg", 8), ("pscale", 2), ("headg", 4), ("laminit", 1),
                  ("onemlam", 1), ("lamq", 128), ("lamk", 128), ("poolw", 128), ("fourw", 512)):
    P2[_name] = _n
    _n += _w
P2_W = _n
PRM_W = max(P1_W, P2_W)
ATT_HEADS = 4
POOL_WINDOWS = (2, 4, 8, 16)
ATT_SCALE = 64 ** -0.5

CC = {}
_n = 0
for _name, _w in (("ident", 128), ("onesD", 128), ("ones256", 128), ("ones128", 128), ("rot", 128), ("rep", 128),
                  ("reprot", 128), ("cos", T1), ("sin", T1), ("sel", 12 * 128), ("maskS", 128), ("maskA", 128),
                  ("eps1", 1), ("eps2", 1), ("one", 1), ("band", 4 * 2 * 256), ("cs", 512), ("ss", 512),
                  ("ccos", 128), ("csin", 128), ("absd", 512), ("slope", 4 * 128)):
    CC[_name] = _n
    _n += _w
CC_W = _n


def shape_constants():
    c = np.zeros((P, CC_W), np.float32)

    def put(name, a, rows=slice(0, P)):
        a = np.asarray(a, np.float64).astype(np.float32)
        c[rows, CC[name]:CC[name] + a.shape[1]] = a

    put("ident", np.eye(P))
    put("onesD", np.full((P, P), 1.0 / D))
    put("ones256", np.full((P, P), 1.0 / 256))
    put("ones128", np.full((P, P), 1.0 / 128))
    r32 = np.zeros((32, 32))
    for i in range(16):
        r32[16 + i, i] = -1.0
        r32[i, 16 + i] = 1.0
    put("rot", np.kron(np.eye(4), r32))
    put("rep", np.tile(np.eye(32), (1, 4)), slice(0, 32))
    put("reprot", np.tile(r32, (1, 4)), slice(0, 32))
    inv = (1.0 / (10000.0 ** (np.arange(0, ROPE, 2, dtype=np.float32) / np.float32(ROPE)))).astype(np.float32)
    ang = (np.arange(T1, dtype=np.float32)[:, None] * inv[None, :]).astype(np.float32).astype(np.float64)
    idx = (np.arange(P) % 32) % 16
    put("cos", np.cos(ang).T[idx])
    put("sin", np.sin(ang).T[idx])
    sel = np.zeros((P, 12, 128))
    for h in range(8):
        sel[ROW0 + h, h] = 1.0
    for h in range(4):
        sel[FROW0 + h, 8 + h] = -1.0 / FOX_SCALE
    put("sel", sel.reshape(P, -1))
    a = np.arange(P)
    put("maskS", np.where(a[None, :] < a[:, None], MASK, 0.0))
    put("maskA", np.where(a[None, :] > a[:, None], MASK, 0.0))
    put("eps1", np.full((P, 1), EPS1))
    put("eps2", np.full((P, 1), EPS2))
    put("one", np.ones((P, 1)))
    band = np.zeros((4, 256, 256))
    for g, w in enumerate(POOL_WINDOWS):
        for t in range(256):
            lo, hi = max(t - w // 2, 0), min(t + w - w // 2, 256)
            band[g, lo:hi, t] += 1.0 / (hi - lo)
            band[g, t, t] -= 1.0
    put("band", band.reshape(4, 2, P, 256).transpose(2, 0, 1, 3).reshape(P, -1))
    s = np.arange(256)
    ang = 2 * np.pi * ((s[:, None] * s[None, :]) % 256) / 256
    put("cs", np.cos(ang).reshape(2, P, 256).transpose(1, 0, 2).reshape(P, -1))
    put("ss", np.sin(ang).reshape(2, P, 256).transpose(1, 0, 2).reshape(P, -1))
    m = np.arange(64)
    ang = 2 * np.pi * ((m[:, None] * m[None, :]) % 64) / 64
    ortho = 1.0 / np.sqrt(256 * 64)
    put("ccos", np.kron(np.eye(2), np.cos(ang) * ortho))
    put("csin", np.kron(np.eye(2), -np.sin(ang) * ortho))
    q = np.arange(256)
    absd = np.abs(q[:, None] - q[None, :])
    put("absd", absd.reshape(2, P, 256).transpose(1, 0, 2).reshape(P, -1))
    slopes = [2.0 ** (-8.0 * (i + 1) / ATT_HEADS) for i in range(ATT_HEADS)]
    put("slope", np.concatenate([np.eye(P) * (-sl / ATT_SCALE) for sl in slopes], axis=1))
    return c


class Signal:

    def __init__(self, sem, per_layer, start):
        self.sem, self.per_layer, self.start = sem, per_layer, start

    def at(self, layer, n):
        return layer * self.per_layer + (n + self.start)


def build(nc, hidden0, w_up, w_down, w_in1, w_out1, w_in2, w_out2, prm1, prm2, consts, out):
    with ExitStack() as ctx:
        def sb(name, shape, dt=F32):
            return ctx.enter_context(nc.sbuf_tensor(name, shape, dt))

        def sem(name):
            return ctx.enter_context(nc.semaphore(name))

        def signal(name, per_layer, start=0):
            return Signal(sem(name), per_layer, start)

        raw = sb("raw", [P, 2, 2 * W_WIDE])
        w_hi = sb("w_hi", [P, 2, 2 * W_WIDE], F32R)
        w_lo = sb("w_lo", [P, 2, 2 * W_WIDE], F32R)
        x_hi = sb("x_hi", [P, KD, T1], F32R)
        x_lo = sb("x_lo", [P, KD, T1], F32R)
        h = sb("h", [P, KD, T1])
        pj = sb("pj", [P, IN1, T1])
        silu = sb("silu", [P, 2, T1])
        prod = sb("prod", [P, 2, T1])
        prm = sb("prm", [P, PRM_W])
        cst = sb("cst", [P, CC_W])
        std = sb("std", [P, 2, T1])
        small = sb("small", [P, 64])
        hid_hi = sb("hid_hi", [P, NF, T1], F32R)
        hid_lo = sb("hid_lo", [P, NF, T1], F32R)
        HID_BYTES = NF * T1 * 4
        hid_at = nc.sbuf_base - 2 * HID_BYTES
        SCRATCH = 2 * NF * T1
        scr = nc.alloc_sbuf_tensor_at("scratch", [P, SCRATCH], F32, offset=hid_at)
        ps = ctx.enter_context(nc.psum_tensor("ps", [P, 8, 512], F32))

        used = [0]

        def take(*shape):
            n = int(np.prod(shape))
            a = scr[:, used[0]:used[0] + n]
            used[0] += n
            assert used[0] <= SCRATCH
            if len(shape) == 2:
                a = a.rearrange("p (a b) -> p a b", a=shape[0])
            if len(shape) == 3:
                a = a.rearrange("p (a b c) -> p a b c", a=shape[0], b=shape[1])
            return a

        def con(name, w=128, rows=slice(0, P)):
            return cst[rows, CC[name]:CC[name] + w]

        def par(table, name, k=0, w=1, rows=slice(0, P)):
            return prm[rows, table[name] + k:table[name] + k + w]

        ident = con("ident")

        h_in = sem("h_in")
        consts_in = sem("consts_in")
        prm_in = sem("prm_in")
        prm_free = sem("prm_free")
        stored = sem("stored")
        raw_landed = [sem("raw_landed0"), sem("raw_landed1")]
        hi_done = sem("hi_done")
        lo_done = sem("lo_done")
        unit_used = sem("unit_used")
        xh_first = sem("xh_first")
        x_ready = sem("x_ready")
        silu_done = sem("silu_done")
        up_free = sem("up_free")
        hid_ready = sem("hid_ready")
        resid_ready = sem("resid_ready")
        mean_ready = sem("mean_ready")
        centered = sem("centered")
        ln_sq = sem("ln_sq")
        rms_sq = sem("rms_sq")
        var_ready = sem("var_ready")
        std_ready = sem("std_ready")
        xn_ready = sem("xn_ready")
        xh_ready = sem("xh_ready")
        CREDIT, START = 2, 1

        NH = FOX_HEADS + MLA_HEADS
        conv_seed = signal("conv_seed", 6)
        conv_done = signal("conv_done", 1)
        xc_ready = signal("xc_ready", 1)
        proj_ready = signal("proj_ready", IN1, START)
        rows_u = signal("rows_u", 1)
        rows_ln = signal("rows_ln", 1)
        rows_ready = signal("rows_ready", 1)
        mla_sq = signal("mla_sq", 1)
        mla_ss = signal("mla_ss", 1)
        mla_std = signal("mla_std", 1)
        cqn_ready = signal("cqn_ready", 1)
        kr_raw = signal("kr_raw", 1)
        kr_ready = signal("kr_ready", 1)
        uq_done = signal("uq_done", 1)
        ukv_done = signal("ukv_done", 1)
        qn_ready = signal("qn_ready", 1)
        kv_ready = signal("kv_ready", 1)
        qrot_done = signal("qrot_done", 1)
        qr_ready = signal("qr_ready", 1)
        vf_t = signal("vf_t", 1)
        vf_ready = signal("vf_ready", 1)
        xs_t = signal("xs_t", 1)
        rows_t = signal("rows_t", 1)
        tok_ready = signal("tok_ready", 1)
        g_ready = signal("g_ready", 2)
        d_ready = signal("d_ready", SSD_HEADS)
        decay = signal("decay", SSD_HEADS)
        ssd_w = signal("ssd_w", SSD_HEADS)
        y_ready = signal("y_ready", SSD_HEADS)
        yz_ready = signal("yz_ready", 4)
        sqy_ready = signal("sqy_ready", 1)
        yss_ready = signal("yss_ready", 1)
        ystd_ready = signal("ystd_ready", 1)
        ssd_cat = signal("ssd_cat", 1)
        s_ready = signal("s_ready", NH)
        nm_ready = signal("nm_ready", NH)
        exp_done = signal("exp_done", NH)
        p_ready = signal("p_ready", NH)
        t_ready = signal("t_ready", NH)
        pt_ready = signal("pt_ready", NH)
        o_ready = signal("o_ready", NH)
        o_evac = signal("o_evac", NH // 2)
        cat_hi = signal("cat_hi", KD)
        proj2_ready = signal("proj2_ready", IN2, START)
        af_t = signal("af_t", 1)
        af_ready = signal("af_ready", 1)
        v_t = signal("v_t", 1)
        v_ready = signal("v_ready", 1)
        pm_done = signal("pm_done", 1)
        pm_ready = signal("pm_ready", 1)
        uv_done = signal("uv_done", 1)
        uv_ready = signal("uv_ready", 1)
        py_done = signal("py_done", 1)
        pool_cat = signal("pool_cat", 1)
        f2_done = signal("f2_done", 1)
        f2_ready = signal("f2_ready", 1)
        f3_done = signal("f3_done", 1)
        lam_dot = signal("lam_dot", 1)
        lam_exp = signal("lam_exp", 1)
        s2_ready = signal("s2_ready", ATT_HEADS)
        nm2_ready = signal("nm2_ready", ATT_HEADS)
        exp2_done = signal("exp2_done", ATT_HEADS)
        a2_ready = signal("a2_ready", ATT_HEADS)
        t2_ready = signal("t2_ready", ATT_HEADS)
        at2_ready = signal("at2_ready", ATT_HEADS)
        o2_ready = signal("o2_ready", ATT_HEADS)
        o2_sq = signal("o2_sq", 1)
        o2_ss = signal("o2_ss", 1)
        o2_std = signal("o2_std", 1)
        att_cat = signal("att_cat", 1)
        cat2_hi = signal("cat2_hi", KD)

        xc = take(6, T1)
        xtok = take(3, 512)
        tok_ncum = take(3, 64)
        tok_dt = take(3, 64)
        vfox = take(3, 256)
        vmla = take(3, 256)
        cqn = take(3, T1)
        qn = take(2, T1)
        qr = take(T1)
        kn = take(2, T1)
        kr = take(T1)
        qraw = take(T1)
        rot_t = take(2, T1)
        row_u = take(T1)
        row_l = take(T1)
        row_sp = take(T1)
        row_cum = take(T1)
        prob = take(2, 3, T1)
        ptr = take(2, 432)
        used[0] = 0
        aftok = take(2, 512)
        vtok = take(2, 512)
        poolm = take(2, T2)
        uu = take(2, T2)
        vv = take(2, T2)
        y4 = take(2, T2)
        prob2 = take(2, 4, T2)
        attn = take(2, 2, T2)
        attn_t = take(2, 2, T2)
        sqo = take(4, T2)
        std4 = take(4, T2)
        ROWS = slice(ROW0, P)
        head_rows = lambda hh: slice(64 * (hh % 2), 64 * (hh % 2) + 64)

        amax, nmax, asum, rsum = (small[:, 8 * i:8 * i + 8].rearrange("p (a b) -> p a b", a=2) for i in range(4))
        acoef = small[:, 32:33]
        lam_s, lam_e, neg_lam = small[:, 33:35], small[:, 35:37], small[:, 37:38]
        g_lam = small[:, 38:42]
        rlam = small[:, 42:46].rearrange("p (a b) -> p a b", a=2)

        FFN_T, UP_T, DOWN_T = FFN_PAIRS // 2, UP_PAIRS // 2, DOWN_PAIRS // 2
        SEC1 = {"ffn1": 0, "in": FFN_T, "out": FFN_T + IN1 // 4, "ffn2": FFN_T + IN1 // 4 + OUTB // 4}
        SEC2 = {"ffn1": 0, "in": FFN_T, "out": FFN_T + IN2 // 4, "ffn2": FFN_T + IN2 // 4 + OUTB // 4}
        TURNS1, TURNS2 = LAYER1_PAIRS // 2, LAYER2_PAIRS // 2
        BLOCK2_TURN = DEPTH * TURNS1
        ALL_TURNS = BLOCK2_TURN + DEPTH * TURNS2
        NORM2 = 3 * DEPTH + 1
        EVENT2 = 4 * DEPTH + 1

        prob_flat = prob.rearrange("p a b t -> p (a b t)")
        decays = [prob_flat[:, s * 432:s * 432 + 432] for s in range(2)]

        block = ctx.enter_context(nc.Block())

        @block.sync
        def _(sp):
            def load_pair(j, src, width):
                sp.dma_start(raw[:, j, 0:2 * width], src).then_inc(raw_landed[j], 16)

            def section(turn0, n, src, width, next_src, next_width):
                with sp.Fori(0, n - 1) as it:
                    for j in range(2):
                        sp.wait_ge(lo_done, turn0 * 4 + it * 4 + (2 * j + 2))
                        load_pair(j, src(it * 2 + (2 + j)), width)
                for j in range(2):
                    sp.wait_ge(lo_done, turn0 * 4 + (4 * (n - 1) + 2 * j + 2))
                    load_pair(j, next_src(j), next_width)

            def ffn(q, turn0, next_src, next_width):
                section(turn0, UP_T, lambda i: w_up[q * NF + i], W_NARROW, lambda i: w_down[q * KD + i], W_WIDE)
                section(turn0 + UP_T, DOWN_T, lambda i: w_down[q * KD + i], W_WIDE, next_src, next_width)

            def layer(l, turn0, sec, q, w_in, n_in, w_out):
                def win(i):
                    return w_in[l * (n_in // 2) + i]

                def wout(i):
                    return w_out[l * (OUTB // 2) + i]

                ffn(q, turn0 + sec["ffn1"], win, W_NARROW)
                section(turn0 + sec["in"], n_in // 4, win, W_NARROW, wout, W_NARROW)
                section(turn0 + sec["out"], OUTB // 4, wout, W_NARROW, lambda i: w_up[(q + 1) * NF + i], W_NARROW)
                ffn(q + 1, turn0 + sec["ffn2"], lambda i: w_up[(q + 2) * NF + i], W_NARROW)

            sp.dma_start(h[:], hidden0).then_inc(h_in, 16)
            for j in range(2):
                load_pair(j, w_up[j], W_NARROW)
            sp.dma_start(cst[:], consts).then_inc(consts_in, 16)
            with sp.Fori(0, DEPTH) as l:
                sp.wait_ge(prm_free, l * 1 + START)
                sp.dma_start(prm[:, 0:P1_W], prm1[l]).then_inc(prm_in, 16)
                layer(l, l * TURNS1, SEC1, l * 2, w_in1, IN1, w_out1)
            with sp.Fori(0, DEPTH) as l:
                sp.wait_ge(prm_free, l * 1 + (DEPTH + START))
                sp.dma_start(prm[:, 0:P2_W], prm2[l]).then_inc(prm_in, 16)
                layer(l, l * TURNS2 + BLOCK2_TURN, SEC2, l * 2 + 2 * DEPTH, w_in2, IN2, w_out2)
            for j in range(2):
                sp.wait_ge(raw_landed[j], 16 * (ALL_TURNS + 1))
            sp.wait_ge(xn_ready, KD * (NORM2 + 3 * DEPTH))
            sp.dma_start(out, pj[:, 0:KD, 0:T2]).then_inc(stored, 16)
            sp.wait_ge(stored, 16)

        @block.tensor
        def _(pe):
            mm = nc.tensor.matmul
            tr = nc.tensor.transpose

            def three(dst, j, cols, xa, xb, first, last):
                mm(dst, w_lo[:, j, cols], xa, start=first, stop=False)
                mm(dst, w_hi[:, j, cols], xb, start=False, stop=False)
                return mm(dst, w_hi[:, j, cols], xa, start=False, stop=last)

            def narrow_unit(turn, j, u, dst, T):
                pe.wait_ge(lo_done, turn * 4 + (2 * j + u + 1))
                for k in range(KD):
                    c = u * W_NARROW + k * P
                    last = three(dst, j, slice(c, c + P), x_hi[:, k, 0:T], x_lo[:, k, 0:T], k == 0, k == KD - 1)
                last.then_inc(unit_used, 1)

            def wait_x(event):
                pe.wait_ge(x_ready, event * KD + KD)

            def up(q, turn0, event, T):
                with pe.Fori(0, UP_T) as it:
                    wait_x(event)
                    for j in range(2):
                        pe.wait_ge(up_free, q * NF + it * 2 + (j - 1 + CREDIT))
                        for u in range(2):
                            narrow_unit(turn0 + it, j, u, ps[:, 2 * j + u, 0:T], T)

            def one_chunk(buf, m, cols):
                if isinstance(m, int):
                    return buf[:, m, cols]
                return buf[:, bass.ds(m, 1), cols].rearrange("p a t -> p (a t)")

            def stats(rms, norm, T, m, first, last):
                if rms:
                    pe.wait_ge(rms_sq, norm * KD + (m + 1))
                    return mm(ps[:, 7, 0:T], con("onesD"), one_chunk(pj, m + KD, slice(0, T)), start=first, stop=last)
                pe.wait_ge(resid_ready, norm * KD + (m + 1 + CREDIT))
                return mm(ps[:, 6, 0:T], con("onesD"), one_chunk(h, m, slice(T1 - T, T1)), start=first, stop=last)

            def end_stats(rms, norm, T, m):
                last = stats(rms, norm, T, m, m == 0, True)
                if rms:
                    last.then_inc(var_ready, 1)
                    return
                last.then_inc(mean_ready, 1)
                for k in range(KD):
                    if k % 4 == 0:
                        pe.wait_ge(ln_sq, norm * 2 + (k // 4 + 1))
                    last = mm(ps[:, 7, 0:T], con("onesD"), pj[:, KD + k, 0:T], start=k == 0, stop=k == KD - 1)
                last.then_inc(var_ready, 1)

            def down(q, turn0, resid, rms, norm, T):
                pe.wait_ge(hid_ready, q * NF + NF)

                def turn(it):
                    for j in range(2):
                        pe.wait_ge(resid_ready, resid * KD + it * 2 + (j - 1 + CREDIT))
                        for u in range(2):
                            pe.wait_ge(lo_done, turn0 * 4 + it * 4 + (2 * j + u + 1))
                            for c in range(HALF_F):
                                f = u * HALF_F + c
                                col = u * W_WIDE + c * P
                                last = three(ps[:, 4 + j, 0:T], j, slice(col, col + P),
                                             hid_hi[:, f, 0:T], hid_lo[:, f, 0:T], f == 0, f == NF - 1)
                            last.then_inc(unit_used, 1)
                        if not (isinstance(it, int) and j == 0):
                            stats(rms, norm, T, it * 2 + (j - 1), isinstance(it, int), False)

                turn(0)
                with pe.Fori(1, DOWN_T) as it:
                    turn(it)
                end_stats(rms, norm, T, KD - 1)

            def out_proj(turn0, event, resid, rms, norm, T):
                wait_x(event)
                for m in range(KD):
                    pe.wait_ge(resid_ready, resid * KD + (m - 1 + CREDIT))
                    narrow_unit(turn0 + m // 4, (m // 2) % 2, m % 2, ps[:, 4 + m % 2, 0:T], T)
                    if m >= 1:
                        stats(rms, norm, T, m - 1, m == 1, False)
                end_stats(rms, norm, T, KD - 1)

            def in_proj(l, turn0, event, n, ready, T):
                with pe.Fori(0, n // 4) as it:
                    wait_x(event)
                    pe.wait_ge(ready.sem, ready.at(l, 0) + it * 4)
                    for i in range(4):
                        narrow_unit(turn0 + it, i // 2, i % 2, ps[:, i, 0:T], T)

            def tri_bank(bank, i):
                n, w = TILES[i][1], TRI_W[i]
                return ps[0:n, bank, TRI[i]:TRI[i] + w]

            def mixer1(l):
                pe.wait_ge(proj_ready.sem, proj_ready.at(l, IN1))
                for i, (t, n) in enumerate(TILES):
                    for c in range(2):
                        col = 256 * (i % 2) + P * c
                        last = tr(ps[0:n, 4 + i // 2, col:col + P], pj[:, FV0 + c, t:t + n], ident)
                last.then_inc(vf_t.sem, 1)
                pe.wait_ge(mla_sq.sem, mla_sq.at(l, 1))
                mm(ps[:, 6, 0:T1], con("ones256"), prob[:, 0, 0, :], start=True, stop=False)
                mm(ps[:, 6, 0:T1], con("ones256"), prob[:, 0, 1, :], start=False, stop=True)
                mm(ps[:, 7, 0:T1], con("ones128"), prob[:, 0, 2, :], start=True, stop=True).then_inc(mla_ss.sem, 1)
                krope = pj[0:ROPE, MISC, :]
                mm(ps[:, 0, 0:T1], con("rep", rows=slice(0, ROPE)), krope, start=True, stop=True)
                mm(ps[:, 1, 0:T1], con("reprot", rows=slice(0, ROPE)), krope, start=True, stop=True)\
                    .then_inc(kr_raw.sem, 1)
                pe.wait_ge(cqn_ready.sem, cqn_ready.at(l, 1))
                for b, bank in enumerate((2, 3, 6)):
                    for k in range(2):
                        c = P1["uq"] + 384 * k + P * b
                        last = mm(ps[:, bank, 0:T1], prm[:, c:c + P], cqn[:, k, :], start=k == 0, stop=k == 1)
                last.then_inc(uq_done.sem, 1)
                pe.wait_ge(vf_ready.sem, vf_ready.at(l, 1))
                for b in range(2):
                    c = P1["ukv"] + P * b
                    mm(ps[:, 4 + b, 0:T1], prm[:, c:c + P], cqn[:, 2, :], start=True, stop=True)
                pe.wait_ge(kr_ready.sem, kr_ready.at(l, 1))
                for i, (t, n) in enumerate(TILES):
                    c = P1["ukv"] + 2 * P
                    dst = ps[0:n, 7, 256 * i:256 * i + 256] if i < 2 else ps[0:n, 0, 0:256]
                    last = mm(dst, cqn[:, 2, t:t + n], prm[:, c:c + 256], start=True, stop=True)
                last.then_inc(ukv_done.sem, 1)
                pe.wait_ge(qn_ready.sem, qn_ready.at(l, 1))
                mm(ps[:, 1, 0:T1], con("rot"), qraw, start=True, stop=True).then_inc(qrot_done.sem, 1)
                pe.wait_ge(xc_ready.sem, xc_ready.at(l, 1))
                pe.wait_ge(kv_ready.sem, kv_ready.at(l, 1))
                pe.wait_ge(rows_ready.sem, rows_ready.at(l, 1))
                for i, (t, n) in enumerate(TILES):
                    for c in range(4):
                        last = tr(ps[0:n, 2 + i, P * c:P * c + P], xc[:, c, t:t + n], ident)
                last.then_inc(xs_t.sem, 1)
                for i, (t, n) in enumerate(TILES):
                    for r, src in enumerate((row_cum, row_sp)):
                        c = (2 * i + r) * 64
                        last = tr(ps[0:n, 5, c:c + 64], src[ROWS, t:t + n], ident[ROWS, ROWS])
                last.then_inc(rows_t.sem, 1)
                pe.wait_ge(qr_ready.sem, qr_ready.at(l, 1))
                for g in range(2):
                    gr = slice(64 * g, 64 * g + 64)
                    for i, (t, n) in enumerate(TILES):
                        last = mm(tri_bank(g, i), xc[gr, 4, t:t + n], xc[gr, 5, t:T1], start=True, stop=True)
                    last.then_inc(g_ready.sem, 1)

                def ssd_d(hh):
                    if hh < 2:
                        pe.wait_ge(tok_ready.sem, tok_ready.at(l, 1))
                    else:
                        pe.wait_ge(decay.sem, decay.at(l, hh - 1))
                    bank = 2 + hh % 2
                    for i, (t, n) in enumerate(TILES):
                        mm(tri_bank(bank, i), con("sel", 12 * P)[:, hh * P:hh * P + n], row_cum[:, t:T1],
                           start=True, stop=False)
                        last = mm(ps[0:n, bank, TRI[i]:TRI[i] + n], ident[:, 0:n], con("maskS", n),
                                  start=False, stop=True)
                    last.then_inc(d_ready.sem, 1)

                def ssd_y(hh):
                    pe.wait_ge(ssd_w.sem, ssd_w.at(l, hh + 1))
                    if hh % 2 == 0 and hh >= 4:
                        pe.wait_ge(yz_ready.sem, yz_ready.at(l, hh // 2 - 1))
                    for i, (t, n) in enumerate(TILES):
                        last = mm(ps[head_rows(hh), 4 + (hh // 2) % 2, t:T1], xtok[0:n, i, HD * hh:HD * hh + HD],
                                  ptr[0:n, hh % 2, TRI[i]:TRI[i] + TRI_W[i]], start=i == 0, stop=i == 2)
                    last.then_inc(y_ready.sem, 1)

                ssd_d(0)
                for hh in range(SSD_HEADS):
                    if hh + 1 < SSD_HEADS:
                        ssd_d(hh + 1)
                    ssd_y(hh)
                pe.wait_ge(sqy_ready.sem, sqy_ready.at(l, 1))
                for g in range(2):
                    for c in range(2):
                        last = mm(ps[:, 6 + g, 0:T1], con("ones256"), prob_flat[:, (2 * g + c) * T1:(2 * g + c + 1) * T1],
                                  start=c == 0, stop=c == 1)
                last.then_inc(yss_ready.sem, 1)

                def att_s(n_):
                    if n_ == 0:
                        pe.wait_ge(ssd_w.sem, ssd_w.at(l, SSD_HEADS))
                    if n_ >= 2:
                        pe.wait_ge(exp_done.sem, exp_done.at(l, n_ - 1))
                    for i, (t, n) in enumerate(TILES):
                        bank, col, kw = S_BANK[i]
                        dst = ps[0:n, 2 * (n_ % 2) + bank, col:col + kw]
                        hr = head_rows(n_)
                        if n_ < FOX_HEADS:
                            b = n_ // 2
                            mm(dst, pj[hr, FQ0 + b, t:t + n], pj[hr, FK0 + b, 0:kw], start=True, stop=False)
                            mm(dst, con("sel", 12 * P)[:, (8 + n_) * P:(8 + n_) * P + n], row_cum[:, 0:kw],
                               start=False, stop=False)
                        else:
                            b = (n_ - FOX_HEADS) // 2
                            rr = slice(ROPE * (n_ - FOX_HEADS), ROPE * (n_ - FOX_HEADS) + ROPE)
                            mm(dst, qn[hr, b, t:t + n], kn[hr, b, 0:kw], start=True, stop=False)
                            mm(dst, qr[rr, t:t + n], kr[rr, 0:kw], start=False, stop=False)
                        last = mm(ps[0:n, 2 * (n_ % 2) + bank, col + t:col + t + n], ident[:, 0:n],
                                  con("maskA", n), start=False, stop=True)
                    last.then_inc(s_ready.sem, 1)

                def att_t(n_):
                    pe.wait_ge(p_ready.sem, p_ready.at(l, n_ + 1))
                    if n_ >= 2:
                        pe.wait_ge(pt_ready.sem, pt_ready.at(l, n_ - 1))
                    if n_ == 0:
                        pe.wait_ge(yz_ready.sem, yz_ready.at(l, 4))
                    for i, (t, n) in enumerate(TILES):
                        for k in range(i + 1):
                            tk, nk = TILES[k]
                            c = TRI[k] + t - tk
                            last = tr(ps[0:nk, 4 + n_ % 2, c:c + n], prob[0:n, n_ % 2, i, tk:tk + nk], ident[0:n, 0:n])
                    last.then_inc(t_ready.sem, 1)

                def att_o(n_):
                    pe.wait_ge(pt_ready.sem, pt_ready.at(l, n_ + 1))
                    pair = n_ // 2
                    if n_ == 0:
                        pe.wait_ge(ystd_ready.sem, ystd_ready.at(l, 1))
                    if n_ % 2 == 0 and pair >= 2:
                        pe.wait_ge(o_evac.sem, o_evac.at(l, pair - 1))
                    v = vfox if n_ < FOX_HEADS else vmla
                    hd = n_ % FOX_HEADS
                    for k, (t, n) in enumerate(TILES):
                        last = mm(ps[head_rows(n_), 6 + pair % 2, t:T1], v[0:n, k, HD * hd:HD * hd + HD],
                                  ptr[0:n, n_ % 2, TRI[k]:TRI[k] + TRI_W[k]], start=k == 0, stop=k == 2)
                    last.then_inc(o_ready.sem, 1)

                att_s(0)
                for n_ in range(NH):
                    if n_ + 1 < NH:
                        att_s(n_ + 1)
                    att_t(n_)
                    if n_ >= 1:
                        att_o(n_ - 1)
                att_o(NH - 1)

            def mixer2(l):
                pe.wait_ge(proj2_ready.sem, proj2_ready.at(l, IN2))
                for i in range(2):
                    for c in range(4):
                        last = tr(ps[:, i, P * c:P * c + P], pj[:, c, P * i:P * i + P], ident)
                last.then_inc(af_t.sem, 1)
                for i in range(2):
                    for c in range(4):
                        last = tr(ps[:, 2 + i, P * c:P * c + P], pj[:, 12 + c, P * i:P * i + P], ident)
                last.then_inc(v_t.sem, 1)
                pe.wait_ge(af_ready.sem, af_ready.at(l, 1))
                for g in range(4):
                    for i in range(2):
                        c = CC["band"] + (2 * g + i) * T2
                        last = mm(ps[head_rows(g), 4, 256 * (g // 2):256 * (g // 2) + T2],
                                  aftok[:, i, 64 * g:64 * g + 64], cst[:, c:c + T2], start=i == 0, stop=i == 1)
                last.then_inc(pm_done.sem, 1)
                for r, name in enumerate(("cs", "ss")):
                    if r == 1:
                        pe.wait_ge(pm_ready.sem, pm_ready.at(l, 1))
                    for b in range(2):
                        for i in range(2):
                            c = CC[name] + i * T2
                            last = mm(ps[:, 6 + r, 256 * b:256 * b + T2], aftok[:, i, 256 + P * b:256 + P * b + P],
                                      cst[:, c:c + T2], start=i == 0, stop=i == 1)
                last.then_inc(uv_done.sem, 1)
                for g in range(4):
                    c = P2["poolw"] + 64 * (g // 2)
                    last = mm(ps[head_rows(g), 5, 256 * (g // 2):256 * (g // 2) + T2], prm[head_rows(g), c:c + 64],
                              poolm[head_rows(g), g // 2, :], start=True, stop=True)
                last.then_inc(py_done.sem, 1)
                pe.wait_ge(uv_ready.sem, uv_ready.at(l, 1))
                for b in range(2):
                    dst = ps[:, 6, 256 * b:256 * b + T2]
                    mm(dst, con("ccos"), uu[:, b, :], start=True, stop=False)
                    last = mm(dst, con("csin"), vv[:, b, :], start=False, stop=True)
                last.then_inc(f2_done.sem, 1)
                pe.wait_ge(f2_ready.sem, f2_ready.at(l, 1))
                for b in range(2):
                    for k in range(2):
                        c = P2["fourw"] + 256 * k + P * b
                        last = mm(ps[:, 7, 256 * b:256 * b + T2], prm[:, c:c + P], y4[:, k, :], start=k == 0, stop=k == 1)
                last.then_inc(f3_done.sem, 1)

                def att_s(hh):
                    if hh == 0:
                        pe.wait_ge(v_ready.sem, v_ready.at(l, 1))
                    if hh >= 2:
                        pe.wait_ge(exp2_done.sem, exp2_done.at(l, hh - 1))
                    for i in range(2):
                        for j in range(2):
                            dst = ps[:, 2 * (hh % 2) + j, 256 * i:256 * i + T2]
                            mm(dst, pj[head_rows(j), 4 + hh, P * i:P * i + P], pj[head_rows(j), 8 + hh, 0:T2],
                               start=True, stop=False)
                            c = CC["absd"] + i * T2
                            s = CC["slope"] + hh * P
                            last = mm(dst, cst[:, s:s + P], cst[:, c:c + T2], start=False, stop=True)
                    last.then_inc(s2_ready.sem, 1)

                def att_t(hh):
                    pe.wait_ge(a2_ready.sem, a2_ready.at(l, hh + 1))
                    if hh == 0:
                        pe.wait_ge(pool_cat.sem, pool_cat.at(l, 1))
                    if hh >= 2:
                        pe.wait_ge(at2_ready.sem, at2_ready.at(l, hh - 1))
                    for i in range(2):
                        for k in range(2):
                            c = 256 * k + P * i
                            last = tr(ps[:, 4 + hh % 2, c:c + P], attn[:, hh % 2, i, P * k:P * k + P], ident)
                    last.then_inc(t2_ready.sem, 1)

                def att_o(hh):
                    pe.wait_ge(at2_ready.sem, at2_ready.at(l, hh + 1))
                    dst = ps[:, 6 + hh // 2, 256 * (hh % 2):256 * (hh % 2) + T2]
                    for k in range(2):
                        last = mm(dst, vtok[:, k, P * hh:P * hh + P], attn_t[:, hh % 2, k, :], start=k == 0, stop=k == 1)
                    last.then_inc(o2_ready.sem, 1)

                att_s(0)
                for hh in range(ATT_HEADS):
                    if hh + 1 < ATT_HEADS:
                        att_s(hh + 1)
                    att_t(hh)
                    if hh >= 1:
                        att_o(hh - 1)
                att_o(ATT_HEADS - 1)
                pe.wait_ge(o2_sq.sem, o2_sq.at(l, 1))
                for hh in range(ATT_HEADS):
                    last = mm(ps[:, hh // 2, 256 * (hh % 2):256 * (hh % 2) + T2], con("ones128"), sqo[:, hh, :],
                              start=True, stop=True)
                last.then_inc(o2_ss.sem, 1)

            pe.nop().then_inc(unit_used, START)
            pe.wait_ge(consts_in, 16)
            with pe.Fori(0, DEPTH) as l:
                t0, q, e0, r0 = l * TURNS1, l * 2, l * 4, l * 3
                up(q, t0 + SEC1["ffn1"], e0, T1)
                down(q, t0 + SEC1["ffn1"] + UP_T, r0, False, r0, T1)
                in_proj(l, t0 + SEC1["in"], e0 + 1, IN1, proj_ready, T1)
                pe.wait_ge(prm_in, l * 16 + 16)
                mixer1(l)
                out_proj(t0 + SEC1["out"], e0 + 2, r0 + 1, False, r0 + 1, T1)
                up(q + 1, t0 + SEC1["ffn2"], e0 + 3, T1)
                down(q + 1, t0 + SEC1["ffn2"] + UP_T, r0 + 2, False, r0 + 2, T1)
            for k in range(KD - 1):
                stats(True, 0, T2, k, k == 0, False)
            end_stats(True, 0, T2, KD - 1)
            with pe.Fori(0, DEPTH) as l:
                t0, q, e0, r0 = l * TURNS2 + BLOCK2_TURN, l * 2 + 2 * DEPTH, l * 4 + EVENT2, l * 3 + 3 * DEPTH
                up(q, t0 + SEC2["ffn1"], e0, T2)
                down(q, t0 + SEC2["ffn1"] + UP_T, r0, True, l * 3 + 1, T2)
                in_proj(l, t0 + SEC2["in"], e0 + 1, IN2, proj2_ready, T2)
                pe.wait_ge(prm_in, l * 16 + (16 * DEPTH + 16))
                mixer2(l)
                out_proj(t0 + SEC2["out"], e0 + 2, r0 + 1, True, l * 3 + 2, T2)
                up(q + 1, t0 + SEC2["ffn2"], e0 + 3, T2)
                down(q + 1, t0 + SEC2["ffn2"] + UP_T, r0 + 2, True, l * 3 + 3, T2)

        @block.scalar
        def _(act):
            fn = nc.scalar.activation

            def split_hi(turn, j, width, wait_slot=True):
                act.wait_ge(raw_landed[j], turn * 16 + 16)
                if wait_slot:
                    act.wait_ge(unit_used, turn * 4 + (2 * j - 2 + START))
                for u in range(2):
                    c = slice(u * width, (u + 1) * width)
                    fn(w_hi[:, j, c], raw[:, j, c], ACT.Copy).then_inc(hi_done, 1)

            def split_next(turn, j, width):
                split_hi(turn + j, 1 - j, width)

            def up(q, turn0, T):
                def turn(it, next_width):
                    for j in range(2):
                        split_next(turn0 + it, j, W_NARROW if j == 0 else next_width)
                        act.wait_ge(unit_used, turn0 * 4 + it * 4 + (2 * j + 1 + START))
                        act.wait_ge(up_free, q * NF + it * 2 + (j - 1 + CREDIT))
                        fn(silu[:, j, 0:T], ps[:, 2 * j, 0:T], ACT.Silu).then_inc(silu_done, 1)

                with act.Fori(0, UP_T - 1) as it:
                    turn(it, W_NARROW)
                turn(UP_T - 1, W_WIDE)

            def square(norm, resid, m, T):
                act.wait_ge(resid_ready, resid * KD + (m + 1 + CREDIT))
                if isinstance(m, int):
                    dst, src = pj[:, KD + m, 0:T], h[:, m, T1 - T:T1]
                else:
                    dst, src = pj[:, bass.ds(m + KD, 1), 0:T], h[:, bass.ds(m, 1), T1 - T:T1]
                fn(dst, src, ACT.Square).then_inc(rms_sq, 1)

            def down(turn0, resid, rms, norm, T):
                def turn(it, next_width):
                    for j in range(2):
                        split_next(turn0 + it, j, W_WIDE if j == 0 else next_width)
                        if rms:
                            square(norm, resid, it * 2 + j, T)

                with act.Fori(0, DOWN_T - 1) as it:
                    turn(it, W_WIDE)
                turn(DOWN_T - 1, W_NARROW)

            def out_proj(turn0, resid, rms, norm, T):
                for p in range(OUTB // 2):
                    split_next(turn0 + p // 2, p % 2, W_NARROW)
                    if rms:
                        for u in range(2):
                            square(norm, resid, 2 * p + u, T)

            def in_proj(turn0, n, ready, T):
                def turn(it):
                    for j in range(2):
                        split_next(turn0 + it, j, W_NARROW)
                        for u in range(2):
                            act.wait_ge(unit_used, turn0 * 4 + it * 4 + (2 * j + u + 1 + START))
                            dst = pj[:, bass.ds(it * 4 + (2 * j + u), 1), 0:T]
                            fn(dst, ps[:, 2 * j + u:2 * j + u + 1, 0:T], ACT.Copy).then_inc(ready.sem, 1)

                with act.Fori(0, n // 4) as it:
                    turn(it)

            def layer_norm(norm, bias):
                for s in range(2):
                    act.wait_ge(centered, norm * 2 + (s + 1))
                    fn(pj[:, KD + 4 * s:KD + 4 * s + 4, :], h[:, 4 * s:4 * s + 4, :], ACT.Square).then_inc(ln_sq, 1)
                act.wait_ge(var_ready, norm + 1)
                fn(std[:, 0, :], ps[:, 7, 0:T1], ACT.Sqrt, bias=con("eps1", 1)).then_inc(std_ready, 1)
                for k in range(KD):
                    act.wait_ge(xn_ready, norm * KD + (k + 1))
                    fn(h[:, k, :], pj[:, k, :], ACT.Identity, bias=par(P1, bias, k))
                    fn(x_hi[:, k, :], pj[:, k, :], ACT.Identity, bias=par(P1, bias, k)).then_inc(xh_ready, 1)

            def rms_norm(number):
                act.wait_ge(var_ready, number + 1)
                fn(std[:, 0, 0:T2], ps[:, 7, 0:T2], ACT.Sqrt, bias=con("eps2", 1)).then_inc(std_ready, 1)
                for k in range(KD):
                    act.wait_ge(xn_ready, number * KD + (k + 1))
                    fn(x_hi[:, k, 0:T2], pj[:, k, 0:T2], ACT.Copy).then_inc(xh_ready, 1)

            def mixer1(l):
                act.drain()
                fn(prob[:, 0, :, :], pj[:, CQ0:CQ0 + 3, :], ACT.Square).then_inc(mla_sq.sem, 1)
                for c in range(6):
                    fn(xc[:, c, :], pj[:, XBC0 + c, :], ACT.Identity, bias=par(P1, "convb", c),
                       scale=par(P1, "convw", CONV * c + CONV - 1)).then_inc(conv_seed.sem, 1)
                act.wait_ge(mla_ss.sem, mla_ss.at(l, 1))
                fn(std[:, :, :], ps[:, 6:8, 0:T1], ACT.Sqrt, bias=con("eps1", 1)).then_inc(mla_std.sem, 1)
                act.wait_ge(vf_t.sem, vf_t.at(l, 1))
                fn(vfox[:, 0:2, :], ps[:, 4, :].rearrange("p (a b) -> p a b", a=2), ACT.Copy)
                fn(vfox[0:16, 2, :], ps[0:16, 5, 0:256], ACT.Copy).then_inc(vf_ready.sem, 1)
                act.wait_ge(uq_done.sem, uq_done.at(l, 1))
                fn(qn, ps[:, 2:4, 0:T1], ACT.Copy)
                fn(qraw, ps[:, 6, 0:T1], ACT.Copy).then_inc(qn_ready.sem, 1)
                act.wait_ge(conv_done.sem, conv_done.at(l, 1))
                fn(xc, xc, ACT.Silu)
                fn(pj[:, Z0:Z0 + 4, :], pj[:, Z0:Z0 + 4, :], ACT.Silu).then_inc(xc_ready.sem, 1)
                act.wait_ge(rows_u.sem, rows_u.at(l, 1))
                fn(row_l[ROWS, :], row_u[ROWS, :], ACT.Abs)
                act.drain()
                fn(row_l[ROWS, :], row_l[ROWS, :], ACT.Exp, scale=-1.0)
                fn(acoef[ROWS, :], par(P1, "alog", rows=ROWS), ACT.Exp)
                act.drain()
                fn(row_l[ROWS, :], row_l[ROWS, :], ACT.Ln, bias=con("one", 1, ROWS)).then_inc(rows_ln.sem, 1)
                act.wait_ge(tok_ready.sem, tok_ready.at(l, 1))
                for hh in range(SSD_HEADS):
                    act.wait_ge(d_ready.sem, d_ready.at(l, hh + 1))
                    if hh >= 2:
                        act.wait_ge(ssd_w.sem, ssd_w.at(l, hh - 1))
                    for i, (t, n) in enumerate(TILES):
                        c = slice(TRI[i], TRI[i] + TRI_W[i])
                        last = fn(decays[hh % 2][0:n, c], ps[0:n, 2 + hh % 2, c], ACT.Exp,
                                  bias=tok_ncum[0:n, i, hh:hh + 1])
                    last.then_inc(decay.sem, 1)
                act.wait_ge(yz_ready.sem, yz_ready.at(l, 4))
                fn(prob_flat[:, 0:4 * T1], xc[:, 0:4, :].rearrange("p a t -> p (a t)"), ACT.Square)\
                    .then_inc(sqy_ready.sem, 1)
                act.wait_ge(yss_ready.sem, yss_ready.at(l, 1))
                fn(std[:, :, :], ps[:, 6:8, 0:T1], ACT.Sqrt, bias=con("eps1", 1)).then_inc(ystd_ready.sem, 1)

                def exps(n_):
                    act.wait_ge(nm_ready.sem, nm_ready.at(l, n_ + 1))
                    if n_ >= 2:
                        act.wait_ge(t_ready.sem, t_ready.at(l, n_ - 1))
                    s = n_ % 2
                    for i, (t, n) in enumerate(TILES):
                        bank, col, kw = S_BANK[i]
                        last = fn(prob[0:n, s, i, 0:kw], ps[0:n, 2 * s + bank, col:col + kw], ACT.Exp,
                                  bias=nmax[0:n, s, i:i + 1], scale=FOX_SCALE if n_ < FOX_HEADS else MLA_SCALE,
                                  accum_out=asum[0:n, s, i:i + 1])
                    last.then_inc(exp_done.sem, 1)

                def pt_copy(n_):
                    act.wait_ge(t_ready.sem, t_ready.at(l, n_ + 1))
                    if n_ >= 2:
                        act.wait_ge(o_ready.sem, o_ready.at(l, n_ - 1))
                    fn(ptr[:, n_ % 2, 0:TRI[2]], ps[:, 4 + n_ % 2, 0:TRI[2]], ACT.Copy)
                    fn(ptr[0:16, n_ % 2, TRI[2]:432], ps[0:16, 4 + n_ % 2, TRI[2]:432], ACT.Copy)\
                        .then_inc(pt_ready.sem, 1)

                def o_copy(pair):
                    act.wait_ge(o_ready.sem, o_ready.at(l, 2 * pair + 2))
                    fn(pj[:, 4 + pair, :], ps[:, 6 + pair % 2, 0:T1], ACT.Copy).then_inc(o_evac.sem, 1)

                exps(0)
                for n_ in range(NH):
                    if n_ + 1 < NH:
                        exps(n_ + 1)
                    pt_copy(n_)
                    if n_ % 2 == 0 and n_ >= 2:
                        o_copy(n_ // 2 - 1)
                o_copy(NH // 2 - 1)
                act.drain()
                act.wait_ge(ssd_cat.sem, ssd_cat.at(l, 1))
                for k in range(KD):
                    fn(x_hi[:, k, :], pj[:, k, :], ACT.Copy).then_inc(cat_hi.sem, 1)

            def mixer2(l):
                act.wait_ge(af_t.sem, af_t.at(l, 1))
                fn(aftok, ps[:, 0:2, :], ACT.Copy).then_inc(af_ready.sem, 1)
                act.wait_ge(lam_dot.sem, lam_dot.at(l, 1))
                fn(lam_e, lam_s, ACT.Exp).then_inc(lam_exp.sem, 1)
                act.wait_ge(uv_done.sem, uv_done.at(l, 1))
                fn(uu, ps[:, 6, :].rearrange("p (a t) -> p a t", a=2), ACT.Copy)
                fn(vv, ps[:, 7, :].rearrange("p (a t) -> p a t", a=2), ACT.Copy).then_inc(uv_ready.sem, 1)
                act.wait_ge(f2_done.sem, f2_done.at(l, 1))
                fn(y4, ps[:, 6, :].rearrange("p (a t) -> p a t", a=2), ACT.Copy).then_inc(f2_ready.sem, 1)
                act.wait_ge(f3_done.sem, f3_done.at(l, 1))
                fn(pj[:, 2:4, 0:T2], ps[:, 7, :].rearrange("p (a t) -> p a t", a=2), ACT.Copy)

                def exps(hh):
                    act.wait_ge(nm2_ready.sem, nm2_ready.at(l, hh + 1))
                    if hh >= 2:
                        act.wait_ge(a2_ready.sem, a2_ready.at(l, hh - 1))
                    s = hh % 2
                    for j in range(2):
                        for i in range(2):
                            c = 2 * j + i
                            last = fn(prob2[:, s, c, :], ps[:, 2 * s + j, 256 * i:256 * i + T2], ACT.Exp,
                                      bias=nmax[:, s, c:c + 1], scale=ATT_SCALE, accum_out=asum[:, s, c:c + 1])
                    last.then_inc(exp2_done.sem, 1)

                def at_copy(hh):
                    act.wait_ge(t2_ready.sem, t2_ready.at(l, hh + 1))
                    if hh >= 2:
                        act.wait_ge(o2_ready.sem, o2_ready.at(l, hh - 1))
                    fn(attn_t[:, hh % 2, :, :], ps[:, 4 + hh % 2, :].rearrange("p (a t) -> p a t", a=2), ACT.Copy)\
                        .then_inc(at2_ready.sem, 1)

                exps(0)
                for hh in range(ATT_HEADS):
                    if hh + 1 < ATT_HEADS:
                        exps(hh + 1)
                    at_copy(hh)
                act.wait_ge(o2_ready.sem, o2_ready.at(l, ATT_HEADS))
                for b in range(2):
                    src = ps[:, 6 + b, :].rearrange("p (a t) -> p a t", a=2)
                    fn(sqo[:, 2 * b:2 * b + 2, :], src, ACT.Square)
                    last = fn(pj[:, 4 + 2 * b:6 + 2 * b, 0:T2], src, ACT.Copy)
                last.then_inc(o2_sq.sem, 1)
                act.wait_ge(o2_ss.sem, o2_ss.at(l, 1))
                fn(std4, ps[:, 0:2, :].rearrange("p a (b t) -> p (a b) t", b=2), ACT.Sqrt, bias=con("eps2", 1))\
                    .then_inc(o2_std.sem, 1)
                act.drain()
                act.wait_ge(pool_cat.sem, pool_cat.at(l, 1))
                for k in range(KD):
                    if k == 4:
                        act.wait_ge(att_cat.sem, att_cat.at(l, 1))
                    fn(x_hi[:, k, 0:T2], pj[:, k, 0:T2], ACT.Copy).then_inc(cat2_hi.sem, 1)

            act.nop().then_inc(proj_ready.sem, START)
            act.nop().then_inc(proj2_ready.sem, START)
            act.wait_ge(h_in, 16)
            for k in range(KD):
                fn(x_hi[:, k, :], h[:, k, :], ACT.Copy).then_inc(xh_first, 1)
            split_hi(0, 0, W_NARROW, wait_slot=False)
            act.wait_ge(consts_in, 16)
            with act.Fori(0, DEPTH) as l:
                t0, q, r0 = l * TURNS1, l * 2, l * 3
                up(q, t0 + SEC1["ffn1"], T1)
                down(t0 + SEC1["ffn1"] + UP_T, r0, False, r0, T1)
                act.wait_ge(prm_in, l * 16 + 16)
                layer_norm(r0, "ln1b")
                in_proj(t0 + SEC1["in"], IN1, proj_ready, T1)
                mixer1(l)
                out_proj(t0 + SEC1["out"], r0 + 1, False, r0 + 1, T1)
                layer_norm(r0 + 1, "ln2b")
                up(q + 1, t0 + SEC1["ffn2"], T1)
                down(t0 + SEC1["ffn2"] + UP_T, r0 + 2, False, r0 + 2, T1)
                layer_norm(r0 + 2, "ln3b")
            act.drain()
            for k in range(KD):
                fn(pj[:, KD + k, 0:T2], h[:, k, T1 - T2:T1], ACT.Square).then_inc(rms_sq, 1)
            rms_norm(3 * DEPTH)
            with act.Fori(0, DEPTH) as l:
                t0, q, r0 = l * TURNS2 + BLOCK2_TURN, l * 2 + 2 * DEPTH, l * 3 + 3 * DEPTH
                n0 = l * 3 + NORM2
                up(q, t0 + SEC2["ffn1"], T2)
                down(t0 + SEC2["ffn1"] + UP_T, r0, True, None, T2)
                rms_norm(n0)
                in_proj(t0 + SEC2["in"], IN2, proj2_ready, T2)
                mixer2(l)
                out_proj(t0 + SEC2["out"], r0 + 1, True, None, T2)
                rms_norm(n0 + 1)
                up(q + 1, t0 + SEC2["ffn2"], T2)
                down(t0 + SEC2["ffn2"] + UP_T, r0 + 2, True, None, T2)
                rms_norm(n0 + 2)

        @block.vector
        def _(dve):
            v = nc.vector

            def split_lo(turn, j, width):
                for u in range(2):
                    dve.wait_ge(hi_done, turn * 4 + (2 * j + u + 1))
                    c = slice(u * width, (u + 1) * width)
                    v.tensor_tensor(w_lo[:, j, c], raw[:, j, c], w_hi[:, j, c].bitcast(F32), ALU.subtract)\
                        .then_inc(lo_done, 1)

            def split_next(turn, j, width):
                split_lo(turn + j, 1 - j, width)

            def up(q, turn0, T):
                def turn(it, next_width):
                    for j in range(2):
                        split_next(turn0 + it, j, W_NARROW if j == 0 else next_width)
                        dve.wait_ge(unit_used, turn0 * 4 + it * 4 + (2 * j + 2 + START))
                        dve.wait_ge(silu_done, q * NF + it * 2 + (j + 1))
                        v.scalar_tensor_tensor(out=prod[:, j, 0:T], in0=ps[:, 2 * j + 1, 0:T], scalar=0.5,
                                               in1=silu[:, j, 0:T], op0=ALU.mult, op1=ALU.mult).then_inc(up_free, 1)
                        f = it * 2 + j
                        f = slice(f, f + 1) if isinstance(f, int) else bass.ds(f, 1)
                        src = prod[:, j:j + 1, 0:T]
                        dve.drain()
                        v.tensor_copy(hid_hi[:, f, 0:T], src)
                        dve.drain()
                        v.tensor_tensor(hid_lo[:, f, 0:T], src, hid_hi[:, f, 0:T].bitcast(F32), ALU.subtract)\
                            .then_inc(hid_ready, 1)

                with dve.Fori(0, UP_T - 1) as it:
                    turn(it, W_NARROW)
                turn(UP_T - 1, W_WIDE)

            def resid(alpha, m, bank, T):
                c = slice(m, m + 1) if isinstance(m, int) else bass.ds(m, 1)
                dst = h[:, c, T1 - T:T1]
                v.scalar_tensor_tensor(out=dst, in0=dst, scalar=alpha, in1=ps[:, bank:bank + 1, 0:T],
                                       op0=ALU.mult, op1=ALU.add).then_inc(resid_ready, 1)

            def down(turn0, alpha, T):
                def turn(it, next_width):
                    for j in range(2):
                        split_next(turn0 + it, j, W_WIDE if j == 0 else next_width)
                        dve.wait_ge(unit_used, turn0 * 4 + it * 4 + (2 * j + 2 + START))
                        resid(alpha, it * 2 + j, 4 + j, T)

                with dve.Fori(0, DOWN_T - 1) as it:
                    turn(it, W_WIDE)
                turn(DOWN_T - 1, W_NARROW)

            def out_proj(turn0, alpha, T):
                for p in range(OUTB // 2):
                    split_next(turn0 + p // 2, p % 2, W_NARROW)
                    for u in range(2):
                        dve.wait_ge(unit_used, turn0 * 4 + (2 * p + u + 1 + START))
                        resid(alpha, 2 * p + u, 4 + u, T)

            def in_proj(turn0, n):
                with dve.Fori(0, n // 4) as it:
                    for j in range(2):
                        split_next(turn0 + it, j, W_NARROW)

            def norm_chunks(number, event, gain, table, T, src):
                dve.wait_ge(std_ready, number + 1)
                v.reciprocal(std[:, 1, 0:T], std[:, 0, 0:T])
                dve.drain()

                def low(k):
                    dve.wait_ge(xh_ready, number * KD + (k + 1))
                    v.tensor_tensor(x_lo[:, k, 0:T], src[:, k, 0:T], x_hi[:, k, 0:T].bitcast(F32), ALU.subtract)\
                        .then_inc(x_ready, 1)

                for k in range(KD):
                    v.scalar_tensor_tensor(out=pj[:, k, 0:T], in0=h[:, k, T1 - T:T1], scalar=par(table, gain, k),
                                           in1=std[:, 1, 0:T], op0=ALU.mult, op1=ALU.mult).then_inc(xn_ready, 1)
                    if k >= 2:
                        low(k - 2)
                low(KD - 2)
                low(KD - 1)

            def layer_norm(norm, event, gain):
                dve.wait_ge(mean_ready, norm + 1)
                for s in range(2):
                    c = slice(4 * s, 4 * s + 4)
                    v.tensor_tensor(h[:, c, :], h[:, c, :], ps[:, 6:7, 0:T1].broadcast_to([P, 4, T1]), ALU.subtract)\
                        .then_inc(centered, 1)
                norm_chunks(norm, event, gain, P1, T1, h)

            def rms_norm(number, event, gain):
                norm_chunks(number, event, gain, P2, T2, pj)

            def cat_low(l, hi, T):
                for k in range(KD):
                    dve.wait_ge(hi.sem, hi.at(l, k + 1))
                    v.tensor_tensor(x_lo[:, k, 0:T], pj[:, k, 0:T], x_hi[:, k, 0:T].bitcast(F32), ALU.subtract)\
                        .then_inc(x_ready, 1)

            def mixer1(l):
                dve.wait_ge(proj_ready.sem, proj_ready.at(l, IN1))
                v.tensor_scalar(row_u[ROWS, :], pj[ROWS, MISC, :], par(P1, "rowbias", rows=ROWS),
                                par(P1, "rowsign", rows=ROWS), ALU.add, ALU.mult).then_inc(rows_u.sem, 1)
                dve.wait_ge(conv_seed.sem, conv_seed.at(l, 6))
                for d in range(1, CONV):
                    for c in range(6):
                        last = v.scalar_tensor_tensor(out=xc[:, c, d:T1], in0=pj[:, XBC0 + c, 0:T1 - d],
                                                      scalar=par(P1, "convw", CONV * c + CONV - 1 - d),
                                                      in1=xc[:, c, d:T1], op0=ALU.mult, op1=ALU.add)
                    if d < CONV - 1:
                        dve.drain()
                last.then_inc(conv_done.sem, 1)
                dve.wait_ge(mla_std.sem, mla_std.at(l, 1))
                v.reciprocal(std[:, :, :], std[:, :, :])
                dve.drain()
                for b in range(3):
                    gain = par(P1, "qg", b) if b < 2 else par(P1, "kvg")
                    last = v.scalar_tensor_tensor(out=cqn[:, b, :], in0=pj[:, CQ0 + b, :], scalar=gain,
                                                  in1=std[:, b // 2, :], op0=ALU.mult, op1=ALU.mult)
                last.then_inc(cqn_ready.sem, 1)

                def rotate(dst, plain, bank, ready):
                    v.tensor_tensor(rot_t[:, 0, :], plain, con("cos", T1), ALU.mult)
                    v.tensor_tensor(rot_t[:, 1, :], ps[:, bank, 0:T1], con("sin", T1), ALU.mult)
                    dve.drain()
                    v.tensor_tensor(dst, rot_t[:, 0, :], rot_t[:, 1, :], ALU.add).then_inc(ready.sem, 1)

                dve.wait_ge(kr_raw.sem, kr_raw.at(l, 1))
                rotate(kr, ps[:, 0, 0:T1], 1, kr_ready)
                dve.wait_ge(ukv_done.sem, ukv_done.at(l, 1))
                v.tensor_copy(kn, ps[:, 4:6, 0:T1])
                v.tensor_copy(vmla[:, 0:2, :], ps[:, 7, :].rearrange("p (a b) -> p a b", a=2))
                v.tensor_copy(vmla[0:16, 2, :], ps[0:16, 0, 0:256]).then_inc(kv_ready.sem, 1)
                dve.wait_ge(qrot_done.sem, qrot_done.at(l, 1))
                rotate(qr, qraw, 1, qr_ready)
                v.memset(row_cum[0:ROW0, :], 0.0)
                dve.wait_ge(rows_ln.sem, rows_ln.at(l, 1))
                v.scalar_tensor_tensor(out=row_sp[ROWS, :], in0=row_u[ROWS, :], scalar=0.0, in1=row_l[ROWS, :],
                                       op0=ALU.max, op1=ALU.add)
                dve.drain()
                v.tensor_scalar(row_u[ROWS, :], row_sp[ROWS, :], acoef[ROWS, :], -1.0, ALU.mult, ALU.mult)
                dve.drain()
                v.tensor_tensor_scan(row_cum[ROWS, :], con("one", 1, ROWS).broadcast_to([P - ROW0, T1]), row_u[ROWS, :],
                                     0.0, ALU.mult, ALU.add).then_inc(rows_ready.sem, 1)
                dve.wait_ge(xs_t.sem, xs_t.at(l, 1))
                v.tensor_copy(xtok[:, 0:2, :], ps[:, 2:4, :])
                v.tensor_copy(xtok[0:16, 2, :], ps[0:16, 4, :])
                dve.wait_ge(rows_t.sem, rows_t.at(l, 1))
                rows = ps[:, 5, 0:384].rearrange("p (i r c) -> p i r c", i=3, r=2)
                v.tensor_scalar(tok_ncum[:, 0:2, :], rows[:, 0:2, 0, :], -1.0, None, ALU.mult)
                v.tensor_scalar(tok_ncum[0:16, 2, :], rows[0:16, 2, 0, :], -1.0, None, ALU.mult)
                v.tensor_copy(tok_dt[:, 0:2, :], rows[:, 0:2, 1, :])
                v.tensor_copy(tok_dt[0:16, 2, :], rows[0:16, 2, 1, :]).then_inc(tok_ready.sem, 1)

                def gate(c):
                    dve.wait_ge(y_ready.sem, y_ready.at(l, 2 * c + 2))
                    v.scalar_tensor_tensor(out=xc[:, c, :], in0=xc[:, c, :], scalar=par(P1, "dskip", c),
                                           in1=ps[:, 4 + c % 2, 0:T1], op0=ALU.mult, op1=ALU.add)
                    dve.drain()
                    v.tensor_tensor(xc[:, c, :], xc[:, c, :], pj[:, Z0 + c, :], ALU.mult).then_inc(yz_ready.sem, 1)

                dve.drain()
                for hh in range(SSD_HEADS):
                    dve.wait_ge(g_ready.sem, g_ready.at(l, hh // 4 + 1))
                    dve.wait_ge(decay.sem, decay.at(l, hh + 1))
                    if hh >= 2:
                        dve.wait_ge(y_ready.sem, y_ready.at(l, hh - 1))
                    for i, (t, n) in enumerate(TILES):
                        c = slice(TRI[i], TRI[i] + TRI_W[i])
                        last = v.scalar_tensor_tensor(out=ptr[0:n, hh % 2, c], in0=ps[0:n, hh // 4, c],
                                                      scalar=tok_dt[0:n, i, hh:hh + 1], in1=decays[hh % 2][0:n, c],
                                                      op0=ALU.mult, op1=ALU.mult)
                    last.then_inc(ssd_w.sem, 1)
                    if hh % 2 == 0 and hh >= 2:
                        gate(hh // 2 - 1)
                gate(3)
                dve.wait_ge(ystd_ready.sem, ystd_ready.at(l, 1))
                v.reciprocal(std[:, :, :], std[:, :, :])
                dve.drain()
                for c in range(4):
                    last = v.scalar_tensor_tensor(out=pj[:, c, :], in0=xc[:, c, :], scalar=par(P1, "ssdg", c),
                                                  in1=std[:, c // 2, :], op0=ALU.mult, op1=ALU.mult)
                last.then_inc(ssd_cat.sem, 1)

                def maxima(n_):
                    dve.wait_ge(s_ready.sem, s_ready.at(l, n_ + 1))
                    s = n_ % 2
                    for i, (t, n) in enumerate(TILES):
                        bank, col, kw = S_BANK[i]
                        v.reduce_max(amax[0:n, s, i:i + 1], ps[0:n, 2 * s + bank, col:col + kw], AX_X)
                    dve.drain()
                    scale = -(FOX_SCALE if n_ < FOX_HEADS else MLA_SCALE)
                    v.tensor_scalar(nmax[:, s, 0:2], amax[:, s, 0:2], scale, None, ALU.mult)
                    v.tensor_scalar(nmax[0:16, s, 2:3], amax[0:16, s, 2:3], scale, None, ALU.mult)\
                        .then_inc(nm_ready.sem, 1)

                def normalise(n_):
                    dve.wait_ge(exp_done.sem, exp_done.at(l, n_ + 1))
                    s = n_ % 2
                    v.reciprocal(rsum[:, s, 0:2], asum[:, s, 0:2])
                    v.reciprocal(rsum[0:16, s, 2:3], asum[0:16, s, 2:3])
                    dve.drain()
                    for i, (t, n) in enumerate(TILES):
                        kw = S_BANK[i][2]
                        p = prob[0:n, s, i, 0:kw]
                        last = v.tensor_scalar(p, p, rsum[0:n, s, i:i + 1], None, ALU.mult)
                    last.then_inc(p_ready.sem, 1)

                maxima(0)
                for n_ in range(NH):
                    if n_ + 1 < NH:
                        maxima(n_ + 1)
                    normalise(n_)
                cat_low(l, cat_hi, T1)

            def mixer2(l):
                lq = par(P2, "lamq", 0, 128)
                v.tensor_tensor(prod[:, 0, 0:128], lq, par(P2, "lamk", 0, 128), ALU.mult)
                dve.drain()
                v.reduce_sum(lam_s, prod[:, 0, 0:128].rearrange("p (a b) -> p a b", a=2), AX_X).then_inc(lam_dot.sem, 1)
                v.tensor_scalar(g_lam, par(P2, "headg", 0, 4), par(P2, "onemlam"), None, ALU.mult)
                dve.wait_ge(lam_exp.sem, lam_exp.at(l, 1))
                v.tensor_scalar(neg_lam, lam_e[:, 1:2], lam_e[:, 0:1], par(P2, "laminit"), ALU.subtract, ALU.subtract)
                dve.wait_ge(v_t.sem, v_t.at(l, 1))
                v.tensor_copy(vtok, ps[:, 2:4, :]).then_inc(v_ready.sem, 1)
                dve.wait_ge(pm_done.sem, pm_done.at(l, 1))
                v.tensor_copy(poolm, ps[:, 4, :].rearrange("p (a t) -> p a t", a=2)).then_inc(pm_ready.sem, 1)
                dve.wait_ge(py_done.sem, py_done.at(l, 1))
                for b in range(2):
                    last = v.tensor_scalar(pj[:, b, 0:T2], ps[:, 5, 256 * b:256 * b + T2], par(P2, "pscale", b), None,
                                           ALU.mult)
                last.then_inc(pool_cat.sem, 1)

                def maxima(hh):
                    dve.wait_ge(s2_ready.sem, s2_ready.at(l, hh + 1))
                    s = hh % 2
                    v.reduce_max(amax[:, s, :], ps[:, 2 * s:2 * s + 2, :].rearrange("p j (i k) -> p (j i) k", i=2), AX_X)
                    dve.drain()
                    v.tensor_scalar(nmax[:, s, :], amax[:, s, :], -ATT_SCALE, None, ALU.mult).then_inc(nm2_ready.sem, 1)

                def difference(hh):
                    dve.wait_ge(exp2_done.sem, exp2_done.at(l, hh + 1))
                    if hh >= 2:
                        dve.wait_ge(t2_ready.sem, t2_ready.at(l, hh - 1))
                    s = hh % 2
                    v.reciprocal(rsum[:, s, :], asum[:, s, :])
                    dve.drain()
                    v.tensor_scalar(rlam[:, s, :], rsum[:, s, 2:4], neg_lam, None, ALU.mult)
                    for i in range(2):
                        v.tensor_scalar(prob2[:, s, i, :], prob2[:, s, i, :], rsum[:, s, i:i + 1], None, ALU.mult)
                    dve.drain()
                    for i in range(2):
                        last = v.scalar_tensor_tensor(out=attn[:, s, i, :], in0=prob2[:, s, 2 + i, :],
                                                      scalar=rlam[:, s, i:i + 1], in1=prob2[:, s, i, :],
                                                      op0=ALU.mult, op1=ALU.add)
                    last.then_inc(a2_ready.sem, 1)

                maxima(0)
                for hh in range(ATT_HEADS):
                    if hh + 1 < ATT_HEADS:
                        maxima(hh + 1)
                    difference(hh)
                dve.wait_ge(o2_std.sem, o2_std.at(l, 1))
                v.reciprocal(std4, std4)
                dve.drain()
                for hh in range(ATT_HEADS):
                    o = pj[:, 4 + hh, 0:T2]
                    last = v.scalar_tensor_tensor(out=o, in0=o, scalar=g_lam[:, hh:hh + 1], in1=std4[:, hh, :],
                                                  op0=ALU.mult, op1=ALU.mult)
                last.then_inc(att_cat.sem, 1)
                cat_low(l, cat2_hi, T2)

            dve.nop().then_inc(up_free, CREDIT)
            dve.nop().then_inc(resid_ready, CREDIT)
            dve.nop().then_inc(prm_free, START)
            dve.wait_ge(h_in, 16)
            for k in range(KD):
                dve.wait_ge(xh_first, k + 1)
                v.tensor_tensor(x_lo[:, k, :], h[:, k, :], x_hi[:, k, :].bitcast(F32), ALU.subtract).then_inc(x_ready, 1)
            split_lo(0, 0, W_NARROW)
            dve.wait_ge(consts_in, 16)
            with dve.Fori(0, DEPTH) as l:
                t0, q, r0 = l * TURNS1, l * 2, l * 3
                up(q, t0 + SEC1["ffn1"], T1)
                down(t0 + SEC1["ffn1"] + UP_T, ALPHA, T1)
                dve.wait_ge(prm_in, l * 16 + 16)
                layer_norm(r0, None, "ln1g")
                in_proj(t0 + SEC1["in"], IN1)
                mixer1(l)
                out_proj(t0 + SEC1["out"], ALPHA, T1)
                layer_norm(r0 + 1, None, "ln2g")
                up(q + 1, t0 + SEC1["ffn2"], T1)
                down(t0 + SEC1["ffn2"] + UP_T, ALPHA, T1)
                layer_norm(r0 + 2, None, "ln3g")
                dve.drain().then_inc(prm_free, 1)
            dve.wait_ge(prm_in, 16 * DEPTH + 16)
            rms_norm(3 * DEPTH, None, "firstg")
            with dve.Fori(0, DEPTH) as l:
                t0, q = l * TURNS2 + BLOCK2_TURN, l * 2 + 2 * DEPTH
                n0 = l * 3 + NORM2
                up(q, t0 + SEC2["ffn1"], T2)
                down(t0 + SEC2["ffn1"] + UP_T, 1.0, T2)
                dve.wait_ge(prm_in, l * 16 + (16 * DEPTH + 16))
                rms_norm(n0, None, "mixg")
                in_proj(t0 + SEC2["in"], IN2)
                mixer2(l)
                out_proj(t0 + SEC2["out"], 1.0, T2)
                rms_norm(n0 + 1, None, "ffn2g")
                up(q + 1, t0 + SEC2["ffn2"], T2)
                down(t0 + SEC2["ffn2"] + UP_T, 1.0, T2)
                rms_norm(n0 + 2, None, "nextg")
                dve.drain().then_inc(prm_free, 1)


def blocks_of(w, n_chunks):
    k, n = w.shape
    return w.reshape(n_chunks, P, n // P, P).transpose(2, 1, 0, 3).reshape(n // P, P, n_chunks * P)


def in_pairs(b):
    n, p, w = b.shape
    return b.reshape(n // 2, 2, p, w).transpose(0, 2, 1, 3).reshape(n // 2, p, 2 * w)


def columns(v):
    return v.reshape(-1, P).T


def kernel(**inputs):
    import concourse.bacc as bacc
    from concourse.bass_utils import run_bass_kernel_spmd

    a = {k: np.asarray(v) for k, v in inputs.items()}
    f32 = np.float32
    ffn = [(s, f, l) for s in ("", "_2") for l in range(DEPTH) for f in ("ffn1", "ffn2")]
    w_up = np.zeros((len(ffn) * NF + PAD_PAIRS, P, 2 * W_NARROW), f32)
    w_down = np.zeros((len(ffn) * KD, P, 2 * W_WIDE), f32)
    for n, (s, f, l) in enumerate(ffn):
        w_up[n * NF:(n + 1) * NF, :, 0:W_NARROW] = blocks_of(a[f"{f}_w_gate{s}"][l], KD)
        w_up[n * NF:(n + 1) * NF, :, W_NARROW:] = blocks_of(a[f"{f}_w_up{s}"][l], KD)
        w_down[n * KD:(n + 1) * KD] = blocks_of(a[f"{f}_w_down{s}"][l], NF)
    hd2 = HD + ROPE
    w_in1, prm1, prm2 = [], np.zeros((DEPTH, P, P1_W), f32), np.zeros((DEPTH, P, P2_W), f32)
    for l in range(DEPTH):
        w = a["w_in"][l]
        z, xbc, dt, fq, fk, fv, fr, cq, ckv, kr = np.split(w, np.cumsum([512, 768, 8, 256, 256, 256, 4, 256, 128])
                                                           .tolist(), axis=1)
        misc = np.zeros((D, P), f32)
        misc[:, 0:ROPE], misc[:, ROW0:ROW0 + 8], misc[:, FROW0:FROW0 + 4] = kr, dt, fr
        w_in1.append(in_pairs(blocks_of(np.concatenate([z, xbc, fq, fk, fv, cq, ckv, misc], axis=1), KD)))

        p = prm1[l]

        def put(table, dst, name, v):
            dst[:, table[name]:table[name] + v.shape[1]] = v

        for name, key in (("ln1g", "ln1_g"), ("ln1b", "ln1_b"), ("ln2g", "ln2_g"), ("ln2b", "ln2_b"), ("ln3g", "ln3_g"),
                          ("ln3b", "ln3_b"), ("convb", "conv_b"), ("ssdg", "ssd_norm_g"), ("qg", "mla_q_norm_g"),
                          ("kvg", "mla_kv_norm_g")):
            put(P1, p, name, columns(a[key][l]))
        put(P1, p, "convw", a["conv_w"][l].reshape(CONV, 6, P).transpose(2, 1, 0).reshape(P, 6 * CONV))
        put(P1, p, "dskip", columns(np.repeat(a["d_skip"][l], HD)))
        p[ROW0:ROW0 + 8, P1["rowbias"]] = a["dt_bias"][l]
        p[FROW0:FROW0 + 4, P1["rowbias"]] = a["fox_f_b"][l]
        p[ROW0:ROW0 + 8, P1["rowsign"]] = 1.0
        p[FROW0:FROW0 + 4, P1["rowsign"]] = -1.0
        p[ROW0:ROW0 + 8, P1["alog"]] = a["a_log"][l]
        uq = a["mla_w_uq"][l].reshape(256, MLA_HEADS, hd2)
        uq = np.concatenate([uq[:, :, :HD].reshape(256, -1), uq[:, :, HD:].reshape(256, -1)], axis=1)
        put(P1, p, "uq", uq.reshape(2, P, 384).transpose(1, 0, 2).reshape(P, -1))
        ukv = a["mla_w_ukv"][l].reshape(P, MLA_HEADS, 2 * HD)
        put(P1, p, "ukv", np.concatenate([ukv[:, :, :HD].reshape(P, -1), ukv[:, :, HD:].reshape(P, -1)], axis=1))

        p = prm2[l]
        last = l == DEPTH - 1
        put(P2, p, "mixg", columns(a["mix_norm_2"][l]))
        put(P2, p, "ffn2g", columns(a["ffn2_norm_2"][l]))
        put(P2, p, "nextg", columns(a["final_norm_2"] if last else a["ffn1_norm_2"][l + 1]))
        put(P2, p, "firstg", columns(a["ffn1_norm_2"][0]))
        put(P2, p, "pscale", columns(a["pool_scale_2"][l]))
        put(P2, p, "headg", columns(a["attn_head_norm_2"][l]))
        lam_init = 0.8 - 0.6 * np.exp(-0.3 * l)
        p[:, P2["laminit"]] = lam_init
        p[:, P2["onemlam"]] = 1.0 - lam_init
        put(P2, p, "lamq", np.broadcast_to(np.concatenate([a["lam_q1_2"][l], a["lam_q2_2"][l]]), (P, 128)))
        put(P2, p, "lamk", np.broadcast_to(np.concatenate([a["lam_k1_2"][l], a["lam_k2_2"][l]]), (P, 128)))
        put(P2, p, "poolw", a["pool_w_2"][l].reshape(2, P, 64).transpose(1, 0, 2).reshape(P, -1))
        put(P2, p, "fourw", a["fourier_w_2"][l].reshape(2, P, 256).transpose(1, 0, 2).reshape(P, -1))
    w_out1 = [in_pairs(blocks_of(a["w_out"][l], KD)) for l in range(DEPTH)]
    w_in2 = [in_pairs(blocks_of(a["w_in_2"][l], KD)) for l in range(DEPTH)]
    w_out2 = [in_pairs(blocks_of(a["w_out_2"][l], KD)) for l in range(DEPTH)]
    hidden = np.concatenate([a["meta"], a["x"][0]], axis=0)
    arrays = {
        "hidden0": np.ascontiguousarray(hidden.T.reshape(KD, P, T1).transpose(1, 0, 2)),
        "w_up": w_up,
        "w_down": w_down,
        "w_in1": np.concatenate(w_in1),
        "w_out1": np.concatenate(w_out1),
        "w_in2": np.concatenate(w_in2),
        "w_out2": np.concatenate(w_out2),
        "prm1": prm1,
        "prm2": prm2,
        "consts": shape_constants(),
    }
    nc = bacc.Bacc("TRN2", target_bir_lowering=False, num_devices=1)
    args = [nc.dram_tensor(f"in_{n}", v.shape, mybir.dt.from_np(v.dtype), kind="ExternalInput").ap()
            for n, v in arrays.items()]
    args.append(nc.dram_tensor("out_0", (P, KD, T2), F32, kind="ExternalOutput").ap())
    build(nc, *args)
    r = run_bass_kernel_spmd(nc, [{f"in_{n}": v for n, v in arrays.items()}], core_ids=[0])
    y = np.asarray(r.results[0]["out_0"])
    return np.ascontiguousarray(y.transpose(1, 0, 2).reshape(D, T2).T)[None]
```

```python
from contextlib import ExitStack

import numpy as np

import concourse.bass as bass
from concourse import mybir

F32 = mybir.dt.float32
F32R = mybir.dt.float32r
BF16 = mybir.dt.bfloat16
ALU = mybir.AluOpType
ACT = mybir.ActivationFunctionType
AX_X = mybir.AxisListType.X

P = 128
D = 1024
KD = D // P
DEPTH = 2
SEQ = 256
N_META = 16
T1 = SEQ + N_META
T2 = SEQ
D_FF = 2816
NF = D_FF // P
HALF_F = NF // 2
ALPHA = (2 * DEPTH) ** 0.25
EPS1, EPS2 = 1e-5, 1e-6

W_NARROW = KD * P
W_WIDE = HALF_F * P
IN1, IN2, OUTB = 20, 16, 8
UP_PAIRS, DOWN_PAIRS = NF, KD
FFN_PAIRS = UP_PAIRS + DOWN_PAIRS
LAYER1_PAIRS = 2 * FFN_PAIRS + IN1 // 2 + OUTB // 2
LAYER2_PAIRS = 2 * FFN_PAIRS + IN2 // 2 + OUTB // 2
BLOCK2_PAIR0 = DEPTH * LAYER1_PAIRS
PAD_PAIRS = 2

MISC, CKV, CQ0, XBC0, Z0, FQ0, FK0, FV0 = 0, 1, 2, 4, 10, 14, 16, 18
SSD_HEADS, FOX_HEADS, MLA_HEADS, HD, ROPE = 8, 4, 4, 64, 32
CONV = 4
ROW0 = 64
FROW0 = 96
MLA_SCALE = float(np.float32((HD + ROPE) ** -0.5))
FOX_SCALE = HD ** -0.5
MASK = -1e30
TILES = [(0, 128), (128, 128), (256, 16)]
TRI = [0, 272, 416]
TRI_W = [T1 - t for t, _ in TILES]
QTILES = [(0, N_META), (N_META, P), (N_META + P, P)]
KEYS = [t + n for t, n in QTILES]
S_COL = [0, KEYS[0], KEYS[0] + KEYS[1]]
S_W = sum(KEYS)
PT_K1, PT_META, PT_END1, PT_END2, PT_W = 2 * P, 3 * P, 3 * P + N_META, 3 * P + N_META + 48, 4 * P

P1 = {}
_n = 0
for _name, _w in (("ln1g", 8), ("ln1b", 8), ("ln2g", 8), ("ln2b", 8), ("ln3g", 8), ("ln3b", 8), ("convw", 24),
                  ("convb", 6), ("dskip", 4), ("ssdg", 4), ("qg", 2), ("kvg", 1), ("rowbias", 1), ("rowsign", 1),
                  ("alog", 1), ("uq", 2 * 384), ("ukv", 512)):
    P1[_name] = _n
    _n += _w
P1_W = _n
P2 = {}
_n = 0
for _name, _w in (("mixg", 8), ("ffn2g", 8), ("nextg", 8), ("firstg", 8), ("pscale", 2), ("headg", 4), ("laminit", 1),
                  ("onemlam", 1), ("lamq", 128), ("lamk", 128), ("poolw", 128), ("fourw", 512)):
    P2[_name] = _n
    _n += _w
P2_W = _n
PRM_W = max(P1_W, P2_W)
ATT_HEADS = 4
POOL_WINDOWS = (2, 4, 8, 16)
ATT_SCALE = 64 ** -0.5

CC = {}
_n = 0
for _name, _w in (("ident", 128), ("maskS", 128), ("maskA", 128), ("onesD", 128), ("ones256", 128), ("ones128", 128), ("rot", 128), ("rep", 128),
                  ("reprot", 128), ("cos", T1), ("sin", T1), ("sel", 12 * 128), 
                  ("eps1", 1), ("eps2", 1), ("one", 1), ("band", 4 * 2 * 256), ("cs", 512), ("ss", 512),
                  ("ccos", 128), ("csin", 128), ("absd", 512), ("slope", 4 * 128)):
    CC[_name] = _n
    _n += _w
CC_W = _n
CC_FIRST = CC["band"]


def shape_constants():
    c = np.zeros((P, CC_W), np.float32)

    def put(name, a, rows=slice(0, P)):
        a = np.asarray(a, np.float64).astype(np.float32)
        c[rows, CC[name]:CC[name] + a.shape[1]] = a

    put("ident", np.eye(P))
    put("onesD", np.full((P, P), 1.0 / D))
    put("ones256", np.full((P, P), 1.0 / 256))
    put("ones128", np.full((P, P), 1.0 / 128))
    r32 = np.zeros((32, 32))
    for i in range(16):
        r32[16 + i, i] = -1.0
        r32[i, 16 + i] = 1.0
    put("rot", np.kron(np.eye(4), r32))
    put("rep", np.tile(np.eye(32), (1, 4)), slice(0, 32))
    put("reprot", np.tile(r32, (1, 4)), slice(0, 32))
    inv = (1.0 / (10000.0 ** (np.arange(0, ROPE, 2, dtype=np.float32) / np.float32(ROPE)))).astype(np.float32)
    ang = (np.arange(T1, dtype=np.float32)[:, None] * inv[None, :]).astype(np.float32).astype(np.float64)
    idx = (np.arange(P) % 32) % 16
    put("cos", np.cos(ang).T[idx])
    put("sin", np.sin(ang).T[idx])
    sel = np.zeros((P, 12, 128))
    for h in range(8):
        sel[ROW0 + h, h] = 1.0
    for h in range(4):
        sel[FROW0 + h, 8 + h] = -1.0 / FOX_SCALE
    put("sel", sel.reshape(P, -1))
    a = np.arange(P)
    put("maskS", np.where(a[None, :] < a[:, None], MASK, 0.0))
    put("maskA", np.where(a[None, :] > a[:, None], MASK, 0.0))
    put("eps1", np.full((P, 1), EPS1))
    put("eps2", np.full((P, 1), EPS2))
    put("one", np.ones((P, 1)))
    band = np.zeros((4, 256, 256))
    for g, w in enumerate(POOL_WINDOWS):
        for t in range(256):
            lo, hi = max(t - w // 2, 0), min(t + w - w // 2, 256)
            band[g, lo:hi, t] += 1.0 / (hi - lo)
            band[g, t, t] -= 1.0
    put("band", band.reshape(4, 2, P, 256).transpose(2, 0, 1, 3).reshape(P, -1))
    s = np.arange(256)
    ang = 2 * np.pi * ((s[:, None] * s[None, :]) % 256) / 256
    put("cs", np.cos(ang).reshape(2, P, 256).transpose(1, 0, 2).reshape(P, -1))
    put("ss", np.sin(ang).reshape(2, P, 256).transpose(1, 0, 2).reshape(P, -1))
    m = np.arange(64)
    ang = 2 * np.pi * ((m[:, None] * m[None, :]) % 64) / 64
    ortho = 1.0 / np.sqrt(256 * 64)
    put("ccos", np.kron(np.eye(2), np.cos(ang) * ortho))
    put("csin", np.kron(np.eye(2), -np.sin(ang) * ortho))
    q = np.arange(256)
    absd = np.abs(q[:, None] - q[None, :])
    put("absd", absd.reshape(2, P, 256).transpose(1, 0, 2).reshape(P, -1))
    slopes = [2.0 ** (-8.0 * (i + 1) / ATT_HEADS) for i in range(ATT_HEADS)]
    put("slope", np.concatenate([np.eye(P) * (-sl / ATT_SCALE) for sl in slopes], axis=1))
    return c


class Signal:

    def __init__(self, sem, per_layer, start):
        self.sem, self.per_layer, self.start = sem, per_layer, start

    def at(self, layer, n):
        return layer * self.per_layer + (n + self.start)


def build(nc, hidden0, w_up, w_down, w_in1, w_out1, w_in2, w_out2, prm1, prm2, consts, out):
    with ExitStack() as ctx:
        def sb(name, shape, dt=F32):
            return ctx.enter_context(nc.sbuf_tensor(name, shape, dt))

        def sem(name):
            return ctx.enter_context(nc.semaphore(name))

        def signal(name, per_layer, start=0):
            return Signal(sem(name), per_layer, start)

        raw = sb("raw", [P, 2, 2 * W_WIDE])
        w_hi = sb("w_hi", [P, 2, 2 * W_WIDE], F32R)
        w_lo = sb("w_lo", [P, 2, 2 * W_WIDE], F32R)
        x_hi = sb("x_hi", [P, KD, T1], F32R)
        x_lo = sb("x_lo", [P, KD, T1], F32R)
        h = sb("h", [P, KD, T1])
        pj = sb("pj", [P, IN1, T1])
        silu = sb("silu", [P, 2, T1])
        prod = sb("prod", [P, 2, T1])
        prm = sb("prm", [P, PRM_W])
        cst = sb("cst", [P, CC_W])
        std = sb("std", [P, 2, T1])
        small = sb("small", [P, 96])
        masks = sb("masks", [P, 3 * P], BF16)
        hid_hi = sb("hid_hi", [P, NF, T1], F32R)
        hid_lo = sb("hid_lo", [P, NF, T1], F32R)
        HID_BYTES = NF * T1 * 4
        hid_at = nc.sbuf_base - 2 * HID_BYTES
        SCRATCH = 2 * NF * T1
        scr = nc.alloc_sbuf_tensor_at("scratch", [P, SCRATCH], F32, offset=hid_at)
        ps = ctx.enter_context(nc.psum_tensor("ps", [P, 8, 512], F32))

        used = [0]

        def take(*shape):
            n = int(np.prod(shape))
            a = scr[:, used[0]:used[0] + n]
            used[0] += n
            assert used[0] <= SCRATCH
            if len(shape) == 2:
                a = a.rearrange("p (a b) -> p a b", a=shape[0])
            if len(shape) == 3:
                a = a.rearrange("p (a b c) -> p a b c", a=shape[0], b=shape[1])
            return a

        def con(name, w=128, rows=slice(0, P)):
            return cst[rows, CC[name]:CC[name] + w]

        def par(table, name, k=0, w=1, rows=slice(0, P)):
            return prm[rows, table[name] + k:table[name] + k + w]

        ident = con("ident")

        h_in = sem("h_in")
        consts_in = sem("consts_in")
        prm_in = sem("prm_in")
        prm_free = sem("prm_free")
        stored = sem("stored")
        raw_landed = [sem("raw_landed0"), sem("raw_landed1")]
        hi_done = sem("hi_done")
        lo_done = sem("lo_done")
        unit_used = sem("unit_used")
        xh_first = sem("xh_first")
        x_ready = sem("x_ready")
        silu_done = sem("silu_done")
        up_free = sem("up_free")
        hid_ready = sem("hid_ready")
        resid_ready = sem("resid_ready")
        mean_ready = sem("mean_ready")
        centered = sem("centered")
        ln_sq = sem("ln_sq")
        rms_sq = sem("rms_sq")
        var_ready = sem("var_ready")
        std_ready = sem("std_ready")
        xn_ready = sem("xn_ready")
        h_ready = sem("h_ready")
        xh_ready = sem("xh_ready")
        CREDIT, START = 2, 1
        masks_ready = sem("masks_ready")

        NH = FOX_HEADS + MLA_HEADS
        conv_seed = signal("conv_seed", 6)
        conv_done = signal("conv_done", 1)
        xc_ready = signal("xc_ready", 1)
        proj_ready = signal("proj_ready", IN1, START)
        rows_u = signal("rows_u", 1)
        rows_ln = signal("rows_ln", 1)
        rows_ready = signal("rows_ready", 1)
        mla_sq = signal("mla_sq", 1)
        mla_ss = signal("mla_ss", 1)
        mla_std = signal("mla_std", 1)
        cqn_ready = signal("cqn_ready", 1)
        kr_raw = signal("kr_raw", 1)
        kr_ready = signal("kr_ready", 1)
        uq_done = signal("uq_done", 1)
        ukv_done = signal("ukv_done", 1)
        qn_ready = signal("qn_ready", 1)
        kv_ready = signal("kv_ready", 1)
        qrot_done = signal("qrot_done", 1)
        qr_ready = signal("qr_ready", 1)
        vf_t = signal("vf_t", 1)
        vf_ready = signal("vf_ready", 1)
        xs_t = signal("xs_t", 1)
        rows_t = signal("rows_t", 1)
        tokrow_ready = signal("tokrow_ready", 1)
        tok_ready = signal("tok_ready", 1)
        g_ready = signal("g_ready", 2)
        d_ready = signal("d_ready", SSD_HEADS)
        decay = signal("decay", SSD_HEADS)
        ssd_w = signal("ssd_w", SSD_HEADS)
        y_ready = signal("y_ready", SSD_HEADS)
        yz_ready = signal("yz_ready", 4)
        sqy_ready = signal("sqy_ready", 1)
        yss_ready = signal("yss_ready", 1)
        ystd_ready = signal("ystd_ready", 1)
        ssd_cat = signal("ssd_cat", 1)
        s_ready = signal("s_ready", NH)
        nm_ready = signal("nm_ready", NH)
        exp_done = signal("exp_done", NH)
        p_ready = signal("p_ready", NH)
        t_ready = signal("t_ready", NH)
        pt_ready = signal("pt_ready", NH)
        o_ready = signal("o_ready", NH)
        cat_hi = signal("cat_hi", KD)
        proj2_ready = signal("proj2_ready", IN2, START)
        af_t = signal("af_t", 1)
        af_ready = signal("af_ready", 1)
        v_t = signal("v_t", 1)
        v_ready = signal("v_ready", 1)
        pm_done = signal("pm_done", 1)
        pm_ready = signal("pm_ready", 1)
        uv_done = signal("uv_done", 1)
        uv_ready = signal("uv_ready", 1)
        py_done = signal("py_done", 1)
        pool_cat = signal("pool_cat", 1)
        f2_done = signal("f2_done", 1)
        f2_ready = signal("f2_ready", 1)
        f3_done = signal("f3_done", 1)
        lam_dot = signal("lam_dot", 1)
        lam_exp = signal("lam_exp", 1)
        s2_ready = signal("s2_ready", ATT_HEADS)
        nm2_ready = signal("nm2_ready", ATT_HEADS)
        exp2_done = signal("exp2_done", ATT_HEADS)
        a2_ready = signal("a2_ready", ATT_HEADS)
        t2_ready = signal("t2_ready", ATT_HEADS)
        at2_ready = signal("at2_ready", ATT_HEADS)
        o2_ready = signal("o2_ready", ATT_HEADS)
        o2_sq = signal("o2_sq", 1)
        o2_ss = signal("o2_ss", 1)
        o2_std = signal("o2_std", 1)
        att_cat = signal("att_cat", 1)
        cat2_hi = signal("cat2_hi", KD)

        xc = take(6, T1)
        xtok = take(3, 512)
        tok_ncum = take(3, 64)
        tok_dt = take(3, 64)
        vfox = take(3, 256)
        vmla = take(3, 256)
        cqn = take(3, T1)
        qn = take(2, T1)
        qr = take(T1)
        kn = take(2, T1)
        kr = take(T1)
        qraw = take(T1)
        rot_t = take(2, T1)
        row_u = take(T1)
        row_l = take(T1)
        row_sp = take(T1)
        row_cum = take(T1)
        prob = take(3, S_W)
        ptr = take(2, PT_W)
        lat_sq = prob.rearrange("p a w -> p (a w)")[:, 0:3 * T1].rearrange("p (a t) -> p a t", a=3)
        ssd_sq = (silu, prod)
        used[0] = 0
        aftok = take(2, 512)
        vtok = take(2, 512)
        poolm = take(2, T2)
        uu = take(2, T2)
        vv = take(2, T2)
        y4 = take(2, T2)
        prob2 = take(2, 4, T2)
        attn = take(2, 2, T2)
        attn_t = take(2, 2, T2)
        sqo = take(4, T2)
        std4 = take(4, T2)
        ROWS = slice(ROW0, P)
        head_rows = lambda hh: slice(64 * (hh % 2), 64 * (hh % 2) + 64)

        amax, nmax, asum, rsum = (small[:, 12 * i:12 * i + 12].rearrange("p (a b) -> p a b", a=3) for i in range(4))
        acoef = small[:, 48:49]
        lam_s, lam_e, neg_lam = small[:, 49:51], small[:, 51:53], small[:, 53:54]
        g_lam = small[:, 54:58]
        rlam = small[:, 58:64].rearrange("p (a b) -> p a b", a=3)

        FFN_T, UP_T, DOWN_T = FFN_PAIRS // 2, UP_PAIRS // 2, DOWN_PAIRS // 2
        SEC1 = {"ffn1": 0, "in": FFN_T, "out": FFN_T + IN1 // 4, "ffn2": FFN_T + IN1 // 4 + OUTB // 4}
        SEC2 = {"ffn1": 0, "in": FFN_T, "out": FFN_T + IN2 // 4, "ffn2": FFN_T + IN2 // 4 + OUTB // 4}
        TURNS1, TURNS2 = LAYER1_PAIRS // 2, LAYER2_PAIRS // 2
        BLOCK2_TURN = DEPTH * TURNS1
        ALL_TURNS = BLOCK2_TURN + DEPTH * TURNS2
        NORM2 = 3 * DEPTH + 1
        EVENT2 = 4 * DEPTH + 1

        D_BANK, S_BANK, O_BANK = (2, 3, 6), (7, 6, 0), (4, 1)
        ident_bf, maskS_bf, maskA_bf = (masks[:, P * i:P * i + P] for i in range(3))

        block = ctx.enter_context(nc.Block())

        @block.sync
        def _(sp):
            def load_pair(j, src, width):
                sp.dma_start(raw[:, j, 0:2 * width], src).then_inc(raw_landed[j], 16)

            def section(turn0, n, src, width, next_src, next_width):
                with sp.Fori(0, n - 1) as it:
                    for j in range(2):
                        sp.wait_ge(lo_done, turn0 * 4 + it * 4 + (2 * j + 2))
                        load_pair(j, src(it * 2 + (2 + j)), width)
                for j in range(2):
                    sp.wait_ge(lo_done, turn0 * 4 + (4 * (n - 1) + 2 * j + 2))
                    load_pair(j, next_src(j), next_width)

            def ffn(q, turn0, next_src, next_width):
                section(turn0, UP_T, lambda i: w_up[q * NF + i], W_NARROW, lambda i: w_down[q * KD + i], W_WIDE)
                section(turn0 + UP_T, DOWN_T, lambda i: w_down[q * KD + i], W_WIDE, next_src, next_width)

            def layer(l, turn0, sec, q, w_in, n_in, w_out):
                def win(i):
                    return w_in[l * (n_in // 2) + i]

                def wout(i):
                    return w_out[l * (OUTB // 2) + i]

                ffn(q, turn0 + sec["ffn1"], win, W_NARROW)
                section(turn0 + sec["in"], n_in // 4, win, W_NARROW, wout, W_NARROW)
                section(turn0 + sec["out"], OUTB // 4, wout, W_NARROW, lambda i: w_up[(q + 1) * NF + i], W_NARROW)
                ffn(q + 1, turn0 + sec["ffn2"], lambda i: w_up[(q + 2) * NF + i], W_NARROW)

            sp.dma_start(h[:], hidden0).then_inc(h_in, 16)
            for j in range(2):
                load_pair(j, w_up[j], W_NARROW)
            sp.dma_start(cst[:, 0:CC_FIRST], consts[:, 0:CC_FIRST]).then_inc(consts_in, 16)
            with sp.Fori(0, DEPTH) as l:
                sp.wait_ge(prm_free, l * 1 + START)
                sp.dma_start(prm[:, 0:P1_W], prm1[l]).then_inc(prm_in, 16)
                layer(l, l * TURNS1, SEC1, l * 2, w_in1, IN1, w_out1)
            sp.dma_start(cst[:, CC_FIRST:], consts[:, CC_FIRST:]).then_inc(consts_in, 16)
            with sp.Fori(0, DEPTH) as l:
                sp.wait_ge(prm_free, l * 1 + (DEPTH + START))
                sp.dma_start(prm[:, 0:P2_W], prm2[l]).then_inc(prm_in, 16)
                layer(l, l * TURNS2 + BLOCK2_TURN, SEC2, l * 2 + 2 * DEPTH, w_in2, IN2, w_out2)
            for j in range(2):
                sp.wait_ge(raw_landed[j], 16 * (ALL_TURNS + 1))
            sp.wait_ge(xn_ready, KD * (NORM2 + 3 * DEPTH))
            sp.dma_start(out, pj[:, 0:KD, 0:T2]).then_inc(stored, 16)
            sp.wait_ge(stored, 16)

        @block.tensor
        def _(pe):
            mm = nc.tensor.matmul
            tr = nc.tensor.transpose

            def three(dst, j, cols, xa, xb, first, last):
                mm(dst, w_lo[:, j, cols], xa, start=first, stop=False)
                mm(dst, w_hi[:, j, cols], xb, start=False, stop=False)
                return mm(dst, w_hi[:, j, cols], xa, start=False, stop=last)

            def narrow_unit(turn, j, u, dst, T):
                pe.wait_ge(lo_done, turn * 4 + (2 * j + u + 1))
                for k in range(KD):
                    c = u * W_NARROW + k * P
                    last = three(dst, j, slice(c, c + P), x_hi[:, k, 0:T], x_lo[:, k, 0:T], k == 0, k == KD - 1)
                last.then_inc(unit_used, 1)

            def first_pair(turn, event, bank, T):
                pe.wait_ge(lo_done, turn * 4 + 2)
                for k in range(KD):
                    pe.wait_ge(x_ready, event * KD + (k + 1))
                    for u in range(2):
                        c = u * W_NARROW + k * P
                        last = three(ps[:, bank + u, 0:T], 0, slice(c, c + P), x_hi[:, k, 0:T], x_lo[:, k, 0:T],
                                     k == 0, k == KD - 1)
                        if k == KD - 1:
                            last.then_inc(unit_used, 1)

            def up(q, turn0, event, T):
                pe.wait_ge(up_free, q * NF + (CREDIT - 1))
                first_pair(turn0, event, 0, T)
                pe.wait_ge(up_free, q * NF + CREDIT)
                for u in range(2):
                    narrow_unit(turn0, 1, u, ps[:, 2 + u, 0:T], T)
                with pe.Fori(1, UP_T) as it:
                    for j in range(2):
                        pe.wait_ge(up_free, q * NF + it * 2 + (j - 1 + CREDIT))
                        for u in range(2):
                            narrow_unit(turn0 + it, j, u, ps[:, 2 * j + u, 0:T], T)

            def one_chunk(buf, m, cols):
                if isinstance(m, int):
                    return buf[:, m, cols]
                return buf[:, bass.ds(m, 1), cols].rearrange("p a t -> p (a t)")

            def stats(rms, norm, T, m, first, last):
                if rms:
                    pe.wait_ge(rms_sq, norm * KD + (m + 1))
                    return mm(ps[:, 7, 0:T], con("onesD"), one_chunk(pj, m + KD, slice(0, T)), start=first, stop=last)
                pe.wait_ge(resid_ready, norm * KD + (m + 1 + CREDIT))
                return mm(ps[:, 6, 0:T], con("onesD"), one_chunk(h, m, slice(T1 - T, T1)), start=first, stop=last)

            def end_stats(rms, norm, T, m):
                last = stats(rms, norm, T, m, m == 0, True)
                if rms:
                    last.then_inc(var_ready, 1)
                    return
                last.then_inc(mean_ready, 1)
                for k in range(KD):
                    if k % 2 == 0:
                        pe.wait_ge(ln_sq, norm * 4 + (k // 2 + 1))
                    last = mm(ps[:, 7, 0:T], con("onesD"), pj[:, KD + k, 0:T], start=k == 0, stop=k == KD - 1)
                last.then_inc(var_ready, 1)

            def down(q, turn0, resid, rms, norm, T):
                def turn(it):
                    for j in range(2):
                        pe.wait_ge(resid_ready, resid * KD + it * 2 + (j - 1 + CREDIT))
                        for u in range(2):
                            if isinstance(it, int) and j == 0:
                                pe.wait_ge(hid_ready, q * NF + (u + 1) * HALF_F)
                            pe.wait_ge(lo_done, turn0 * 4 + it * 4 + (2 * j + u + 1))
                            for c in range(HALF_F):
                                f = u * HALF_F + c
                                col = u * W_WIDE + c * P
                                last = three(ps[:, 4 + j, 0:T], j, slice(col, col + P),
                                             hid_hi[:, f, 0:T], hid_lo[:, f, 0:T], f == 0, f == NF - 1)
                            last.then_inc(unit_used, 1)
                        if not (isinstance(it, int) and j == 0):
                            stats(rms, norm, T, it * 2 + (j - 1), isinstance(it, int), False)

                turn(0)
                with pe.Fori(1, DOWN_T) as it:
                    turn(it)
                end_stats(rms, norm, T, KD - 1)

            def out_proj(turn0, event, resid, rms, norm, T):
                pe.wait_ge(resid_ready, resid * KD + CREDIT)
                first_pair(turn0, event, 4, T)
                for m in range(1, KD):
                    if m >= 2:
                        pe.wait_ge(resid_ready, resid * KD + (m - 1 + CREDIT))
                        narrow_unit(turn0 + m // 4, (m // 2) % 2, m % 2, ps[:, 4 + m % 2, 0:T], T)
                    stats(rms, norm, T, m - 1, m == 1, False)
                end_stats(rms, norm, T, KD - 1)

            def in_proj(l, turn0, event, n, ready, T):
                first_pair(turn0, event, 0, T)
                for u in range(2):
                    narrow_unit(turn0, 1, u, ps[:, 2 + u, 0:T], T)
                with pe.Fori(1, n // 4) as it:
                    pe.wait_ge(ready.sem, ready.at(l, 0) + it * 4)
                    for i in range(4):
                        narrow_unit(turn0 + it, i // 2, i % 2, ps[:, i, 0:T], T)

            def tri_bank(bank, i):
                n, w = TILES[i][1], TRI_W[i]
                return ps[0:n, bank, TRI[i]:TRI[i] + w]

            def mixer1(l, turn0, event):
                def block(i):
                    if i >= 4:
                        pe.wait_ge(proj_ready.sem, proj_ready.at(l, i - 3))
                    narrow_unit(turn0 + i // 4, (i // 2) % 2, i % 2, ps[:, i % 4, 0:T1], T1)

                first_pair(turn0, event, 0, T1)
                for i in range(2, 6):
                    block(i)
                pe.wait_ge(mla_sq.sem, mla_sq.at(l, 1))
                mm(ps[:, 6, 0:T1], con("ones256"), lat_sq[:, 1, :], start=True, stop=False)
                mm(ps[:, 6, 0:T1], con("ones256"), lat_sq[:, 2, :], start=False, stop=True)
                mm(ps[:, 7, 0:T1], con("ones128"), lat_sq[:, 0, :], start=True, stop=True).then_inc(mla_ss.sem, 1)
                krope = pj[0:ROPE, MISC, :]
                mm(ps[:, 4, 0:T1], con("rep", rows=slice(0, ROPE)), krope, start=True, stop=True)
                mm(ps[:, 5, 0:T1], con("reprot", rows=slice(0, ROPE)), krope, start=True, stop=True)\
                    .then_inc(kr_raw.sem, 1)
                for i in range(6, 10):
                    block(i)
                pe.wait_ge(cqn_ready.sem, cqn_ready.at(l, 1))
                pe.wait_ge(kr_ready.sem, kr_ready.at(l, 1))
                for b, bank in enumerate((6, 7, 4)):
                    for k in range(2):
                        c = P1["uq"] + 384 * k + P * b
                        last = mm(ps[:, bank, 0:T1], prm[:, c:c + P], cqn[:, k, :], start=k == 0, stop=k == 1)
                last.then_inc(uq_done.sem, 1)
                for i in range(10, 12):
                    block(i)
                pe.wait_ge(qn_ready.sem, qn_ready.at(l, 1))
                for b in range(2):
                    c = P1["ukv"] + P * b
                    mm(ps[:, 6 + b, 0:T1], prm[:, c:c + P], cqn[:, 2, :], start=True, stop=True)
                for i, (t, n) in enumerate(TILES):
                    c = P1["ukv"] + 2 * P
                    dst = ps[0:n, 5, 256 * i:256 * i + 256] if i < 2 else ps[0:n, 4, 0:256]
                    last = mm(dst, cqn[:, 2, t:t + n], prm[:, c:c + 256], start=True, stop=True)
                last.then_inc(ukv_done.sem, 1)
                for i in range(12, 14):
                    block(i)
                pe.wait_ge(kv_ready.sem, kv_ready.at(l, 1))
                pe.wait_ge(rows_ready.sem, rows_ready.at(l, 1))
                mm(ps[:, 6, 0:T1], con("rot"), qraw, start=True, stop=True).then_inc(qrot_done.sem, 1)
                for i, (t, n) in enumerate(TILES):
                    for r, src in enumerate((row_cum, row_sp)):
                        c = (2 * i + r) * 64
                        last = tr(ps[0:n, 7, c:c + 64], src[ROWS, t:t + n], ident[ROWS, ROWS])
                last.then_inc(rows_t.sem, 1)
                for i in range(14, 17):
                    block(i)
                pe.wait_ge(xc_ready.sem, xc_ready.at(l, 1))
                pe.wait_ge(qr_ready.sem, qr_ready.at(l, 1))
                for i, (t, n) in enumerate(TILES):
                    for c in range(4):
                        last = tr(ps[0:n, 4 + i, P * c:P * c + P], xc[:, c, t:t + n], ident)
                last.then_inc(xs_t.sem, 1)
                for i in range(17, 20):
                    block(i)
                pe.wait_ge(proj_ready.sem, proj_ready.at(l, IN1))
                for g in range(2):
                    gr = slice(64 * g, 64 * g + 64)
                    for i, (t, n) in enumerate(TILES):
                        last = mm(tri_bank(g, i), xc[gr, 4, t:t + n], xc[gr, 5, t:T1], start=True, stop=True)
                    last.then_inc(g_ready.sem, 1)
                pe.wait_ge(tok_ready.sem, tok_ready.at(l, 1))
                for i, (t, n) in enumerate(TILES):
                    for c in range(2):
                        bank, col = (7, 256 * i + P * c) if i < 2 else (6, P * c)
                        last = tr(ps[0:n, bank, col:col + P], pj[:, FV0 + c, t:t + n], ident)
                last.then_inc(vf_t.sem, 1)

                def ssd_d(hh):
                    if hh == 2:
                        pe.wait_ge(vf_ready.sem, vf_ready.at(l, 1))
                    if hh >= 3:
                        pe.wait_ge(decay.sem, decay.at(l, hh - 2))
                    bank = D_BANK[hh % 3]
                    for i, (t, n) in enumerate(TILES):
                        mm(tri_bank(bank, i), con("sel", 12 * P)[:, hh * P:hh * P + n], row_cum[:, t:T1],
                           start=True, stop=False)
                        last = mm(ps[0:n, bank, TRI[i]:TRI[i] + n], ident_bf[:, 0:n], maskS_bf[:, 0:n],
                                  start=False, stop=True)
                    last.then_inc(d_ready.sem, 1)

                def ssd_y(hh):
                    pe.wait_ge(ssd_w.sem, ssd_w.at(l, hh + 1))
                    if hh % 2 == 0 and hh >= 4:
                        pe.wait_ge(yz_ready.sem, yz_ready.at(l, hh // 2 - 1))
                    for i, (t, n) in enumerate(TILES):
                        last = mm(ps[head_rows(hh), 4 + (hh // 2) % 2, t:T1], xtok[0:n, i, HD * hh:HD * hh + HD],
                                  ptr[0:n, hh % 2, TRI[i]:TRI[i] + TRI_W[i]], start=i == 0, stop=i == 2)
                    last.then_inc(y_ready.sem, 1)

                def att_s(n_):
                    if n_ == 1:
                        pe.wait_ge(decay.sem, decay.at(l, 6))
                    if n_ == 2:
                        pe.wait_ge(ssd_w.sem, ssd_w.at(l, 4))
                    if n_ >= 3:
                        pe.wait_ge(exp_done.sem, exp_done.at(l, n_ - 2))
                    bank = S_BANK[n_ % 3]
                    hr = head_rows(n_)
                    for i in (2, 1, 0):
                        t, n = QTILES[i]
                        c, kw = S_COL[i], KEYS[i]
                        dst = ps[0:n, bank, c:c + kw]
                        if n_ < MLA_HEADS:
                            rr = slice(ROPE * n_, ROPE * n_ + ROPE)
                            mm(dst, qn[hr, n_ // 2, t:t + n], kn[hr, n_ // 2, 0:kw], start=True, stop=False)
                            mm(dst, qr[rr, t:t + n], kr[rr, 0:kw], start=False, stop=False)
                        else:
                            hd = n_ - MLA_HEADS
                            mm(dst, pj[hr, FQ0 + hd // 2, t:t + n], pj[hr, FK0 + hd // 2, 0:kw], start=True, stop=False)
                            mm(dst, con("sel", 12 * P)[:, (8 + hd) * P:(8 + hd) * P + n], row_cum[:, 0:kw],
                               start=False, stop=False)
                        last = mm(ps[0:n, bank, c + t:c + kw], ident_bf[:, 0:n], maskA_bf[:, 0:n],
                                  start=False, stop=True)
                    last.then_inc(s_ready.sem, 1)

                def att_t(n_):
                    pe.wait_ge(p_ready.sem, p_ready.at(l, n_ + 1))
                    if n_ >= 2:
                        pe.wait_ge(pt_ready.sem, pt_ready.at(l, n_ - 1))
                    bank, p = 2 + n_ % 2, prob[:, n_ % 3, :]
                    ends = slice(64, P)
                    c1, c2 = S_COL[1], S_COL[2]
                    tr(ps[:, bank, 0:P], p[:, c1:c1 + P], ident)
                    tr(ps[:, bank, P:2 * P], p[:, c2:c2 + P], ident)
                    tr(ps[:, bank, PT_K1:PT_K1 + P], p[:, c2 + P:c2 + 2 * P], ident)
                    tr(ps[0:N_META, bank, PT_META:PT_END1], p[0:N_META, 0:N_META], ident[0:N_META, 0:N_META])
                    tr(ps[0:N_META, bank, PT_END2:PT_W], p[ends, c2 + 2 * P:S_W], ident[ends, ends])
                    tr(ps[0:N_META, bank, PT_END1:PT_END1 + 64], p[ends, c1 + P:c2], ident[ends, ends])\
                        .then_inc(t_ready.sem, 1)

                def att_o(n_):
                    pe.wait_ge(pt_ready.sem, pt_ready.at(l, n_ + 1))
                    pair = n_ // 2
                    if n_ == 0:
                        pe.wait_ge(ystd_ready.sem, ystd_ready.at(l, 1))
                    if n_ % 2 == 0 and pair >= 2:
                        pe.wait_ge(x_ready, (event + 1) * KD + (4 + pair - 1))
                    v = vmla if n_ < MLA_HEADS else vfox
                    hd = slice(HD * (n_ % MLA_HEADS), HD * (n_ % MLA_HEADS) + HD)
                    o, p = ps[head_rows(n_), O_BANK[pair % 2], :], ptr[:, n_ % 2, :]
                    t1, t2 = QTILES[1][0], QTILES[2][0]
                    mm(o[:, 0:N_META], v[0:N_META, 0, hd], p[0:N_META, PT_META:PT_END1], start=True, stop=True)
                    mm(o[:, t1:T1], v[:, 0, hd], p[:, 0:2 * P], start=True, stop=False)
                    mm(o[:, t2:T1], v[:, 1, hd], p[:, PT_K1:PT_K1 + P], start=False, stop=False)
                    mm(o[:, t2 - N_META:t2], v[0:N_META, 1, hd], p[0:N_META, PT_END1 + 48:PT_END1 + 64],
                       start=False, stop=False)
                    mm(o[:, T1 - N_META:T1], v[0:N_META, 2, hd], p[0:N_META, PT_W - N_META:PT_W],
                       start=False, stop=True).then_inc(o_ready.sem, 1)

                pe.wait_ge(masks_ready, 1)
                for hh in range(3):
                    ssd_d(hh)
                for hh in range(SSD_HEADS):
                    ssd_y(hh)
                    if hh + 3 < SSD_HEADS:
                        ssd_d(hh + 3)
                    elif hh < SSD_HEADS - 1:
                        att_s(hh + 3 - SSD_HEADS)
                att_s(2)
                pe.wait_ge(sqy_ready.sem, sqy_ready.at(l, 1))
                for g in range(2):
                    for c in range(2):
                        last = mm(ps[:, 4 + g, 0:T1], con("ones256"), ssd_sq[g][:, c, :], start=c == 0, stop=c == 1)
                last.then_inc(yss_ready.sem, 1)
                for n_ in range(NH):
                    att_t(n_)
                    if n_ + 3 < NH:
                        att_s(n_ + 3)
                    att_o(n_)
                pe.wait_ge(x_ready, (event + 1) * KD + (KD - 1))

            def mixer2(l):
                pe.wait_ge(proj2_ready.sem, proj2_ready.at(l, IN2))
                for i in range(2):
                    for c in range(4):
                        last = tr(ps[:, i, P * c:P * c + P], pj[:, c, P * i:P * i + P], ident)
                last.then_inc(af_t.sem, 1)
                for i in range(2):
                    for c in range(4):
                        last = tr(ps[:, 2 + i, P * c:P * c + P], pj[:, 12 + c, P * i:P * i + P], ident)
                last.then_inc(v_t.sem, 1)
                pe.wait_ge(af_ready.sem, af_ready.at(l, 1))
                for g in range(4):
                    for i in range(2):
                        c = CC["band"] + (2 * g + i) * T2
                        last = mm(ps[head_rows(g), 4, 256 * (g // 2):256 * (g // 2) + T2],
                                  aftok[:, i, 64 * g:64 * g + 64], cst[:, c:c + T2], start=i == 0, stop=i == 1)
                last.then_inc(pm_done.sem, 1)
                for r, name in enumerate(("cs", "ss")):
                    if r == 1:
                        pe.wait_ge(pm_ready.sem, pm_ready.at(l, 1))
                    for b in range(2):
                        for i in range(2):
                            c = CC[name] + i * T2
                            last = mm(ps[:, 6 + r, 256 * b:256 * b + T2], aftok[:, i, 256 + P * b:256 + P * b + P],
                                      cst[:, c:c + T2], start=i == 0, stop=i == 1)
                last.then_inc(uv_done.sem, 1)
                for g in range(4):
                    c = P2["poolw"] + 64 * (g // 2)
                    last = mm(ps[head_rows(g), 5, 256 * (g // 2):256 * (g // 2) + T2], prm[head_rows(g), c:c + 64],
                              poolm[head_rows(g), g // 2, :], start=True, stop=True)
                last.then_inc(py_done.sem, 1)
                pe.wait_ge(uv_ready.sem, uv_ready.at(l, 1))
                for b in range(2):
                    dst = ps[:, 6, 256 * b:256 * b + T2]
                    mm(dst, con("ccos"), uu[:, b, :], start=True, stop=False)
                    last = mm(dst, con("csin"), vv[:, b, :], start=False, stop=True)
                last.then_inc(f2_done.sem, 1)
                pe.wait_ge(f2_ready.sem, f2_ready.at(l, 1))
                for b in range(2):
                    for k in range(2):
                        c = P2["fourw"] + 256 * k + P * b
                        last = mm(ps[:, 7, 256 * b:256 * b + T2], prm[:, c:c + P], y4[:, k, :], start=k == 0, stop=k == 1)
                last.then_inc(f3_done.sem, 1)

                def att_s(hh):
                    if hh == 0:
                        pe.wait_ge(v_ready.sem, v_ready.at(l, 1))
                    if hh >= 2:
                        pe.wait_ge(exp2_done.sem, exp2_done.at(l, hh - 1))
                    for i in range(2):
                        for j in range(2):
                            dst = ps[:, 2 * (hh % 2) + j, 256 * i:256 * i + T2]
                            mm(dst, pj[head_rows(j), 4 + hh, P * i:P * i + P], pj[head_rows(j), 8 + hh, 0:T2],
                               start=True, stop=False)
                            c = CC["absd"] + i * T2
                            s = CC["slope"] + hh * P
                            last = mm(dst, cst[:, s:s + P], cst[:, c:c + T2], start=False, stop=True)
                    last.then_inc(s2_ready.sem, 1)

                def att_t(hh):
                    pe.wait_ge(a2_ready.sem, a2_ready.at(l, hh + 1))
                    if hh == 0:
                        pe.wait_ge(pool_cat.sem, pool_cat.at(l, 1))
                    if hh >= 2:
                        pe.wait_ge(at2_ready.sem, at2_ready.at(l, hh - 1))
                    for i in range(2):
                        for k in range(2):
                            c = 256 * k + P * i
                            last = tr(ps[:, 4 + hh % 2, c:c + P], attn[:, hh % 2, i, P * k:P * k + P], ident)
                    last.then_inc(t2_ready.sem, 1)

                def att_o(hh):
                    pe.wait_ge(at2_ready.sem, at2_ready.at(l, hh + 1))
                    dst = ps[:, 6 + hh // 2, 256 * (hh % 2):256 * (hh % 2) + T2]
                    for k in range(2):
                        last = mm(dst, vtok[:, k, P * hh:P * hh + P], attn_t[:, hh % 2, k, :], start=k == 0, stop=k == 1)
                    last.then_inc(o2_ready.sem, 1)

                att_s(0)
                for hh in range(ATT_HEADS):
                    if hh + 1 < ATT_HEADS:
                        att_s(hh + 1)
                    att_t(hh)
                    if hh >= 1:
                        att_o(hh - 1)
                att_o(ATT_HEADS - 1)
                pe.wait_ge(o2_sq.sem, o2_sq.at(l, 1))
                for hh in range(ATT_HEADS):
                    last = mm(ps[:, hh // 2, 256 * (hh % 2):256 * (hh % 2) + T2], con("ones128"), sqo[:, hh, :],
                              start=True, stop=True)
                last.then_inc(o2_ss.sem, 1)

            pe.nop().then_inc(unit_used, START)
            with pe.Fori(0, DEPTH) as l:
                t0, q, e0, r0 = l * TURNS1, l * 2, l * 4, l * 3
                up(q, t0 + SEC1["ffn1"], e0, T1)
                pe.wait_ge(consts_in, 16)
                down(q, t0 + SEC1["ffn1"] + UP_T, r0, False, r0, T1)
                pe.wait_ge(prm_in, l * 16 + 16)
                mixer1(l, t0 + SEC1["in"], e0 + 1)
                out_proj(t0 + SEC1["out"], e0 + 2, r0 + 1, False, r0 + 1, T1)
                up(q + 1, t0 + SEC1["ffn2"], e0 + 3, T1)
                down(q + 1, t0 + SEC1["ffn2"] + UP_T, r0 + 2, False, r0 + 2, T1)
            for k in range(KD - 1):
                stats(True, 0, T2, k, k == 0, False)
            end_stats(True, 0, T2, KD - 1)
            with pe.Fori(0, DEPTH) as l:
                t0, q, e0, r0 = l * TURNS2 + BLOCK2_TURN, l * 2 + 2 * DEPTH, l * 4 + EVENT2, l * 3 + 3 * DEPTH
                up(q, t0 + SEC2["ffn1"], e0, T2)
                down(q, t0 + SEC2["ffn1"] + UP_T, r0, True, l * 3 + 1, T2)
                in_proj(l, t0 + SEC2["in"], e0 + 1, IN2, proj2_ready, T2)
                pe.wait_ge(prm_in, l * 16 + (16 * DEPTH + 16))
                pe.wait_ge(consts_in, 32)
                mixer2(l)
                out_proj(t0 + SEC2["out"], e0 + 2, r0 + 1, True, l * 3 + 2, T2)
                up(q + 1, t0 + SEC2["ffn2"], e0 + 3, T2)
                down(q + 1, t0 + SEC2["ffn2"] + UP_T, r0 + 2, True, l * 3 + 3, T2)

        @block.scalar
        def _(act):
            fn = nc.scalar.activation

            def hi_unit(j, u, width):
                c = slice(u * width, (u + 1) * width)
                fn(w_hi[:, j, c], raw[:, j, c], ACT.Copy).then_inc(hi_done, 1)

            def split_hi(turn, j, width, wait_slot=True):
                act.wait_ge(raw_landed[j], turn * 16 + 16)
                if wait_slot:
                    act.wait_ge(unit_used, turn * 4 + (2 * j - 2 + START))
                for u in range(2):
                    hi_unit(j, u, width)

            def second_pair(turn, u):
                act.wait_ge(raw_landed[1], turn * 16 + 16)
                act.wait_ge(unit_used, turn * 4 + (u - 1 + START))
                hi_unit(1, u, W_NARROW)

            def load_sqrt():
                fn(small[:, 95:96], con("one", 1), ACT.Sqrt)

            def split_next(turn, j, width):
                split_hi(turn + j, 1 - j, width)

            def up(q, turn0, T):
                def turn(it, next_width):
                    for j in range(2):
                        if not (isinstance(it, int) and it == 0 and j == 0):
                            split_next(turn0 + it, j, W_NARROW if j == 0 else next_width)
                        act.wait_ge(unit_used, turn0 * 4 + it * 4 + (2 * j + 1 + START))
                        act.wait_ge(up_free, q * NF + it * 2 + (j - 1 + CREDIT))
                        fn(silu[:, j, 0:T], ps[:, 2 * j, 0:T], ACT.Silu).then_inc(silu_done, 1)

                turn(0, W_NARROW)
                with act.Fori(1, UP_T - 1) as it:
                    turn(it, W_NARROW)
                turn(UP_T - 1, W_WIDE)

            def square(norm, resid, m, T):
                act.wait_ge(resid_ready, resid * KD + (m + 1 + CREDIT))
                if isinstance(m, int):
                    dst, src = pj[:, KD + m, 0:T], h[:, m, T1 - T:T1]
                else:
                    dst, src = pj[:, bass.ds(m + KD, 1), 0:T], h[:, bass.ds(m, 1), T1 - T:T1]
                fn(dst, src, ACT.Square).then_inc(rms_sq, 1)

            def down(turn0, resid, rms, norm, T):
                def turn(it, next_width):
                    for j in range(2):
                        split_next(turn0 + it, j, W_WIDE if j == 0 else next_width)
                        if next_width == W_NARROW and j == 1:
                            second_pair(turn0 + DOWN_T, 0)
                            load_sqrt()
                        if rms:
                            square(norm, resid, it * 2 + j, T)

                with act.Fori(0, DOWN_T - 1) as it:
                    turn(it, W_WIDE)
                turn(DOWN_T - 1, W_NARROW)

            def out_proj(turn0, resid, rms, norm, T):
                for p in range(OUTB // 2):
                    split_next(turn0 + p // 2, p % 2, W_NARROW)
                    if p == OUTB // 2 - 1:
                        second_pair(turn0 + OUTB // 4, 0)
                        load_sqrt()
                    if rms:
                        for u in range(2):
                            square(norm, resid, 2 * p + u, T)

            def in_proj(turn0, n, ready, T):
                def turn(it):
                    for j in range(2):
                        first = isinstance(it, int)
                        if not (first and j == 0):
                            split_next(turn0 + it, j, W_NARROW)
                        for u in range(2):
                            act.wait_ge(unit_used, turn0 * 4 + it * 4 + (2 * j + u + 1 + START))
                            b = it * 4 + (2 * j + u)
                            dst = pj[:, slice(b, b + 1) if first else bass.ds(b, 1), 0:T]
                            fn(dst, ps[:, 2 * j + u:2 * j + u + 1, 0:T], ACT.Copy).then_inc(ready.sem, 1)

                turn(0)
                with act.Fori(1, n // 4) as it:
                    turn(it)

            def layer_norm(norm, bias, next_turn):
                for s in range(4):
                    act.wait_ge(centered, norm * 4 + (s + 1))
                    fn(pj[:, KD + 2 * s:KD + 2 * s + 2, :], h[:, 2 * s:2 * s + 2, :], ACT.Square).then_inc(ln_sq, 1)
                act.wait_ge(var_ready, norm + 1)
                fn(std[:, 0, :], ps[:, 7, 0:T1], ACT.Sqrt, bias=con("eps1", 1)).then_inc(std_ready, 1)
                for k in range(KD):
                    act.wait_ge(xn_ready, norm * KD + (k + 1))
                    fn(x_hi[:, k, :], pj[:, k, :], ACT.Identity, bias=par(P1, bias, k)).then_inc(xh_ready, 1)
                if next_turn is not None:
                    second_pair(next_turn, 1)

            def rms_norm(number, next_turn):
                act.wait_ge(var_ready, number + 1)
                fn(std[:, 0, 0:T2], ps[:, 7, 0:T2], ACT.Sqrt, bias=con("eps2", 1)).then_inc(std_ready, 1)
                for k in range(KD):
                    act.wait_ge(xn_ready, number * KD + (k + 1))
                    fn(x_hi[:, k, 0:T2], pj[:, k, 0:T2], ACT.Copy).then_inc(xh_ready, 1)
                if next_turn is not None:
                    second_pair(next_turn, 1)

            def mixer1(l, turn0):
                def pair(p, *between):
                    if p > 0:
                        split_hi(turn0 + (p + 1) // 2, (p + 1) % 2, W_NARROW)
                    for i in (2 * p, 2 * p + 1):
                        act.wait_ge(unit_used, turn0 * 4 + (i + 1 + START))
                        fn(pj[:, i, :], ps[:, i % 4, 0:T1], ACT.Copy).then_inc(proj_ready.sem, 1)
                        if i % 2 == 0:
                            for step in between:
                                step()

                def rows():
                    act.wait_ge(rows_u.sem, rows_u.at(l, 1))
                    fn(row_l[ROWS, :], row_u[ROWS, :], ACT.Abs)
                    act.drain()
                    fn(row_l[ROWS, :], row_l[ROWS, :], ACT.Exp, scale=-1.0)
                    fn(acoef[ROWS, :], par(P1, "alog", rows=ROWS), ACT.Exp)
                    act.drain()
                    fn(row_l[ROWS, :], row_l[ROWS, :], ACT.Ln, bias=con("one", 1, ROWS)).then_inc(rows_ln.sem, 1)

                def latent_squares():
                    act.drain()
                    fn(lat_sq, pj[:, CKV:CKV + 3, :], ACT.Square).then_inc(mla_sq.sem, 1)

                def latent_roots():
                    act.wait_ge(mla_ss.sem, mla_ss.at(l, 1))
                    fn(std[:, :, :], ps[:, 6:8, 0:T1], ACT.Sqrt, bias=con("eps1", 1)).then_inc(mla_std.sem, 1)

                def seeds(c0):
                    act.drain()
                    for c in (c0, c0 + 1):
                        fn(xc[:, c, :], pj[:, XBC0 + c, :], ACT.Identity, bias=par(P1, "convb", c),
                           scale=par(P1, "convw", CONV * c + CONV - 1)).then_inc(conv_seed.sem, 1)

                def queries():
                    act.wait_ge(uq_done.sem, uq_done.at(l, 1))
                    fn(qn, ps[:, 6:8, 0:T1], ACT.Copy)
                    fn(qraw, ps[:, 4, 0:T1], ACT.Copy).then_inc(qn_ready.sem, 1)

                def silus():
                    act.drain()
                    act.wait_ge(conv_done.sem, conv_done.at(l, 1))
                    fn(xc, xc, ACT.Silu)
                    fn(pj[:, Z0:Z0 + 4, :], pj[:, Z0:Z0 + 4, :], ACT.Silu).then_inc(xc_ready.sem, 1)

                pair(0)
                pair(1, rows)
                pair(2, latent_squares)
                pair(3, latent_roots, lambda: seeds(0))
                pair(4, lambda: seeds(2))
                pair(5, queries, lambda: seeds(4))
                pair(6)
                pair(7, silus)
                pair(8)
                pair(9)

                act.wait_ge(tokrow_ready.sem, tokrow_ready.at(l, 1))
                for hh in range(SSD_HEADS):
                    act.wait_ge(d_ready.sem, d_ready.at(l, hh + 1))
                    if hh >= 3:
                        act.wait_ge(ssd_w.sem, ssd_w.at(l, hh - 2))
                    for i, (t, n) in enumerate(TILES):
                        c = slice(TRI[i], TRI[i] + TRI_W[i])
                        last = fn(prob[0:n, hh % 3, c], ps[0:n, D_BANK[hh % 3], c], ACT.Exp,
                                  bias=tok_ncum[0:n, i, hh:hh + 1])
                    last.then_inc(decay.sem, 1)
                act.wait_ge(yz_ready.sem, yz_ready.at(l, 4))
                for g in range(2):
                    last = fn(ssd_sq[g][:], xc[:, 2 * g:2 * g + 2, :], ACT.Square)
                last.then_inc(sqy_ready.sem, 1)

                def exps(n_):
                    act.wait_ge(nm_ready.sem, nm_ready.at(l, n_ + 1))
                    if n_ >= 3:
                        act.wait_ge(t_ready.sem, t_ready.at(l, n_ - 2))
                    s = n_ % 3
                    for i, (t, n) in enumerate(QTILES):
                        c = slice(S_COL[i], S_COL[i] + KEYS[i])
                        last = fn(prob[0:n, s, c], ps[0:n, S_BANK[s], c], ACT.Exp,
                                  bias=nmax[0:n, s, i:i + 1], scale=MLA_SCALE if n_ < MLA_HEADS else FOX_SCALE,
                                  accum_out=asum[0:n, s, i:i + 1])
                    last.then_inc(exp_done.sem, 1)

                def pt_copy(n_):
                    act.wait_ge(t_ready.sem, t_ready.at(l, n_ + 1))
                    if n_ >= 2:
                        act.wait_ge(o_ready.sem, o_ready.at(l, n_ - 1))
                    fn(ptr[:, n_ % 2, 0:PT_META], ps[:, 2 + n_ % 2, 0:PT_META], ACT.Copy)
                    fn(ptr[0:N_META, n_ % 2, PT_META:PT_W], ps[0:N_META, 2 + n_ % 2, PT_META:PT_W], ACT.Copy)\
                        .then_inc(pt_ready.sem, 1)

                def o_high(pair):
                    act.wait_ge(o_ready.sem, o_ready.at(l, 2 * pair + 2))
                    fn(x_hi[:, 4 + pair, :], ps[:, O_BANK[pair % 2], 0:T1], ACT.Copy).then_inc(cat_hi.sem, 1)

                exps(0)
                exps(1)
                act.wait_ge(yss_ready.sem, yss_ready.at(l, 1))
                fn(std[:, :, :], ps[:, 4:6, 0:T1], ACT.Sqrt, bias=con("eps1", 1)).then_inc(ystd_ready.sem, 1)
                for n_ in range(NH):
                    pt_copy(n_)
                    if n_ + 2 < NH:
                        exps(n_ + 2)
                    if n_ == 1:
                        act.wait_ge(ssd_cat.sem, ssd_cat.at(l, 1))
                        for k in range(4):
                            fn(x_hi[:, k, :], pj[:, k, :], ACT.Copy).then_inc(cat_hi.sem, 1)
                    if n_ % 2 == 0 and n_ >= 2:
                        o_high(n_ // 2 - 1)
                o_high(NH // 2 - 1)

            def mixer2(l):
                act.wait_ge(af_t.sem, af_t.at(l, 1))
                fn(aftok, ps[:, 0:2, :], ACT.Copy).then_inc(af_ready.sem, 1)
                act.wait_ge(lam_dot.sem, lam_dot.at(l, 1))
                fn(lam_e, lam_s, ACT.Exp).then_inc(lam_exp.sem, 1)
                act.wait_ge(uv_done.sem, uv_done.at(l, 1))
                fn(uu, ps[:, 6, :].rearrange("p (a t) -> p a t", a=2), ACT.Copy)
                fn(vv, ps[:, 7, :].rearrange("p (a t) -> p a t", a=2), ACT.Copy).then_inc(uv_ready.sem, 1)
                act.wait_ge(f2_done.sem, f2_done.at(l, 1))
                fn(y4, ps[:, 6, :].rearrange("p (a t) -> p a t", a=2), ACT.Copy).then_inc(f2_ready.sem, 1)
                act.wait_ge(f3_done.sem, f3_done.at(l, 1))
                fn(pj[:, 2:4, 0:T2], ps[:, 7, :].rearrange("p (a t) -> p a t", a=2), ACT.Copy)

                def exps(hh):
                    act.wait_ge(nm2_ready.sem, nm2_ready.at(l, hh + 1))
                    if hh >= 2:
                        act.wait_ge(a2_ready.sem, a2_ready.at(l, hh - 1))
                    s = hh % 2
                    for j in range(2):
                        for i in range(2):
                            c = 2 * j + i
                            last = fn(prob2[:, s, c, :], ps[:, 2 * s + j, 256 * i:256 * i + T2], ACT.Exp,
                                      bias=nmax[:, s, c:c + 1], scale=ATT_SCALE, accum_out=asum[:, s, c:c + 1])
                    last.then_inc(exp2_done.sem, 1)

                def at_copy(hh):
                    act.wait_ge(t2_ready.sem, t2_ready.at(l, hh + 1))
                    if hh >= 2:
                        act.wait_ge(o2_ready.sem, o2_ready.at(l, hh - 1))
                    fn(attn_t[:, hh % 2, :, :], ps[:, 4 + hh % 2, :].rearrange("p (a t) -> p a t", a=2), ACT.Copy)\
                        .then_inc(at2_ready.sem, 1)

                exps(0)
                for hh in range(ATT_HEADS):
                    if hh + 1 < ATT_HEADS:
                        exps(hh + 1)
                    at_copy(hh)
                act.wait_ge(o2_ready.sem, o2_ready.at(l, ATT_HEADS))
                for b in range(2):
                    src = ps[:, 6 + b, :].rearrange("p (a t) -> p a t", a=2)
                    fn(sqo[:, 2 * b:2 * b + 2, :], src, ACT.Square)
                    last = fn(pj[:, 4 + 2 * b:6 + 2 * b, 0:T2], src, ACT.Copy)
                last.then_inc(o2_sq.sem, 1)
                act.wait_ge(o2_ss.sem, o2_ss.at(l, 1))
                fn(std4, ps[:, 0:2, :].rearrange("p a (b t) -> p (a b) t", b=2), ACT.Sqrt, bias=con("eps2", 1))\
                    .then_inc(o2_std.sem, 1)
                act.drain()
                act.wait_ge(pool_cat.sem, pool_cat.at(l, 1))
                for k in range(KD):
                    if k == 4:
                        act.wait_ge(att_cat.sem, att_cat.at(l, 1))
                    fn(x_hi[:, k, 0:T2], pj[:, k, 0:T2], ACT.Copy).then_inc(cat2_hi.sem, 1)

            act.nop().then_inc(proj_ready.sem, START)
            act.nop().then_inc(proj2_ready.sem, START)
            act.wait_ge(h_in, 16)
            for k in range(KD):
                fn(x_hi[:, k, :], h[:, k, :], ACT.Copy).then_inc(xh_first, 1)
            for j in range(2):
                split_hi(0, j, W_NARROW, wait_slot=False)
            with act.Fori(0, DEPTH) as l:
                t0, q, r0 = l * TURNS1, l * 2, l * 3
                up(q, t0 + SEC1["ffn1"], T1)
                act.wait_ge(consts_in, 16)
                down(t0 + SEC1["ffn1"] + UP_T, r0, False, r0, T1)
                act.wait_ge(prm_in, l * 16 + 16)
                layer_norm(r0, "ln1b", t0 + SEC1["in"])
                act.wait_ge(h_ready, l * (3 * KD) + (KD + START))
                mixer1(l, t0 + SEC1["in"])
                out_proj(t0 + SEC1["out"], r0 + 1, False, r0 + 1, T1)
                layer_norm(r0 + 1, "ln2b", t0 + SEC1["ffn2"])
                up(q + 1, t0 + SEC1["ffn2"], T1)
                down(t0 + SEC1["ffn2"] + UP_T, r0 + 2, False, r0 + 2, T1)
                layer_norm(r0 + 2, "ln3b", t0 + TURNS1)
            for k in range(KD):
                act.wait_ge(h_ready, (3 * DEPTH - 1) * KD + k + 1 + START)
                fn(pj[:, KD + k, 0:T2], h[:, k, T1 - T2:T1], ACT.Square).then_inc(rms_sq, 1)
            rms_norm(3 * DEPTH, None)
            with act.Fori(0, DEPTH) as l:
                t0, q, r0 = l * TURNS2 + BLOCK2_TURN, l * 2 + 2 * DEPTH, l * 3 + 3 * DEPTH
                n0 = l * 3 + NORM2
                up(q, t0 + SEC2["ffn1"], T2)
                down(t0 + SEC2["ffn1"] + UP_T, r0, True, None, T2)
                rms_norm(n0, t0 + SEC2["in"])
                in_proj(t0 + SEC2["in"], IN2, proj2_ready, T2)
                mixer2(l)
                out_proj(t0 + SEC2["out"], r0 + 1, True, None, T2)
                rms_norm(n0 + 1, t0 + SEC2["ffn2"])
                up(q + 1, t0 + SEC2["ffn2"], T2)
                down(t0 + SEC2["ffn2"] + UP_T, r0 + 2, True, None, T2)
                rms_norm(n0 + 2, t0 + TURNS2)

        @block.vector
        def _(dve):
            v = nc.vector

            def split_lo(turn, j, width):
                for u in range(2):
                    lo_unit(turn, j, u, width)

            def lo_unit(turn, j, u, width):
                dve.wait_ge(hi_done, turn * 4 + (2 * j + u + 1))
                c = slice(u * width, (u + 1) * width)
                v.tensor_tensor(w_lo[:, j, c], raw[:, j, c], w_hi[:, j, c].bitcast(F32), ALU.subtract)\
                    .then_inc(lo_done, 1)

            def split_next(turn, j, width):
                split_lo(turn + j, 1 - j, width)

            def up(q, turn0, T, stream=None):
                def turn(it, next_width):
                    for j in range(2):
                        if not (isinstance(it, int) and it == 0 and j == 0):
                            split_next(turn0 + it, j, W_NARROW if j == 0 else next_width)
                        dve.wait_ge(unit_used, turn0 * 4 + it * 4 + (2 * j + 2 + START))
                        dve.wait_ge(silu_done, q * NF + it * 2 + (j + 1))
                        v.scalar_tensor_tensor(out=prod[:, j, 0:T], in0=ps[:, 2 * j + 1, 0:T], scalar=0.5,
                                               in1=silu[:, j, 0:T], op0=ALU.mult, op1=ALU.mult).then_inc(up_free, 1)
                        f = it * 2 + j
                        f = slice(f, f + 1) if isinstance(f, int) else bass.ds(f, 1)
                        src = prod[:, j:j + 1, 0:T]
                        dve.drain()
                        v.tensor_copy(hid_hi[:, f, 0:T], src)
                        dve.drain()
                        v.tensor_tensor(hid_lo[:, f, 0:T], src, hid_hi[:, f, 0:T].bitcast(F32), ALU.subtract)\
                            .then_inc(hid_ready, 1)

                turn(0, W_NARROW)
                with dve.Fori(1, UP_T - 1) as it:
                    turn(it, W_NARROW)
                if stream is not None:
                    dve.wait_ge(h_ready, stream)
                turn(UP_T - 1, W_WIDE)

            def resid(alpha, m, bank, T):
                c = slice(m, m + 1) if isinstance(m, int) else bass.ds(m, 1)
                dst = h[:, c, T1 - T:T1]
                v.scalar_tensor_tensor(out=dst, in0=dst, scalar=alpha, in1=ps[:, bank:bank + 1, 0:T],
                                       op0=ALU.mult, op1=ALU.add).then_inc(resid_ready, 1)

            def down(turn0, alpha, T):
                def turn(it, next_width):
                    for j in range(2):
                        split_next(turn0 + it, j, W_WIDE if j == 0 else next_width)
                        if next_width == W_NARROW and j == 1:
                            lo_unit(turn0 + DOWN_T, 1, 0, W_NARROW)
                        dve.wait_ge(unit_used, turn0 * 4 + it * 4 + (2 * j + 2 + START))
                        resid(alpha, it * 2 + j, 4 + j, T)

                with dve.Fori(0, DOWN_T - 1) as it:
                    turn(it, W_WIDE)
                turn(DOWN_T - 1, W_NARROW)

            def out_proj(turn0, alpha, T):
                for p in range(OUTB // 2):
                    split_next(turn0 + p // 2, p % 2, W_NARROW)
                    for u in range(2):
                        if p == OUTB // 2 - 1 and u == 1:
                            lo_unit(turn0 + OUTB // 4, 1, 0, W_NARROW)
                        dve.wait_ge(unit_used, turn0 * 4 + (2 * p + u + 1 + START))
                        resid(alpha, 2 * p + u, 4 + u, T)

            def in_proj(turn0, n):
                split_next(turn0, 1, W_NARROW)
                with dve.Fori(1, n // 4) as it:
                    for j in range(2):
                        split_next(turn0 + it, j, W_NARROW)

            def norm_chunks(number, gain, table, T, low, next_turn):
                dve.wait_ge(std_ready, number + 1)
                v.reciprocal(std[:, 1, 0:T], std[:, 0, 0:T])
                dve.drain()
                for k in range(KD):
                    v.scalar_tensor_tensor(out=pj[:, k, 0:T], in0=h[:, k, T1 - T:T1], scalar=par(table, gain, k),
                                           in1=std[:, 1, 0:T], op0=ALU.mult, op1=ALU.mult).then_inc(xn_ready, 1)
                    if k >= 2:
                        low(k - 2)
                low(KD - 2)
                low(KD - 1)
                if next_turn is not None:
                    lo_unit(next_turn, 1, 1, W_NARROW)

            def layer_norm(norm, gain, bias, next_turn):
                dve.wait_ge(mean_ready, norm + 1)
                for s in range(4):
                    c = slice(2 * s, 2 * s + 2)
                    v.tensor_tensor(h[:, c, :], h[:, c, :], ps[:, 6:7, 0:T1].broadcast_to([P, 2, T1]), ALU.subtract)\
                        .then_inc(centered, 1)

                def low(k):
                    dve.wait_ge(xh_ready, norm * KD + (k + 1))
                    v.scalar_tensor_tensor(out=x_lo[:, k, :], in0=pj[:, k, :], scalar=par(P1, bias, k),
                                           in1=x_hi[:, k, :].bitcast(F32), op0=ALU.add, op1=ALU.subtract)\
                        .then_inc(x_ready, 1)

                norm_chunks(norm, gain, P1, T1, low, next_turn)

            def rms_norm(number, gain, next_turn):
                def low(k):
                    dve.wait_ge(xh_ready, number * KD + (k + 1))
                    v.tensor_tensor(x_lo[:, k, 0:T2], pj[:, k, 0:T2], x_hi[:, k, 0:T2].bitcast(F32), ALU.subtract)\
                        .then_inc(x_ready, 1)

                norm_chunks(number, gain, P2, T2, low, next_turn)

            def cat_low(l, hi, n, T):
                for k in range(n):
                    dve.wait_ge(hi.sem, hi.at(l, k + 1))
                    v.tensor_tensor(x_lo[:, k, 0:T], pj[:, k, 0:T], x_hi[:, k, 0:T].bitcast(F32), ALU.subtract)\
                        .then_inc(x_ready, 1)

            def mixer1(l, turn0):
                def row_arguments():
                    dve.wait_ge(proj_ready.sem, proj_ready.at(l, MISC + 1))
                    v.tensor_scalar(row_u[ROWS, :], pj[ROWS, MISC, :], par(P1, "rowbias", rows=ROWS),
                                    par(P1, "rowsign", rows=ROWS), ALU.add, ALU.mult).then_inc(rows_u.sem, 1)
                    v.memset(row_cum[0:ROW0, :], 0.0)

                def row_sums():
                    dve.wait_ge(rows_ln.sem, rows_ln.at(l, 1))
                    v.scalar_tensor_tensor(out=row_sp[ROWS, :], in0=row_u[ROWS, :], scalar=0.0, in1=row_l[ROWS, :],
                                           op0=ALU.max, op1=ALU.add)
                    dve.drain()
                    v.tensor_scalar(row_u[ROWS, :], row_sp[ROWS, :], acoef[ROWS, :], -1.0, ALU.mult, ALU.mult)
                    dve.drain()
                    v.tensor_tensor_scan(row_cum[ROWS, :], con("one", 1, ROWS).broadcast_to([P - ROW0, T1]),
                                         row_u[ROWS, :], 0.0, ALU.mult, ALU.add).then_inc(rows_ready.sem, 1)

                def latents():
                    dve.wait_ge(mla_std.sem, mla_std.at(l, 1))
                    v.reciprocal(std[:, :, :], std[:, :, :])
                    dve.drain()
                    for b in range(3):
                        src, gain = (CQ0 + b, par(P1, "qg", b)) if b < 2 else (CKV, par(P1, "kvg"))
                        last = v.scalar_tensor_tensor(out=cqn[:, b, :], in0=pj[:, src, :], scalar=gain,
                                                      in1=std[:, b // 2, :], op0=ALU.mult, op1=ALU.mult)
                    last.then_inc(cqn_ready.sem, 1)

                def taps(c0):
                    dve.wait_ge(conv_seed.sem, conv_seed.at(l, c0 + 2))
                    for d in range(1, CONV):
                        for c in (c0, c0 + 1):
                            last = v.scalar_tensor_tensor(out=xc[:, c, d:T1], in0=pj[:, XBC0 + c, 0:T1 - d],
                                                          scalar=par(P1, "convw", CONV * c + CONV - 1 - d),
                                                          in1=xc[:, c, d:T1], op0=ALU.mult, op1=ALU.add)
                        if d < CONV - 1:
                            dve.drain()
                    if c0 == 4:
                        last.then_inc(conv_done.sem, 1)

                def rotate(dst, plain, bank, ready):
                    v.tensor_tensor(rot_t[:, 0, :], plain, con("cos", T1), ALU.mult)
                    v.tensor_tensor(rot_t[:, 1, :], ps[:, bank, 0:T1], con("sin", T1), ALU.mult)
                    dve.drain()
                    v.tensor_tensor(dst, rot_t[:, 0, :], rot_t[:, 1, :], ALU.add).then_inc(ready.sem, 1)

                def rotary_key():
                    dve.wait_ge(kr_raw.sem, kr_raw.at(l, 1))
                    rotate(kr, ps[:, 4, 0:T1], 5, kr_ready)

                def keys_values():
                    dve.wait_ge(ukv_done.sem, ukv_done.at(l, 1))
                    v.tensor_copy(kn, ps[:, 6:8, 0:T1])
                    v.tensor_copy(vmla[:, 0:2, :], ps[:, 5, :].rearrange("p (a b) -> p a b", a=2))
                    v.tensor_copy(vmla[0:16, 2, :], ps[0:16, 4, 0:256]).then_inc(kv_ready.sem, 1)

                def rotary_queries():
                    dve.wait_ge(qrot_done.sem, qrot_done.at(l, 1))
                    rotate(qr, qraw, 6, qr_ready)

                def token_rows():
                    dve.wait_ge(rows_t.sem, rows_t.at(l, 1))
                    rows = ps[:, 7, 0:384].rearrange("p (i r c) -> p i r c", i=3, r=2)
                    v.tensor_scalar(tok_ncum[:, 0:2, :], rows[:, 0:2, 0, :], -1.0, None, ALU.mult)
                    v.tensor_scalar(tok_ncum[0:16, 2, :], rows[0:16, 2, 0, :], -1.0, None, ALU.mult)
                    v.tensor_copy(tok_dt[:, 0:2, :], rows[:, 0:2, 1, :])
                    v.tensor_copy(tok_dt[0:16, 2, :], rows[0:16, 2, 1, :]).then_inc(tokrow_ready.sem, 1)

                def token_inputs():
                    dve.wait_ge(xs_t.sem, xs_t.at(l, 1))
                    v.tensor_copy(xtok[:, 0:2, :], ps[:, 4:6, :])
                    v.tensor_copy(xtok[0:16, 2, :], ps[0:16, 6, :]).then_inc(tok_ready.sem, 1)

                def pair(p, *steps):
                    if p > 0:
                        split_lo(turn0 + (p + 1) // 2, (p + 1) % 2, W_NARROW)
                    for step in steps:
                        step()

                pair(0, row_arguments)
                pair(1)
                pair(2, row_sums)
                pair(3, latents)
                pair(4, rotary_key, lambda: taps(0))
                pair(5, lambda: taps(2))
                pair(6, keys_values, lambda: taps(4))
                pair(7, rotary_queries, token_rows)
                pair(8, token_inputs)
                pair(9)

                dve.wait_ge(vf_t.sem, vf_t.at(l, 1))
                v.tensor_copy(vfox[:, 0:2, :], ps[:, 7, :].rearrange("p (a b) -> p a b", a=2))
                v.tensor_copy(vfox[0:16, 2, :], ps[0:16, 6, 0:256]).then_inc(vf_ready.sem, 1)

                def gate(c):
                    dve.wait_ge(y_ready.sem, y_ready.at(l, 2 * c + 2))
                    v.scalar_tensor_tensor(out=xc[:, c, :], in0=xc[:, c, :], scalar=par(P1, "dskip", c),
                                           in1=ps[:, 4 + c % 2, 0:T1], op0=ALU.mult, op1=ALU.add)
                    dve.drain()
                    v.tensor_tensor(xc[:, c, :], xc[:, c, :], pj[:, Z0 + c, :], ALU.mult).then_inc(yz_ready.sem, 1)

                dve.drain()
                for hh in range(SSD_HEADS):
                    dve.wait_ge(g_ready.sem, g_ready.at(l, hh // 4 + 1))
                    dve.wait_ge(decay.sem, decay.at(l, hh + 1))
                    if hh >= 2:
                        dve.wait_ge(y_ready.sem, y_ready.at(l, hh - 1))
                    for i, (t, n) in enumerate(TILES):
                        c = slice(TRI[i], TRI[i] + TRI_W[i])
                        last = v.scalar_tensor_tensor(out=ptr[0:n, hh % 2, c], in0=ps[0:n, hh // 4, c],
                                                      scalar=tok_dt[0:n, i, hh:hh + 1], in1=prob[0:n, hh % 3, c],
                                                      op0=ALU.mult, op1=ALU.mult)
                    last.then_inc(ssd_w.sem, 1)
                    if hh % 2 == 1 and hh >= 3:
                        gate(hh // 2 - 1)
                gate(3)

                def maxima(n_):
                    dve.wait_ge(s_ready.sem, s_ready.at(l, n_ + 1))
                    s = n_ % 3
                    for i, (t, n) in enumerate(QTILES):
                        v.reduce_max(amax[0:n, s, i:i + 1], ps[0:n, S_BANK[s], S_COL[i]:S_COL[i] + KEYS[i]], AX_X)
                    dve.drain()
                    v.tensor_scalar(nmax[:, s, 0:3], amax[:, s, 0:3], -(MLA_SCALE if n_ < MLA_HEADS else FOX_SCALE),
                                    None, ALU.mult).then_inc(nm_ready.sem, 1)

                def normalise(n_):
                    dve.wait_ge(exp_done.sem, exp_done.at(l, n_ + 1))
                    s = n_ % 3
                    v.reciprocal(rsum[:, s, 0:3], asum[:, s, 0:3])
                    dve.drain()
                    for i, (t, n) in enumerate(QTILES):
                        p = prob[0:n, s, S_COL[i]:S_COL[i] + KEYS[i]]
                        last = v.tensor_scalar(p, p, rsum[0:n, s, i:i + 1], None, ALU.mult)
                    last.then_inc(p_ready.sem, 1)

                def o_low(pair):
                    dve.wait_ge(cat_hi.sem, cat_hi.at(l, 4 + pair + 1))
                    v.tensor_tensor(x_lo[:, 4 + pair, :], ps[:, O_BANK[pair % 2], 0:T1],
                                    x_hi[:, 4 + pair, :].bitcast(F32), ALU.subtract).then_inc(x_ready, 1)

                maxima(0)
                maxima(1)
                normalise(0)
                for n_ in range(NH):
                    if n_ + 2 < NH:
                        maxima(n_ + 2)
                    if n_ + 1 < NH:
                        normalise(n_ + 1)
                    if n_ == 0:
                        dve.wait_ge(ystd_ready.sem, ystd_ready.at(l, 1))
                        v.reciprocal(std[:, :, :], std[:, :, :])
                        dve.drain()
                        for c in range(4):
                            last = v.scalar_tensor_tensor(out=pj[:, c, :], in0=xc[:, c, :], scalar=par(P1, "ssdg", c),
                                                          in1=std[:, c // 2, :], op0=ALU.mult, op1=ALU.mult)
                        last.then_inc(ssd_cat.sem, 1)
                    if n_ == 2:
                        cat_low(l, cat_hi, 4, T1)
                    if n_ % 2 == 1 and n_ >= 3:
                        o_low((n_ - 3) // 2)
                o_low(NH // 2 - 1)

            def mixer2(l):
                lq = par(P2, "lamq", 0, 128)
                v.tensor_tensor(prod[:, 0, 0:128], lq, par(P2, "lamk", 0, 128), ALU.mult)
                dve.drain()
                v.reduce_sum(lam_s, prod[:, 0, 0:128].rearrange("p (a b) -> p a b", a=2), AX_X).then_inc(lam_dot.sem, 1)
                v.tensor_scalar(g_lam, par(P2, "headg", 0, 4), par(P2, "onemlam"), None, ALU.mult)
                dve.wait_ge(lam_exp.sem, lam_exp.at(l, 1))
                v.tensor_scalar(neg_lam, lam_e[:, 1:2], lam_e[:, 0:1], par(P2, "laminit"), ALU.subtract, ALU.subtract)
                dve.wait_ge(v_t.sem, v_t.at(l, 1))
                v.tensor_copy(vtok, ps[:, 2:4, :]).then_inc(v_ready.sem, 1)
                dve.wait_ge(pm_done.sem, pm_done.at(l, 1))
                v.tensor_copy(poolm, ps[:, 4, :].rearrange("p (a t) -> p a t", a=2)).then_inc(pm_ready.sem, 1)
                dve.wait_ge(py_done.sem, py_done.at(l, 1))
                for b in range(2):
                    last = v.tensor_scalar(pj[:, b, 0:T2], ps[:, 5, 256 * b:256 * b + T2], par(P2, "pscale", b), None,
                                           ALU.mult)
                last.then_inc(pool_cat.sem, 1)

                def maxima(hh):
                    dve.wait_ge(s2_ready.sem, s2_ready.at(l, hh + 1))
                    s = hh % 2
                    v.reduce_max(amax[:, s, :], ps[:, 2 * s:2 * s + 2, :].rearrange("p j (i k) -> p (j i) k", i=2), AX_X)
                    dve.drain()
                    v.tensor_scalar(nmax[:, s, :], amax[:, s, :], -ATT_SCALE, None, ALU.mult).then_inc(nm2_ready.sem, 1)

                def difference(hh):
                    dve.wait_ge(exp2_done.sem, exp2_done.at(l, hh + 1))
                    if hh >= 2:
                        dve.wait_ge(t2_ready.sem, t2_ready.at(l, hh - 1))
                    s = hh % 2
                    v.reciprocal(rsum[:, s, :], asum[:, s, :])
                    dve.drain()
                    v.tensor_scalar(rlam[:, s, :], rsum[:, s, 2:4], neg_lam, None, ALU.mult)
                    for i in range(2):
                        v.tensor_scalar(prob2[:, s, i, :], prob2[:, s, i, :], rsum[:, s, i:i + 1], None, ALU.mult)
                    dve.drain()
                    for i in range(2):
                        last = v.scalar_tensor_tensor(out=attn[:, s, i, :], in0=prob2[:, s, 2 + i, :],
                                                      scalar=rlam[:, s, i:i + 1], in1=prob2[:, s, i, :],
                                                      op0=ALU.mult, op1=ALU.add)
                    last.then_inc(a2_ready.sem, 1)

                maxima(0)
                for hh in range(ATT_HEADS):
                    if hh + 1 < ATT_HEADS:
                        maxima(hh + 1)
                    difference(hh)
                dve.wait_ge(o2_std.sem, o2_std.at(l, 1))
                v.reciprocal(std4, std4)
                dve.drain()
                for hh in range(ATT_HEADS):
                    o = pj[:, 4 + hh, 0:T2]
                    last = v.scalar_tensor_tensor(out=o, in0=o, scalar=g_lam[:, hh:hh + 1], in1=std4[:, hh, :],
                                                  op0=ALU.mult, op1=ALU.mult)
                last.then_inc(att_cat.sem, 1)
                cat_low(l, cat2_hi, KD, T2)

            v.memset(small[:], 1.0)
            dve.nop().then_inc(up_free, CREDIT)
            dve.nop().then_inc(resid_ready, CREDIT)
            dve.nop().then_inc(prm_free, START)
            dve.wait_ge(h_in, 16)
            for k in range(KD):
                dve.wait_ge(xh_first, k + 1)
                v.tensor_tensor(x_lo[:, k, :], h[:, k, :], x_hi[:, k, :].bitcast(F32), ALU.subtract).then_inc(x_ready, 1)
            for j in range(2):
                split_lo(0, j, W_NARROW)
            with dve.Fori(0, DEPTH) as l:
                t0, q, r0 = l * TURNS1, l * 2, l * 3
                up(q, t0 + SEC1["ffn1"], T1, l * (3 * KD) + START)
                down(t0 + SEC1["ffn1"] + UP_T, ALPHA, T1)
                dve.wait_ge(prm_in, l * 16 + 16)
                layer_norm(r0, "ln1g", "ln1b", t0 + SEC1["in"])
                dve.wait_ge(consts_in, 16)
                mixer1(l, t0 + SEC1["in"])
                dve.wait_ge(h_ready, l * (3 * KD) + (KD + START))
                out_proj(t0 + SEC1["out"], ALPHA, T1)
                layer_norm(r0 + 1, "ln2g", "ln2b", t0 + SEC1["ffn2"])
                up(q + 1, t0 + SEC1["ffn2"], T1, l * (3 * KD) + (2 * KD + START))
                down(t0 + SEC1["ffn2"] + UP_T, ALPHA, T1)
                layer_norm(r0 + 2, "ln3g", "ln3b", t0 + TURNS1)
            dve.wait_ge(prm_in, 16 * DEPTH + 16)
            rms_norm(3 * DEPTH, "firstg", None)
            with dve.Fori(0, DEPTH) as l:
                t0, q = l * TURNS2 + BLOCK2_TURN, l * 2 + 2 * DEPTH
                n0 = l * 3 + NORM2
                up(q, t0 + SEC2["ffn1"], T2)
                down(t0 + SEC2["ffn1"] + UP_T, 1.0, T2)
                dve.wait_ge(prm_in, l * 16 + (16 * DEPTH + 16))
                rms_norm(n0, "mixg", t0 + SEC2["in"])
                in_proj(t0 + SEC2["in"], IN2)
                mixer2(l)
                out_proj(t0 + SEC2["out"], 1.0, T2)
                rms_norm(n0 + 1, "ffn2g", t0 + SEC2["ffn2"])
                up(q + 1, t0 + SEC2["ffn2"], T2)
                down(t0 + SEC2["ffn2"] + UP_T, 1.0, T2)
                rms_norm(n0 + 2, "nextg", t0 + TURNS2)
                dve.drain().then_inc(prm_free, 1)

        @block.gpsimd
        def _(pool):
            def residual(l, n, bias):
                event = l * 4 + (1, 3, 4)[n]
                for k in range(KD):
                    pool.wait_ge(x_ready, event * KD + (k + 1))
                    nc.gpsimd.tensor_tensor(h[:, k, :], pj[:, k, :], par(P1, bias, k).broadcast_to([P, T1]), ALU.add)\
                        .then_inc(h_ready, 1)

            pool.nop().then_inc(h_ready, START)
            pool.wait_ge(consts_in, 16)
            nc.gpsimd.tensor_copy(masks[:], con("ident", 3 * P)).then_inc(masks_ready, 1)
            with pool.Fori(0, DEPTH) as l:
                residual(l, 0, "ln1b")
                residual(l, 1, "ln2b")
                residual(l, 2, "ln3b")
                pool.drain().then_inc(prm_free, 1)


def blocks_of(w, n_chunks):
    k, n = w.shape
    return w.reshape(n_chunks, P, n // P, P).transpose(2, 1, 0, 3).reshape(n // P, P, n_chunks * P)


def in_pairs(b):
    n, p, w = b.shape
    return b.reshape(n // 2, 2, p, w).transpose(0, 2, 1, 3).reshape(n // 2, p, 2 * w)


def columns(v):
    return v.reshape(-1, P).T


def kernel(**inputs):
    import concourse.bacc as bacc
    from concourse.bass_utils import run_bass_kernel_spmd

    a = {k: np.asarray(v) for k, v in inputs.items()}
    f32 = np.float32
    ffn = [(s, f, l) for s in ("", "_2") for l in range(DEPTH) for f in ("ffn1", "ffn2")]
    w_up = np.zeros((len(ffn) * NF + PAD_PAIRS, P, 2 * W_NARROW), f32)
    w_down = np.zeros((len(ffn) * KD, P, 2 * W_WIDE), f32)
    for n, (s, f, l) in enumerate(ffn):
        w_up[n * NF:(n + 1) * NF, :, 0:W_NARROW] = blocks_of(a[f"{f}_w_gate{s}"][l], KD)
        w_up[n * NF:(n + 1) * NF, :, W_NARROW:] = blocks_of(a[f"{f}_w_up{s}"][l], KD)
        w_down[n * KD:(n + 1) * KD] = blocks_of(a[f"{f}_w_down{s}"][l], NF)
    hd2 = HD + ROPE
    w_in1, prm1, prm2 = [], np.zeros((DEPTH, P, P1_W), f32), np.zeros((DEPTH, P, P2_W), f32)
    for l in range(DEPTH):
        w = a["w_in"][l]
        z, xbc, dt, fq, fk, fv, fr, cq, ckv, kr = np.split(w, np.cumsum([512, 768, 8, 256, 256, 256, 4, 256, 128])
                                                           .tolist(), axis=1)
        misc = np.zeros((D, P), f32)
        misc[:, 0:ROPE], misc[:, ROW0:ROW0 + 8], misc[:, FROW0:FROW0 + 4] = kr, dt, fr
        w_in1.append(in_pairs(blocks_of(np.concatenate([misc, ckv, cq, xbc, z, fq, fk, fv], axis=1), KD)))

        p = prm1[l]

        def put(table, dst, name, v):
            dst[:, table[name]:table[name] + v.shape[1]] = v

        for name, key in (("ln1g", "ln1_g"), ("ln1b", "ln1_b"), ("ln2g", "ln2_g"), ("ln2b", "ln2_b"), ("ln3g", "ln3_g"),
                          ("ln3b", "ln3_b"), ("convb", "conv_b"), ("ssdg", "ssd_norm_g"), ("qg", "mla_q_norm_g"),
                          ("kvg", "mla_kv_norm_g")):
            put(P1, p, name, columns(a[key][l]))
        put(P1, p, "convw", a["conv_w"][l].reshape(CONV, 6, P).transpose(2, 1, 0).reshape(P, 6 * CONV))
        put(P1, p, "dskip", columns(np.repeat(a["d_skip"][l], HD)))
        p[ROW0:ROW0 + 8, P1["rowbias"]] = a["dt_bias"][l]
        p[FROW0:FROW0 + 4, P1["rowbias"]] = a["fox_f_b"][l]
        p[ROW0:ROW0 + 8, P1["rowsign"]] = 1.0
        p[FROW0:FROW0 + 4, P1["rowsign"]] = -1.0
        p[ROW0:ROW0 + 8, P1["alog"]] = a["a_log"][l]
        uq = a["mla_w_uq"][l].reshape(256, MLA_HEADS, hd2)
        uq = np.concatenate([uq[:, :, :HD].reshape(256, -1), uq[:, :, HD:].reshape(256, -1)], axis=1)
        put(P1, p, "uq", uq.reshape(2, P, 384).transpose(1, 0, 2).reshape(P, -1))
        ukv = a["mla_w_ukv"][l].reshape(P, MLA_HEADS, 2 * HD)
        put(P1, p, "ukv", np.concatenate([ukv[:, :, :HD].reshape(P, -1), ukv[:, :, HD:].reshape(P, -1)], axis=1))

        p = prm2[l]
        last = l == DEPTH - 1
        put(P2, p, "mixg", columns(a["mix_norm_2"][l]))
        put(P2, p, "ffn2g", columns(a["ffn2_norm_2"][l]))
        put(P2, p, "nextg", columns(a["final_norm_2"] if last else a["ffn1_norm_2"][l + 1]))
        put(P2, p, "firstg", columns(a["ffn1_norm_2"][0]))
        put(P2, p, "pscale", columns(a["pool_scale_2"][l]))
        put(P2, p, "headg", columns(a["attn_head_norm_2"][l]))
        lam_init = 0.8 - 0.6 * np.exp(-0.3 * l)
        p[:, P2["laminit"]] = lam_init
        p[:, P2["onemlam"]] = 1.0 - lam_init
        put(P2, p, "lamq", np.broadcast_to(np.concatenate([a["lam_q1_2"][l], a["lam_q2_2"][l]]), (P, 128)))
        put(P2, p, "lamk", np.broadcast_to(np.concatenate([a["lam_k1_2"][l], a["lam_k2_2"][l]]), (P, 128)))
        put(P2, p, "poolw", a["pool_w_2"][l].reshape(2, P, 64).transpose(1, 0, 2).reshape(P, -1))
        put(P2, p, "fourw", a["fourier_w_2"][l].reshape(2, P, 256).transpose(1, 0, 2).reshape(P, -1))
    mixed = np.concatenate([np.arange(512), np.arange(768, 1024), np.arange(512, 768)])
    w_out1 = [in_pairs(blocks_of(a["w_out"][l][mixed], KD)) for l in range(DEPTH)]
    w_in2 = [in_pairs(blocks_of(a["w_in_2"][l], KD)) for l in range(DEPTH)]
    w_out2 = [in_pairs(blocks_of(a["w_out_2"][l], KD)) for l in range(DEPTH)]
    hidden = np.concatenate([a["meta"], a["x"][0]], axis=0)
    arrays = {
        "hidden0": np.ascontiguousarray(hidden.T.reshape(KD, P, T1).transpose(1, 0, 2)),
        "w_up": w_up,
        "w_down": w_down,
        "w_in1": np.concatenate(w_in1),
        "w_out1": np.concatenate(w_out1),
        "w_in2": np.concatenate(w_in2),
        "w_out2": np.concatenate(w_out2),
        "prm1": prm1,
        "prm2": prm2,
        "consts": shape_constants(),
    }
    nc = bacc.Bacc("TRN2", target_bir_lowering=False, num_devices=1)
    args = [nc.dram_tensor(f"in_{n}", v.shape, mybir.dt.from_np(v.dtype), kind="ExternalInput").ap()
            for n, v in arrays.items()]
    args.append(nc.dram_tensor("out_0", (P, KD, T2), F32, kind="ExternalOutput").ap())
    build(nc, *args)
    r = run_bass_kernel_spmd(nc, [{f"in_{n}": v for n, v in arrays.items()}], core_ids=[0])
    y = np.asarray(r.results[0]["out_0"])
    return np.ascontiguousarray(y.transpose(1, 0, 2).reshape(D, T2).T)[None]
```

```python
from contextlib import ExitStack

import numpy as np

import concourse.bass as bass
from concourse import mybir

F32 = mybir.dt.float32
F32R = mybir.dt.float32r
BF16 = mybir.dt.bfloat16
ALU = mybir.AluOpType
ACT = mybir.ActivationFunctionType
AX_X = mybir.AxisListType.X

P = 128
D = 1024
KD = D // P
DEPTH = 2
SEQ = 256
N_META = 16
T1 = SEQ + N_META
T2 = SEQ
N1 = T1 + 2
D_FF = 2816
NF = D_FF // P
HALF_F = NF // 2
ALPHA = (2 * DEPTH) ** 0.25
EPS1, EPS2 = 1e-5, 1e-6

W_NARROW = KD * P
W_WIDE = HALF_F * P
IN1, IN2, OUTB = 20, 16, 8
UP_PAIRS, DOWN_PAIRS = NF, KD
FFN_PAIRS = UP_PAIRS + DOWN_PAIRS
LAYER1_PAIRS = 2 * FFN_PAIRS + IN1 // 2 + OUTB // 2
LAYER2_PAIRS = 2 * FFN_PAIRS + IN2 // 2 + OUTB // 2
PAD_PAIRS = 2

MISC, CKV, CQ0, XBC0, Z0, FQ0, FK0, FV0 = 0, 1, 2, 4, 10, 14, 16, 18
SSD_HEADS, FOX_HEADS, MLA_HEADS, HD, ROPE = 8, 4, 4, 64, 32
CONV = 4
ROW0 = 64
FROW0 = 96
MLA_SCALE = float(np.float32((HD + ROPE) ** -0.5))
FOX_SCALE = HD ** -0.5
MASK = -1e30
TILES = [(0, 128), (128, 128), (256, 16)]
TRI = [0, 272, 416]
TRI_W = [T1 - t for t, _ in TILES]
QTILES = [(0, N_META), (N_META, P), (N_META + P, P)]
KEYS = [t + n for t, n in QTILES]
S_COL = [0, KEYS[0], KEYS[0] + KEYS[1]]
S_W = sum(KEYS)
PT_K1, PT_META, PT_END1, PT_END2, PT_W = 2 * P, 3 * P, 3 * P + N_META, 3 * P + N_META + 48, 4 * P

P1 = {}
_n = 0
for _name, _w in (("ln1g", 8), ("ln1b", 8), ("ln2g", 8), ("ln2b", 8), ("ln3g", 8), ("ln3b", 8), ("convw", 24),
                  ("convb", 6), ("dskip", 4), ("ssdg", 4), ("qg", 2), ("kvg", 1), ("rowbias", 1), ("rowsign", 1),
                  ("alog", 1), ("firstg", 8), ("uq", 2 * 384), ("ukv", 512)):
    P1[_name] = _n
    _n += _w
P1_W = _n
P2 = {}
_n = 0
for _name, _w in (("mixg", 8), ("ffn2g", 8), ("nextg", 8), ("pscale", 2), ("headg", 4), ("laminit", 1),
                  ("onemlam", 1), ("lamq", 128), ("lamk", 128), ("poolw", 128), ("fourw", 512)):
    P2[_name] = _n
    _n += _w
P2_W = _n
PRM_W = max(P1_W, P2_W)
ATT_HEADS = 4
POOL_WINDOWS = (2, 4, 8, 16)
ATT_SCALE = 64 ** -0.5

CC = {}
_n = 0
for _name, _w in (("ident", 128), ("maskS", 128), ("maskA", 128), ("onesD", 128), ("ones256", 128), ("ones128", 128), ("rot", 128), ("rep", 128),
                  ("reprot", 128), ("cos", T1), ("sin", T1), ("sel", 12 * 128), 
                  ("eps1", 1), ("eps2", 1), ("one", 1), ("band", 4 * 2 * 256), ("cs", 512), ("ss", 512),
                  ("ccos", 128), ("csin", 128), ("absd", 512), ("slope", 4 * 128)):
    CC[_name] = _n
    _n += _w
CC_W = _n
CC_FIRST = CC["band"]


def shape_constants():
    c = np.zeros((P, CC_W), np.float32)

    def put(name, a, rows=slice(0, P)):
        a = np.asarray(a, np.float64).astype(np.float32)
        c[rows, CC[name]:CC[name] + a.shape[1]] = a

    put("ident", np.eye(P))
    put("onesD", np.full((P, P), 1.0 / D))
    put("ones256", np.full((P, P), 1.0 / 256))
    put("ones128", np.full((P, P), 1.0 / 128))
    r32 = np.zeros((32, 32))
    for i in range(16):
        r32[16 + i, i] = -1.0
        r32[i, 16 + i] = 1.0
    put("rot", np.kron(np.eye(4), r32))
    put("rep", np.tile(np.eye(32), (1, 4)), slice(0, 32))
    put("reprot", np.tile(r32, (1, 4)), slice(0, 32))
    inv = (1.0 / (10000.0 ** (np.arange(0, ROPE, 2, dtype=np.float32) / np.float32(ROPE)))).astype(np.float32)
    ang = (np.arange(T1, dtype=np.float32)[:, None] * inv[None, :]).astype(np.float32).astype(np.float64)
    idx = (np.arange(P) % 32) % 16
    put("cos", np.cos(ang).T[idx])
    put("sin", np.sin(ang).T[idx])
    sel = np.zeros((P, 12, 128))
    for h in range(8):
        sel[ROW0 + h, h] = 1.0
    for h in range(4):
        sel[FROW0 + h, 8 + h] = -1.0 / FOX_SCALE
    put("sel", sel.reshape(P, -1))
    a = np.arange(P)
    put("maskS", np.where(a[None, :] < a[:, None], MASK, 0.0))
    put("maskA", np.where(a[None, :] > a[:, None], MASK, 0.0))
    put("eps1", np.full((P, 1), EPS1))
    put("eps2", np.full((P, 1), EPS2))
    put("one", np.ones((P, 1)))
    band = np.zeros((4, 256, 256))
    for g, w in enumerate(POOL_WINDOWS):
        for t in range(256):
            lo, hi = max(t - w // 2, 0), min(t + w - w // 2, 256)
            band[g, lo:hi, t] += 1.0 / (hi - lo)
            band[g, t, t] -= 1.0
    put("band", band.reshape(4, 2, P, 256).transpose(2, 0, 1, 3).reshape(P, -1))
    s = np.arange(256)
    ang = 2 * np.pi * ((s[:, None] * s[None, :]) % 256) / 256
    put("cs", np.cos(ang).reshape(2, P, 256).transpose(1, 0, 2).reshape(P, -1))
    put("ss", np.sin(ang).reshape(2, P, 256).transpose(1, 0, 2).reshape(P, -1))
    m = np.arange(64)
    ang = 2 * np.pi * ((m[:, None] * m[None, :]) % 64) / 64
    ortho = 1.0 / np.sqrt(256 * 64)
    put("ccos", np.kron(np.eye(2), np.cos(ang) * ortho))
    put("csin", np.kron(np.eye(2), -np.sin(ang) * ortho))
    q = np.arange(256)
    absd = np.abs(q[:, None] - q[None, :])
    put("absd", absd.reshape(2, P, 256).transpose(1, 0, 2).reshape(P, -1))
    slopes = [2.0 ** (-8.0 * (i + 1) / ATT_HEADS) for i in range(ATT_HEADS)]
    put("slope", np.concatenate([np.eye(P) * (-sl / ATT_SCALE) for sl in slopes], axis=1))
    return c


class Signal:

    def __init__(self, sem, per_layer, start):
        self.sem, self.per_layer, self.start = sem, per_layer, start

    def at(self, layer, n):
        return layer * self.per_layer + (n + self.start)


def build(nc, hidden0, w_up, w_down, w_in1, w_out1, w_in2, w_out2, prm1, prm2, consts, out):
    with ExitStack() as ctx:
        def sb(name, shape, dt=F32):
            return ctx.enter_context(nc.sbuf_tensor(name, shape, dt))

        def sem(name):
            return ctx.enter_context(nc.semaphore(name))

        def signal(name, per_layer, start=0):
            return Signal(sem(name), per_layer, start)

        raw = sb("raw", [P, 2, 2 * W_WIDE])
        w_hi = sb("w_hi", [P, 2, 2 * W_WIDE], F32R)
        w_lo = sb("w_lo", [P, 2, 2 * W_WIDE], F32R)
        x_hi = sb("x_hi", [P, KD, N1], F32R)
        x_lo = sb("x_lo", [P, KD, N1], F32R)
        rstd = sb("rstd", [P, T1])
        h = sb("h", [P, KD, T1])
        pj = sb("pj", [P, IN1, T1])
        silu = sb("silu", [P, 2, T1])
        prod = sb("prod", [P, 2, T1])
        prm = sb("prm", [P, PRM_W])
        cst = sb("cst", [P, CC_W])
        std = sb("std", [P, 2, T1])
        h_sum = sb("h_sum", [P, T1])
        sq_sum = sb("sq_sum", [P, T1])
        small = sb("small", [P, 96])
        masks = sb("masks", [P, 3 * P], BF16)
        alibi = sb("alibi", [P, 2 * T2 + ATT_HEADS * P], BF16)
        hid_hi = sb("hid_hi", [P, NF, T1], F32R)
        hid_lo = sb("hid_lo", [P, NF, T1], F32R)
        HID_BYTES = NF * T1 * 4
        hid_at = nc.sbuf_base - 2 * HID_BYTES
        SCRATCH = 2 * NF * T1
        scr = nc.alloc_sbuf_tensor_at("scratch", [P, SCRATCH], F32, offset=hid_at)
        ps = ctx.enter_context(nc.psum_tensor("ps", [P, 8, 512], F32))

        used = [0]

        def take(*shape):
            n = int(np.prod(shape))
            a = scr[:, used[0]:used[0] + n]
            used[0] += n
            assert used[0] <= SCRATCH
            if len(shape) == 2:
                a = a.rearrange("p (a b) -> p a b", a=shape[0])
            if len(shape) == 3:
                a = a.rearrange("p (a b c) -> p a b c", a=shape[0], b=shape[1])
            return a

        def con(name, w=128, rows=slice(0, P)):
            return cst[rows, CC[name]:CC[name] + w]

        def par(table, name, k=0, w=1, rows=slice(0, P)):
            return prm[rows, table[name] + k:table[name] + k + w]

        ident = con("ident")

        h_in = sem("h_in")
        consts_in = sem("consts_in")
        prm_in = sem("prm_in")
        prm_free = sem("prm_free")
        stored = sem("stored")
        raw_landed = [sem("raw_landed0"), sem("raw_landed1")]
        hi_done = sem("hi_done")
        lo_done = sem("lo_done")
        unit_used = sem("unit_used")
        xh_first = sem("xh_first")
        x_ready = sem("x_ready")
        gate_ready = sem("gate_ready")
        silu_done = sem("silu_done")
        up_free = sem("up_free")
        hid_ready = sem("hid_ready")
        resid_ready = sem("resid_ready")
        mean_ready = sem("mean_ready")
        h_summed = sem("h_summed")
        sq_summed = sem("sq_summed")
        centered = sem("centered")
        ln_sq = sem("ln_sq")
        rms_sq = sem("rms_sq")
        var_ready = sem("var_ready")
        std_ready = sem("std_ready")
        rstd_ready = sem("rstd_ready")
        out_ready = sem("out_ready")
        h_ready = sem("h_ready")
        xh_ready = sem("xh_ready")
        CREDIT, START = 2, 1
        masks_ready = sem("masks_ready")

        NH = FOX_HEADS + MLA_HEADS
        conv_seed = signal("conv_seed", 6)
        conv_done = signal("conv_done", 1)
        xc_ready = signal("xc_ready", 1)
        proj_scaled = signal("proj_scaled", IN1)
        proj_ready = signal("proj_ready", IN1)
        rows_u = signal("rows_u", 1)
        rows_ln = signal("rows_ln", 1)
        rows_ready = signal("rows_ready", 1)
        mla_sq = signal("mla_sq", 1)
        mla_ss = signal("mla_ss", 1)
        mla_std = signal("mla_std", 1)
        cqn_ready = signal("cqn_ready", 1)
        ckvn_ready = signal("ckvn_ready", 1)
        kr_raw = signal("kr_raw", 1)
        kr_ready = signal("kr_ready", 1)
        uq_done = signal("uq_done", 1)
        ukv_done = signal("ukv_done", 1)
        qn_ready = signal("qn_ready", 1)
        kv_ready = signal("kv_ready", 1)
        qrot_done = signal("qrot_done", 1)
        qr_ready = signal("qr_ready", 1)
        vf_t = signal("vf_t", 1)
        vf_ready = signal("vf_ready", 1)
        xs_t = signal("xs_t", 1)
        rows_t = signal("rows_t", 1)
        tokrow_ready = signal("tokrow_ready", 1)
        tok_ready = signal("tok_ready", 1)
        g_ready = signal("g_ready", 2)
        d_ready = signal("d_ready", SSD_HEADS)
        decay = signal("decay", SSD_HEADS)
        ssd_w = signal("ssd_w", SSD_HEADS)
        y_ready = signal("y_ready", SSD_HEADS)
        yz_ready = signal("yz_ready", 4)
        sqy_ready = signal("sqy_ready", 1)
        yss_ready = signal("yss_ready", 1)
        ystd_ready = signal("ystd_ready", 1)
        ssd_cat = signal("ssd_cat", 2)
        s_ready = signal("s_ready", NH)
        nm_ready = signal("nm_ready", NH)
        exp_done = signal("exp_done", NH)
        p_ready = signal("p_ready", NH)
        t_ready = signal("t_ready", NH)
        pt_ready = signal("pt_ready", NH)
        o_ready = signal("o_ready", NH)
        cat_hi = signal("cat_hi", KD)
        proj2_ready = signal("proj2_ready", IN2)
        af_t = signal("af_t", 1)
        af_ready = signal("af_ready", 1)
        v_t = signal("v_t", 1)
        v_ready = signal("v_ready", 1)
        pm_done = signal("pm_done", 1)
        pm_ready = signal("pm_ready", 1)
        uv_done = signal("uv_done", 1)
        uv_ready = signal("uv_ready", 1)
        py_done = signal("py_done", 1)
        pool_cat = signal("pool_cat", 1)
        f2_done = signal("f2_done", 1)
        f2_ready = signal("f2_ready", 1)
        f3_done = signal("f3_done", 1)
        four_cat = signal("four_cat", 1)
        lam_dot = signal("lam_dot", 1)
        lam_exp = signal("lam_exp", 1)
        s2_ready = signal("s2_ready", ATT_HEADS)
        nm2_ready = signal("nm2_ready", ATT_HEADS)
        exp2_done = signal("exp2_done", ATT_HEADS)
        a2_ready = signal("a2_ready", ATT_HEADS)
        t2_ready = signal("t2_ready", ATT_HEADS)
        at2_ready = signal("at2_ready", ATT_HEADS)
        o2_ready = signal("o2_ready", ATT_HEADS)
        o2_sq = signal("o2_sq", 2)
        o2_ss = signal("o2_ss", 2)
        o2_std = signal("o2_std", 2)
        att_cat = signal("att_cat", ATT_HEADS)
        cat2_hi = signal("cat2_hi", KD)

        xc = take(6, T1)
        xtok = take(3, 512)
        tok_ncum = take(3, 64)
        tok_dt = take(3, 64)
        vfox = take(3, 256)
        vmla = take(3, 256)
        cqn = take(3, T1)
        qn = take(2, T1)
        qr = take(T1)
        kn = take(2, T1)
        kr = take(T1)
        qraw = take(T1)
        rot_t = take(2, T1)
        row_u = take(T1)
        row_l = take(T1)
        row_sp = take(T1)
        row_cum = take(T1)
        prob = take(3, S_W)
        ptr = take(2, PT_W)
        lat_sq = prob.rearrange("p a w -> p (a w)")[:, 0:3 * T1].rearrange("p (a t) -> p a t", a=3)
        ssd_sq = (silu, prod)
        used[0] = 0
        aftok = take(2, 512)
        vtok = take(2, 512)
        poolm = take(2, T2)
        uu = take(2, T2)
        vv = take(2, T2)
        y4 = take(2, T2)
        prob2 = take(2, 4, T2)
        attn = take(2, 2, T2)
        attn_t = take(2, 2, T2)
        sqo = take(4, T2)
        std4 = take(4, T2)
        ROWS = slice(ROW0, P)
        head_rows = lambda hh: slice(64 * (hh % 2), 64 * (hh % 2) + 64)

        amax, nmax, asum, rsum = (small[:, 12 * i:12 * i + 12].rearrange("p (a b) -> p a b", a=3) for i in range(4))
        acoef = small[:, 48:49]
        lam_s, lam_e, neg_lam = small[:, 49:51], small[:, 51:53], small[:, 53:54]
        g_lam = small[:, 54:58]
        rlam = small[:, 58:64].rearrange("p (a b) -> p a b", a=3)

        wcol, wblk = small[:, 64:68], small[:, 68:68 + IN1]

        FFN_T, UP_T, DOWN_T = FFN_PAIRS // 2, UP_PAIRS // 2, DOWN_PAIRS // 2
        SEC1 = {"ffn1": 0, "in": FFN_T, "out": FFN_T + IN1 // 4, "ffn2": FFN_T + IN1 // 4 + OUTB // 4}
        SEC2 = {"ffn1": 0, "in": FFN_T, "out": FFN_T + IN2 // 4, "ffn2": FFN_T + IN2 // 4 + OUTB // 4}
        TURNS1, TURNS2 = LAYER1_PAIRS // 2, LAYER2_PAIRS // 2
        BLOCK2_TURN = DEPTH * TURNS1
        ALL_TURNS = BLOCK2_TURN + DEPTH * TURNS2
        NORM2 = 3 * DEPTH + 1
        EVENT2 = 4 * DEPTH + 1

        D_BANK, S_BANK, O_BANK = (2, 3, 6), (7, 6, 0), (1, 4, 5, 1)
        S2_BANK = (6, 0, 2, 0)
        absd_bf = alibi[:, 0:2 * T2].rearrange("p (i k) -> p i k", i=2)
        slope_bf = alibi[:, 2 * T2:].rearrange("p (h k) -> p h k", h=ATT_HEADS)
        ident_bf, maskS_bf, maskA_bf = (masks[:, P * i:P * i + P] for i in range(3))

        block = ctx.enter_context(nc.Block())

        @block.sync
        def _(sp):
            def load_pair(j, src, width):
                sp.dma_start(raw[:, j, 0:2 * width], src).then_inc(raw_landed[j], 16)

            def section(turn0, n, src, width, next_src, next_width):
                with sp.Fori(0, n - 1) as it:
                    for j in range(2):
                        sp.wait_ge(lo_done, turn0 * 4 + it * 4 + (2 * j + 2))
                        load_pair(j, src(it * 2 + (2 + j)), width)
                for j in range(2):
                    sp.wait_ge(lo_done, turn0 * 4 + (4 * (n - 1) + 2 * j + 2))
                    load_pair(j, next_src(j), next_width)

            def ffn(q, turn0, next_src, next_width):
                section(turn0, UP_T, lambda i: w_up[q * NF + i], W_NARROW, lambda i: w_down[q * KD + i], W_WIDE)
                section(turn0 + UP_T, DOWN_T, lambda i: w_down[q * KD + i], W_WIDE, next_src, next_width)

            def layer(l, turn0, sec, q, w_in, n_in, w_out):
                def win(i):
                    return w_in[l * (n_in // 2) + i]

                def wout(i):
                    return w_out[l * (OUTB // 2) + i]

                ffn(q, turn0 + sec["ffn1"], win, W_NARROW)
                section(turn0 + sec["in"], n_in // 4, win, W_NARROW, wout, W_NARROW)
                section(turn0 + sec["out"], OUTB // 4, wout, W_NARROW, lambda i: w_up[(q + 1) * NF + i], W_NARROW)
                ffn(q + 1, turn0 + sec["ffn2"], lambda i: w_up[(q + 2) * NF + i], W_NARROW)

            load_pair(0, w_up[0], W_NARROW)
            sp.dma_start(h[:], hidden0).then_inc(h_in, 16)
            load_pair(1, w_up[1], W_NARROW)
            with sp.Fori(0, DEPTH) as l:
                layer(l, l * TURNS1, SEC1, l * 2, w_in1, IN1, w_out1)
            with sp.Fori(0, DEPTH) as l:
                layer(l, l * TURNS2 + BLOCK2_TURN, SEC2, l * 2 + 2 * DEPTH, w_in2, IN2, w_out2)
            for j in range(2):
                sp.wait_ge(raw_landed[j], 16 * (ALL_TURNS + 1))
            for c in range(2):
                half = slice(c * KD // 2, (c + 1) * KD // 2)
                sp.wait_ge(out_ready, (c + 1) * KD // 2)
                sp.dma_start(out[:, half, :], pj[:, half, 0:T2]).then_inc(stored, 16)
            sp.wait_ge(stored, 32)

        @block.tensor
        def _(pe):
            mm = nc.tensor.matmul
            tr = nc.tensor.transpose

            def three(dst, j, cols, xa, xb, first, last):
                mm(dst, w_lo[:, j, cols], xa, start=first, stop=False)
                mm(dst, w_hi[:, j, cols], xb, start=False, stop=False)
                return mm(dst, w_hi[:, j, cols], xa, start=False, stop=last)

            def narrow_unit(turn, j, u, dst, T):
                pe.wait_ge(lo_done, turn * 4 + (2 * j + u + 1))
                for k in range(KD):
                    c = u * W_NARROW + k * P
                    last = three(dst, j, slice(c, c + P), x_hi[:, k, 0:T], x_lo[:, k, 0:T], k == 0, k == KD - 1)
                last.then_inc(unit_used, 1)

            def first_pair(turn, event, bank, T):
                pe.wait_ge(lo_done, turn * 4 + 2)
                for k in range(KD):
                    pe.wait_ge(x_ready, event * KD + (k + 1))
                    for u in range(2):
                        c = u * W_NARROW + k * P
                        last = three(ps[:, bank + u, 0:T], 0, slice(c, c + P), x_hi[:, k, 0:T], x_lo[:, k, 0:T],
                                     k == 0, k == KD - 1)
                        if k == KD - 1:
                            last.then_inc(unit_used, 1)

            def up(q, turn0, event, T, after_first):
                pe.wait_ge(up_free, q * NF + (CREDIT - 1))
                first_pair(turn0, event, 0, T)
                after_first()
                pe.wait_ge(up_free, q * NF + CREDIT)
                for u in range(2):
                    narrow_unit(turn0, 1, u, ps[:, 2 + u, 0:T], T)
                with pe.Fori(0, (UP_T - 1) // 2) as half:
                    for i in range(4):
                        f, j = half * 4 + (2 + i), i % 2
                        pe.wait_ge(up_free, q * NF + f + (CREDIT - 1))
                        for u in range(2):
                            narrow_unit(turn0 + half * 2 + (1 + i // 2), j, u, ps[:, 2 * j + u, 0:T], T)

            def mean(norm):
                pe.wait_ge(h_summed, norm + 1)
                mm(ps[:, 6, 0:T1], con("onesD"), h_sum[:], start=True, stop=False)
                pe.wait_ge(resid_ready, norm * KD + (KD + CREDIT))
                mm(ps[:, 6, 0:T1], con("onesD"), h[:, KD - 1, :], start=False, stop=True).then_inc(mean_ready, 1)

            def mean_square(sums, last_square, n_squares, T):
                pe.wait_ge(sq_summed, sums)
                mm(ps[:, 7, 0:T], con("onesD"), sq_sum[:, 0:T], start=True, stop=False)
                pe.wait_ge(last_square, n_squares)
                mm(ps[:, 7, 0:T], con("onesD"), pj[:, 2 * KD - 1, 0:T], start=False, stop=True).then_inc(var_ready, 1)

            def variance(l, n):
                mean_square(l * 2 + (n + 1), ln_sq, l * (3 * KD) + (n * KD + KD), T1)

            def variance_chunks(l):
                for k in range(KD):
                    pe.wait_ge(ln_sq, l * (3 * KD) + (2 * KD + k + 1))
                    last = mm(ps[:, 7, 0:T1], con("onesD"), pj[:, KD + k, 0:T1], start=k == 0, stop=k == KD - 1)
                last.then_inc(var_ready, 1)

            def rms_mean_square(norm):
                mean_square(norm + (2 * DEPTH + 1), rms_sq, norm * KD + KD, T2)

            def down(q, turn0, resid, T):
                def turn(it):
                    for j in range(2):
                        pe.wait_ge(resid_ready, resid * KD + it * 2 + (j - 1 + CREDIT))
                        for u in range(2):
                            if isinstance(it, int) and j == 0:
                                pe.wait_ge(hid_ready, q * NF + (u + 1) * HALF_F)
                            pe.wait_ge(lo_done, turn0 * 4 + it * 4 + (2 * j + u + 1))
                            for c in range(HALF_F):
                                f = u * HALF_F + c
                                col = u * W_WIDE + c * P
                                last = three(ps[:, 4 + j, 0:T], j, slice(col, col + P),
                                             hid_hi[:, f, 0:T], hid_lo[:, f, 0:T], f == 0, f == NF - 1)
                            last.then_inc(unit_used, 1)

                turn(0)
                with pe.Fori(1, DOWN_T) as it:
                    turn(it)

            def out_proj(turn0, event, resid, T):
                pe.wait_ge(resid_ready, resid * KD + CREDIT)
                first_pair(turn0, event, 4, T)
                for m in range(2, KD):
                    pe.wait_ge(resid_ready, resid * KD + (m - 1 + CREDIT))
                    narrow_unit(turn0 + m // 4, (m // 2) % 2, m % 2, ps[:, 4 + m % 2, 0:T], T)

            def tri_bank(bank, i):
                n, w = TILES[i][1], TRI_W[i]
                return ps[0:n, bank, TRI[i]:TRI[i] + w]

            def mixer1(l, turn0, event):
                def block(i):
                    if i >= 4:
                        pe.wait_ge(proj_scaled.sem, proj_scaled.at(l, i - 3))
                    narrow_unit(turn0 + i // 4, (i // 2) % 2, i % 2, ps[:, i % 4, 0:N1], N1)

                first_pair(turn0, event, 0, N1)
                variance(l, 0)
                for i in range(2, 6):
                    block(i)
                pe.wait_ge(mla_sq.sem, mla_sq.at(l, 1))
                mm(ps[:, 6, 0:T1], con("ones256"), lat_sq[:, 1, :], start=True, stop=False)
                mm(ps[:, 6, 0:T1], con("ones256"), lat_sq[:, 2, :], start=False, stop=True)
                mm(ps[:, 7, 0:T1], con("ones128"), lat_sq[:, 0, :], start=True, stop=True).then_inc(mla_ss.sem, 1)
                krope = pj[0:ROPE, MISC, :]
                mm(ps[:, 4, 0:T1], con("rep", rows=slice(0, ROPE)), krope, start=True, stop=True)
                mm(ps[:, 5, 0:T1], con("reprot", rows=slice(0, ROPE)), krope, start=True, stop=True)\
                    .then_inc(kr_raw.sem, 1)
                for i in range(6, 12):
                    block(i)
                pe.wait_ge(cqn_ready.sem, cqn_ready.at(l, 1))
                pe.wait_ge(kr_ready.sem, kr_ready.at(l, 1))
                for b, bank in enumerate((6, 7, 4)):
                    for k in range(2):
                        c = P1["uq"] + 384 * k + P * b
                        last = mm(ps[:, bank, 0:T1], prm[:, c:c + P], cqn[:, k, :], start=k == 0, stop=k == 1)
                last.then_inc(uq_done.sem, 1)
                for i in range(12, 13):
                    block(i)
                pe.wait_ge(ckvn_ready.sem, ckvn_ready.at(l, 1))
                pe.wait_ge(qn_ready.sem, qn_ready.at(l, 1))
                for b in range(2):
                    c = P1["ukv"] + P * b
                    mm(ps[:, 6 + b, 0:T1], prm[:, c:c + P], cqn[:, 2, :], start=True, stop=True)
                for i, (t, n) in enumerate(TILES):
                    c = P1["ukv"] + 2 * P
                    dst = ps[0:n, 5, 256 * i:256 * i + 256] if i < 2 else ps[0:n, 4, 0:256]
                    last = mm(dst, cqn[:, 2, t:t + n], prm[:, c:c + 256], start=True, stop=True)
                last.then_inc(ukv_done.sem, 1)
                for i in range(13, 15):
                    block(i)
                pe.wait_ge(kv_ready.sem, kv_ready.at(l, 1))
                pe.wait_ge(rows_ready.sem, rows_ready.at(l, 1))
                mm(ps[:, 6, 0:T1], con("rot"), qraw, start=True, stop=True).then_inc(qrot_done.sem, 1)
                for i, (t, n) in enumerate(TILES):
                    for r, src in enumerate((row_cum, row_sp)):
                        c = (2 * i + r) * 64
                        last = tr(ps[0:n, 7, c:c + 64], src[ROWS, t:t + n], ident[ROWS, ROWS])
                last.then_inc(rows_t.sem, 1)
                for i in range(15, 18):
                    block(i)
                pe.wait_ge(xc_ready.sem, xc_ready.at(l, 1))
                pe.wait_ge(qr_ready.sem, qr_ready.at(l, 1))
                for i, (t, n) in enumerate(TILES):
                    for c in range(4):
                        last = tr(ps[0:n, 4 + i, P * c:P * c + P], xc[:, c, t:t + n], ident)
                last.then_inc(xs_t.sem, 1)
                for i in range(18, 20):
                    block(i)
                pe.wait_ge(proj_scaled.sem, proj_scaled.at(l, IN1 - 2))
                for g in range(2):
                    gr = slice(64 * g, 64 * g + 64)
                    for i, (t, n) in enumerate(TILES):
                        last = mm(tri_bank(g, i), xc[gr, 4, t:t + n], xc[gr, 5, t:T1], start=True, stop=True)
                    last.then_inc(g_ready.sem, 1)
                pe.wait_ge(proj_ready.sem, proj_ready.at(l, IN1))
                pe.wait_ge(tok_ready.sem, tok_ready.at(l, 1))
                for i, (t, n) in enumerate(TILES):
                    for c in range(2):
                        bank, col = (7, 256 * i + P * c) if i < 2 else (6, P * c)
                        last = tr(ps[0:n, bank, col:col + P], pj[:, FV0 + c, t:t + n], ident)
                last.then_inc(vf_t.sem, 1)

                def ssd_d(hh):
                    if hh == 2:
                        pe.wait_ge(vf_ready.sem, vf_ready.at(l, 1))
                    if hh >= 3:
                        pe.wait_ge(decay.sem, decay.at(l, hh - 2))
                    bank = D_BANK[hh % 3]
                    for i, (t, n) in enumerate(TILES):
                        mm(tri_bank(bank, i), con("sel", 12 * P)[:, hh * P:hh * P + n], row_cum[:, t:T1],
                           start=True, stop=False)
                        last = mm(ps[0:n, bank, TRI[i]:TRI[i] + n], ident_bf[:, 0:n], maskS_bf[:, 0:n],
                                  start=False, stop=True)
                    last.then_inc(d_ready.sem, 1)

                def ssd_y(hh):
                    pe.wait_ge(ssd_w.sem, ssd_w.at(l, hh + 1))
                    if hh % 2 == 0 and hh >= 4:
                        pe.wait_ge(yz_ready.sem, yz_ready.at(l, hh // 2 - 1))
                    for i, (t, n) in enumerate(TILES):
                        last = mm(ps[head_rows(hh), 4 + (hh // 2) % 2, t:T1], xtok[0:n, i, HD * hh:HD * hh + HD],
                                  ptr[0:n, hh % 2, TRI[i]:TRI[i] + TRI_W[i]], start=i == 0, stop=i == 2)
                    last.then_inc(y_ready.sem, 1)

                def att_s(n_):
                    if n_ == 1:
                        pe.wait_ge(decay.sem, decay.at(l, 6))
                    if n_ == 2:
                        pe.wait_ge(ssd_w.sem, ssd_w.at(l, 4))
                    if n_ >= 3:
                        pe.wait_ge(exp_done.sem, exp_done.at(l, n_ - 2))
                    bank = S_BANK[n_ % 3]
                    hr = head_rows(n_)
                    for i in (2, 1, 0):
                        t, n = QTILES[i]
                        c, kw = S_COL[i], KEYS[i]
                        dst = ps[0:n, bank, c:c + kw]
                        if n_ < MLA_HEADS:
                            rr = slice(ROPE * n_, ROPE * n_ + ROPE)
                            mm(dst, qn[hr, n_ // 2, t:t + n], kn[hr, n_ // 2, 0:kw], start=True, stop=False)
                            mm(dst, qr[rr, t:t + n], kr[rr, 0:kw], start=False, stop=False)
                        else:
                            hd = n_ - MLA_HEADS
                            mm(dst, pj[hr, FQ0 + hd // 2, t:t + n], pj[hr, FK0 + hd // 2, 0:kw], start=True, stop=False)
                            mm(dst, con("sel", 12 * P)[:, (8 + hd) * P:(8 + hd) * P + n], row_cum[:, 0:kw],
                               start=False, stop=False)
                        last = mm(ps[0:n, bank, c + t:c + kw], ident_bf[:, 0:n], maskA_bf[:, 0:n],
                                  start=False, stop=True)
                    last.then_inc(s_ready.sem, 1)

                def att_t(n_):
                    pe.wait_ge(p_ready.sem, p_ready.at(l, n_ + 1))
                    if n_ >= 2:
                        pe.wait_ge(pt_ready.sem, pt_ready.at(l, n_ - 1))
                    bank, p = 2 + n_ % 2, prob[:, n_ % 3, :]
                    ends = slice(64, P)
                    c1, c2 = S_COL[1], S_COL[2]
                    tr(ps[:, bank, 0:P], p[:, c1:c1 + P], ident)
                    tr(ps[:, bank, P:2 * P], p[:, c2:c2 + P], ident)
                    tr(ps[:, bank, PT_K1:PT_K1 + P], p[:, c2 + P:c2 + 2 * P], ident)
                    tr(ps[0:N_META, bank, PT_META:PT_END1], p[0:N_META, 0:N_META], ident[0:N_META, 0:N_META])
                    tr(ps[0:N_META, bank, PT_END2:PT_W], p[ends, c2 + 2 * P:S_W], ident[ends, ends])
                    tr(ps[0:N_META, bank, PT_END1:PT_END1 + 64], p[ends, c1 + P:c2], ident[ends, ends])\
                        .then_inc(t_ready.sem, 1)

                def att_o(n_):
                    pe.wait_ge(pt_ready.sem, pt_ready.at(l, n_ + 1))
                    pair = n_ // 2
                    if n_ == 2:
                        pe.wait_ge(ystd_ready.sem, ystd_ready.at(l, 1))
                    if n_ == NH - 2:
                        pe.wait_ge(x_ready, (event + 1) * KD + 5)
                    v = vmla if n_ < MLA_HEADS else vfox
                    hd = slice(HD * (n_ % MLA_HEADS), HD * (n_ % MLA_HEADS) + HD)
                    o, p = ps[head_rows(n_), O_BANK[pair], :], ptr[:, n_ % 2, :]
                    t1, t2 = QTILES[1][0], QTILES[2][0]
                    mm(o[:, 0:N_META], v[0:N_META, 0, hd], p[0:N_META, PT_META:PT_END1], start=True, stop=True)
                    mm(o[:, t1:T1], v[:, 0, hd], p[:, 0:2 * P], start=True, stop=False)
                    mm(o[:, t2:T1], v[:, 1, hd], p[:, PT_K1:PT_K1 + P], start=False, stop=False)
                    mm(o[:, t2 - N_META:t2], v[0:N_META, 1, hd], p[0:N_META, PT_END1 + 48:PT_END1 + 64],
                       start=False, stop=False)
                    mm(o[:, T1 - N_META:T1], v[0:N_META, 2, hd], p[0:N_META, PT_W - N_META:PT_W],
                       start=False, stop=True).then_inc(o_ready.sem, 1)

                pe.wait_ge(masks_ready, 1)
                for hh in range(3):
                    ssd_d(hh)
                for hh in range(SSD_HEADS):
                    ssd_y(hh)
                    if hh + 3 < SSD_HEADS:
                        ssd_d(hh + 3)
                    elif hh < SSD_HEADS - 1:
                        att_s(hh + 3 - SSD_HEADS)
                att_s(2)
                pe.wait_ge(sqy_ready.sem, sqy_ready.at(l, 1))
                for g in range(2):
                    for c in range(2):
                        last = mm(ps[:, 4 + g, 0:T1], con("ones256"), ssd_sq[g][:, c, :], start=c == 0, stop=c == 1)
                last.then_inc(yss_ready.sem, 1)
                for n_ in range(NH):
                    att_t(n_)
                    if n_ + 3 < NH:
                        att_s(n_ + 3)
                    att_o(n_)
                pe.wait_ge(x_ready, (event + 1) * KD + (KD - 1))

            def mixer2(l, turn0, event, norm):
                def block(i):
                    if i >= 4:
                        pe.wait_ge(proj2_ready.sem, proj2_ready.at(l, i - 3))
                    narrow_unit(turn0 + i // 4, (i // 2) % 2, i % 2, ps[:, i % 4, 0:T2], T2)

                def att_s(hh):
                    bank = S2_BANK[hh]
                    if hh == 3:
                        pe.wait_ge(exp2_done.sem, exp2_done.at(l, 2))
                    for i in range(2):
                        for j in range(2):
                            dst = ps[:, bank + j, 256 * i:256 * i + T2]
                            mm(dst, pj[head_rows(j), 4 + hh, P * i:P * i + P], pj[head_rows(j), 8 + hh, 0:T2],
                               start=True, stop=False)
                            last = mm(dst, slope_bf[:, hh, :], absd_bf[:, i, :], start=False, stop=True)
                    last.then_inc(s2_ready.sem, 1)

                first_pair(turn0, event, 0, T2)
                rms_mean_square(norm)
                for i in range(2, 6):
                    block(i)
                pe.wait_ge(proj2_ready.sem, proj2_ready.at(l, 4))
                for i in range(2):
                    for c in range(4):
                        last = tr(ps[:, 4 + i, P * c:P * c + P], pj[:, c, P * i:P * i + P], ident)
                last.then_inc(af_t.sem, 1)
                for i in range(6, 8):
                    block(i)
                pe.wait_ge(af_ready.sem, af_ready.at(l, 1))
                for g in range(4):
                    for i in range(2):
                        c = CC["band"] + (2 * g + i) * T2
                        last = mm(ps[head_rows(g), 6, 256 * (g // 2):256 * (g // 2) + T2],
                                  aftok[:, i, 64 * g:64 * g + 64], cst[:, c:c + T2], start=i == 0, stop=i == 1)
                last.then_inc(pm_done.sem, 1)
                for name, bank in (("cs", 7), ("ss", 4)):
                    for b in range(2):
                        for i in range(2):
                            c = CC[name] + i * T2
                            last = mm(ps[:, bank, 256 * b:256 * b + T2], aftok[:, i, 256 + P * b:256 + P * b + P],
                                      cst[:, c:c + T2], start=i == 0, stop=i == 1)
                last.then_inc(uv_done.sem, 1)
                for i in range(8, 10):
                    block(i)
                pe.wait_ge(uv_ready.sem, uv_ready.at(l, 1))
                pe.wait_ge(pm_ready.sem, pm_ready.at(l, 1))
                for b in range(2):
                    dst = ps[:, 6, 256 * b:256 * b + T2]
                    mm(dst, con("ccos"), uu[:, b, :], start=True, stop=False)
                    last = mm(dst, con("csin"), vv[:, b, :], start=False, stop=True)
                last.then_inc(f2_done.sem, 1)
                for g in range(4):
                    c = P2["poolw"] + 64 * (g // 2)
                    last = mm(ps[head_rows(g), 5, 256 * (g // 2):256 * (g // 2) + T2], prm[head_rows(g), c:c + 64],
                              poolm[head_rows(g), g // 2, :], start=True, stop=True)
                last.then_inc(py_done.sem, 1)
                for i in range(10, 12):
                    block(i)
                pe.wait_ge(f2_ready.sem, f2_ready.at(l, 1))
                for b in range(2):
                    for k in range(2):
                        c = P2["fourw"] + 256 * k + P * b
                        last = mm(ps[:, 7, 256 * b:256 * b + T2], prm[:, c:c + P], y4[:, k, :], start=k == 0, stop=k == 1)
                last.then_inc(f3_done.sem, 1)
                for i in range(12, 14):
                    block(i)
                pe.wait_ge(masks_ready, 2)
                pe.wait_ge(four_cat.sem, four_cat.at(l, 1))
                att_s(0)
                for i in range(14, 16):
                    block(i)
                pe.wait_ge(proj2_ready.sem, proj2_ready.at(l, 14))
                att_s(1)
                pe.wait_ge(pool_cat.sem, pool_cat.at(l, 1))
                pe.wait_ge(proj2_ready.sem, proj2_ready.at(l, IN2))
                for i in range(2):
                    for c in range(4):
                        last = tr(ps[:, 4 + i, P * c:P * c + P], pj[:, 12 + c, P * i:P * i + P], ident)
                last.then_inc(v_t.sem, 1)
                att_s(2)

                def att_t(hh):
                    pe.wait_ge(a2_ready.sem, a2_ready.at(l, hh + 1))
                    if hh == 0:
                        pe.wait_ge(v_ready.sem, v_ready.at(l, 1))
                    if hh >= 2:
                        pe.wait_ge(at2_ready.sem, at2_ready.at(l, hh - 1))
                    for i in range(2):
                        for k in range(2):
                            c = 256 * k + P * i
                            last = tr(ps[:, 4 + hh % 2, c:c + P], attn[:, hh % 2, i, P * k:P * k + P], ident)
                    last.then_inc(t2_ready.sem, 1)

                def att_o(hh):
                    pe.wait_ge(at2_ready.sem, at2_ready.at(l, hh + 1))
                    dst = ps[:, 6 + hh // 2, 256 * (hh % 2):256 * (hh % 2) + T2]
                    for k in range(2):
                        last = mm(dst, vtok[:, k, P * hh:P * hh + P], attn_t[:, hh % 2, k, :], start=k == 0, stop=k == 1)
                    last.then_inc(o2_ready.sem, 1)

                def mean_squares(pair):
                    if pair == 0:
                        pe.wait_ge(exp2_done.sem, exp2_done.at(l, 3))
                    pe.wait_ge(o2_sq.sem, o2_sq.at(l, pair + 1))
                    for hh in (2 * pair, 2 * pair + 1):
                        last = mm(ps[:, 2 + pair, 256 * (hh % 2):256 * (hh % 2) + T2], con("ones128"), sqo[:, hh, :],
                                  start=True, stop=True)
                    last.then_inc(o2_ss.sem, 1)

                att_t(0)
                att_s(3)
                for hh in range(1, ATT_HEADS):
                    att_t(hh)
                    att_o(hh - 1)
                mean_squares(0)
                att_o(ATT_HEADS - 1)
                mean_squares(1)

            pe.nop().then_inc(unit_used, START)
            with pe.Fori(0, DEPTH) as l:
                t0, q, e0, r0 = l * TURNS1, l * 2, l * 4, l * 3
                up(q, t0 + SEC1["ffn1"], e0, N1, lambda: None)
                pe.wait_ge(consts_in, 16)
                down(q, t0 + SEC1["ffn1"] + UP_T, r0, T1)
                mean(r0)
                pe.wait_ge(prm_in, l * 16 + 16)
                mixer1(l, t0 + SEC1["in"], e0 + 1)
                out_proj(t0 + SEC1["out"], e0 + 2, r0 + 1, T1)
                mean(r0 + 1)
                up(q + 1, t0 + SEC1["ffn2"], e0 + 3, N1, lambda: variance(l, 1))
                down(q + 1, t0 + SEC1["ffn2"] + UP_T, r0 + 2, T1)
                mean(r0 + 2)
                variance_chunks(l)
            with pe.Fori(0, DEPTH) as l:
                t0, q, e0, r0 = l * TURNS2 + BLOCK2_TURN, l * 2 + 2 * DEPTH, l * 4 + EVENT2, l * 3 + 3 * DEPTH
                up(q, t0 + SEC2["ffn1"], e0, T2, lambda: rms_mean_square(l * 3))
                down(q, t0 + SEC2["ffn1"] + UP_T, r0, T2)
                pe.wait_ge(prm_in, l * 16 + (16 * DEPTH + 16))
                pe.wait_ge(consts_in, 32)
                mixer2(l, t0 + SEC2["in"], e0 + 1, l * 3 + 1)
                out_proj(t0 + SEC2["out"], e0 + 2, r0 + 1, T2)
                up(q + 1, t0 + SEC2["ffn2"], e0 + 3, T2, lambda: rms_mean_square(l * 3 + 2))
                down(q + 1, t0 + SEC2["ffn2"] + UP_T, r0 + 2, T2)
            rms_mean_square(3 * DEPTH)

        @block.scalar
        def _(act):
            fn = nc.scalar.activation

            def hi_unit(j, u, width):
                c = slice(u * width, (u + 1) * width)
                fn(w_hi[:, j, c], raw[:, j, c], ACT.Copy).then_inc(hi_done, 1)

            def split_hi(turn, j, width, wait_slot=True):
                act.wait_ge(raw_landed[j], turn * 16 + 16)
                if wait_slot:
                    act.wait_ge(unit_used, turn * 4 + (2 * j - 2 + START))
                for u in range(2):
                    hi_unit(j, u, width)

            def second_pair(turn, u):
                act.wait_ge(raw_landed[1], turn * 16 + 16)
                act.wait_ge(unit_used, turn * 4 + (u - 1 + START))
                hi_unit(1, u, W_NARROW)

            def load_sqrt():
                fn(small[:, 95:96], con("one", 1), ACT.Sqrt)

            def split_next(turn, j, width):
                split_hi(turn + j, 1 - j, width)

            def up(q, turn0, T, biased):
                def turn(it, next_width):
                    first = isinstance(it, int) and it == 0
                    if first:
                        split_next(turn0, 1, W_NARROW)
                    for j in range(2):
                        if not first:
                            split_next(turn0 + it, j, W_NARROW if j == 0 else next_width)
                        act.wait_ge(gate_ready, q * NF + it * 2 + (j + 1))
                        bias = {"bias": wcol[:, 2 * j:2 * j + 1]} if biased else {}
                        fn(silu[:, j, 0:T], silu[:, j, 0:T], ACT.Silu, **bias).then_inc(silu_done, 1)

                turn(0, W_NARROW)
                with act.Fori(1, UP_T - 1) as it:
                    turn(it, W_NARROW)
                turn(UP_T - 1, W_WIDE)

            def high(table, gain, k, T):
                fn(x_hi[:, k, 0:T], h[:, k, T1 - T:T1], ACT.Identity, scale=par(table, gain, k)).then_inc(xh_ready, 1)

            def square(norm, resid, m, T):
                act.wait_ge(resid_ready, resid * KD + (m + 1 + CREDIT))
                if isinstance(m, int):
                    dst, src = pj[:, KD + m, 0:T], h[:, m, T1 - T:T1]
                else:
                    dst, src = pj[:, bass.ds(m + KD, 1), 0:T], h[:, bass.ds(m, 1), T1 - T:T1]
                fn(dst, src, ACT.Square).then_inc(rms_sq, 1)

            def down(turn0, resid, rms, norm, T, gain=None):
                def turn(it, next_width):
                    for j in range(2):
                        split_next(turn0 + it, j, W_WIDE if j == 0 else next_width)
                        end = next_width == W_NARROW and j == 1
                        if end and rms:
                            for k in range(KD - 1):
                                high(P2, gain, k, T)
                        if end:
                            second_pair(turn0 + DOWN_T, 0)
                            load_sqrt()
                        if rms:
                            square(norm, resid, it * 2 + j, T)
                        if end and rms:
                            high(P2, gain, KD - 1, T)

                with act.Fori(0, DOWN_T - 1) as it:
                    turn(it, W_WIDE)
                turn(DOWN_T - 1, W_NARROW)

            def out_proj(turn0, resid, rms, norm, T, gain=None):
                for p in range(OUTB // 2):
                    if p > 0:
                        split_next(turn0 + p // 2, p % 2, W_NARROW)
                    if p == OUTB // 2 - 1:
                        second_pair(turn0 + OUTB // 4, 0)
                        load_sqrt()
                    if rms:
                        for u in range(2):
                            square(norm, resid, 2 * p + u, T)
                if rms:
                    for k in range(KD):
                        high(P2, gain, k, T)

            def root(number, T, eps):
                act.wait_ge(var_ready, number + 1)
                fn(std[:, 0, 0:T], ps[:, 7, 0:T], ACT.Sqrt, bias=con(eps, 1)).then_inc(std_ready, 1)

            def layer_norm(norm, gain, bias, next_turn):
                fn(x_hi[:, :, T1:N1], par(P1, bias, 0, KD).rearrange("p (k a) -> p k a", a=1).broadcast_to([P, KD, 2]),
                   ACT.Copy)
                for k in range(KD):
                    act.wait_ge(centered, norm * KD + (k + 1))
                    high(P1, gain, k, T1)
                    fn(pj[:, KD + k, :], h[:, k, :], ACT.Square).then_inc(ln_sq, 1)
                second_pair(next_turn, 1)
                root(norm, T1, "eps1")

            def mixer1(l, turn0):
                def pair(p, before=(), between=(), after=()):
                    if p != 1:
                        nxt = max(p + 1, 2)
                        split_hi(turn0 + nxt // 2, nxt % 2, W_NARROW)
                    for step in before:
                        step()
                    for i in (2 * p, 2 * p + 1):
                        act.wait_ge(proj_scaled.sem, proj_scaled.at(l, i + 1))
                        fn(pj[:, i, :], pj[:, i, :], ACT.Identity, bias=wblk[:, i:i + 1]).then_inc(proj_ready.sem, 1)
                        for step in between if i % 2 == 0 else after:
                            step()

                def rows():
                    act.wait_ge(rows_u.sem, rows_u.at(l, 1))
                    fn(row_l[ROWS, :], row_u[ROWS, :], ACT.Abs)
                    act.drain()
                    fn(row_l[ROWS, :], row_l[ROWS, :], ACT.Exp, scale=-1.0)
                    fn(acoef[ROWS, :], par(P1, "alog", rows=ROWS), ACT.Exp)
                    act.drain()
                    fn(row_l[ROWS, :], row_l[ROWS, :], ACT.Ln, bias=con("one", 1, ROWS)).then_inc(rows_ln.sem, 1)

                def latent_squares():
                    act.drain()
                    fn(lat_sq, pj[:, CKV:CKV + 3, :], ACT.Square).then_inc(mla_sq.sem, 1)

                def latent_roots():
                    act.wait_ge(mla_ss.sem, mla_ss.at(l, 1))
                    fn(std[:, :, :], ps[:, 6:8, 0:T1], ACT.Sqrt, bias=con("eps1", 1)).then_inc(mla_std.sem, 1)

                def seeds(c0):
                    act.drain()
                    for c in (c0, c0 + 1):
                        fn(xc[:, c, :], pj[:, XBC0 + c, :], ACT.Identity, bias=par(P1, "convb", c),
                           scale=par(P1, "convw", CONV * c + CONV - 1)).then_inc(conv_seed.sem, 1)

                def queries():
                    act.wait_ge(uq_done.sem, uq_done.at(l, 1))
                    fn(qn, ps[:, 6:8, 0:T1], ACT.Copy)
                    fn(qraw, ps[:, 4, 0:T1], ACT.Copy).then_inc(qn_ready.sem, 1)

                def silus():
                    act.drain()
                    act.wait_ge(conv_done.sem, conv_done.at(l, 1))
                    fn(xc, xc, ACT.Silu)
                    fn(pj[:, Z0:Z0 + 4, :], pj[:, Z0:Z0 + 4, :], ACT.Silu).then_inc(xc_ready.sem, 1)

                pair(0)
                pair(1, after=[latent_squares])
                pair(2, before=[rows])
                pair(3, before=[latent_roots])
                pair(4, before=[lambda: seeds(0)])
                pair(5, before=[lambda: seeds(2)], after=[queries, lambda: seeds(4)])
                pair(6)
                pair(7, between=[silus])
                pair(8)
                pair(9)

                act.wait_ge(tokrow_ready.sem, tokrow_ready.at(l, 1))
                for hh in range(SSD_HEADS):
                    act.wait_ge(d_ready.sem, d_ready.at(l, hh + 1))
                    if hh >= 3:
                        act.wait_ge(ssd_w.sem, ssd_w.at(l, hh - 2))
                    for i, (t, n) in enumerate(TILES):
                        c = slice(TRI[i], TRI[i] + TRI_W[i])
                        last = fn(prob[0:n, hh % 3, c], ps[0:n, D_BANK[hh % 3], c], ACT.Exp,
                                  bias=tok_ncum[0:n, i, hh:hh + 1])
                    last.then_inc(decay.sem, 1)
                split_hi(turn0 + IN1 // 4, 1, W_NARROW)
                act.wait_ge(yz_ready.sem, yz_ready.at(l, 4))
                for g in range(2):
                    last = fn(ssd_sq[g][:], xc[:, 2 * g:2 * g + 2, :], ACT.Square)
                last.then_inc(sqy_ready.sem, 1)

                def exps(n_):
                    act.wait_ge(nm_ready.sem, nm_ready.at(l, n_ + 1))
                    if n_ >= 3:
                        act.wait_ge(t_ready.sem, t_ready.at(l, n_ - 2))
                    s = n_ % 3
                    for i, (t, n) in enumerate(QTILES):
                        c = slice(S_COL[i], S_COL[i] + KEYS[i])
                        last = fn(prob[0:n, s, c], ps[0:n, S_BANK[s], c], ACT.Exp,
                                  bias=nmax[0:n, s, i:i + 1], scale=MLA_SCALE if n_ < MLA_HEADS else FOX_SCALE,
                                  accum_out=asum[0:n, s, i:i + 1])
                    last.then_inc(exp_done.sem, 1)

                def pt_copy(n_):
                    act.wait_ge(t_ready.sem, t_ready.at(l, n_ + 1))
                    if n_ >= 2:
                        act.wait_ge(o_ready.sem, o_ready.at(l, n_ - 1))
                    fn(ptr[:, n_ % 2, 0:PT_META], ps[:, 2 + n_ % 2, 0:PT_META], ACT.Copy)
                    fn(ptr[0:N_META, n_ % 2, PT_META:PT_W], ps[0:N_META, 2 + n_ % 2, PT_META:PT_W], ACT.Copy)\
                        .then_inc(pt_ready.sem, 1)

                def o_high(pair):
                    act.wait_ge(o_ready.sem, o_ready.at(l, 2 * pair + 2))
                    fn(x_hi[:, 4 + pair, 0:T1], ps[:, O_BANK[pair], 0:T1], ACT.Copy).then_inc(cat_hi.sem, 1)

                exps(0)
                exps(1)
                act.wait_ge(yss_ready.sem, yss_ready.at(l, 1))
                fn(std[:, :, :], ps[:, 4:6, 0:T1], ACT.Sqrt, bias=con("eps1", 1)).then_inc(ystd_ready.sem, 1)
                for n_ in range(NH):
                    pt_copy(n_)
                    if n_ + 2 < NH:
                        exps(n_ + 2)
                    if n_ in (2, 4):
                        act.wait_ge(ssd_cat.sem, ssd_cat.at(l, n_ // 2))
                        for k in (n_ - 2, n_ - 1):
                            fn(x_hi[:, k, 0:T1], pj[:, k, :], ACT.Copy).then_inc(cat_hi.sem, 1)
                    if n_ in (4, 5, 6):
                        o_high(n_ - 4)
                o_high(NH // 2 - 1)

            def mixer2(l, turn0):
                def pair(p, *steps):
                    if p != 1:
                        nxt = max(p + 1, 2)
                        split_hi(turn0 + nxt // 2, nxt % 2, W_NARROW)
                    for step in steps:
                        step()

                def halves(bank):
                    return ps[:, bank, :].rearrange("p (a t) -> p a t", a=2)

                def lambda_exp():
                    act.wait_ge(lam_dot.sem, lam_dot.at(l, 1))
                    fn(lam_e, lam_s, ACT.Exp).then_inc(lam_exp.sem, 1)

                def token_major():
                    act.wait_ge(af_t.sem, af_t.at(l, 1))
                    fn(aftok, ps[:, 4:6, :], ACT.Copy).then_inc(af_ready.sem, 1)

                def token_sums():
                    act.wait_ge(uv_done.sem, uv_done.at(l, 1))
                    fn(uu, halves(7), ACT.Copy)
                    fn(vv, halves(4), ACT.Copy).then_inc(uv_ready.sem, 1)

                def feature_sums():
                    act.wait_ge(f2_done.sem, f2_done.at(l, 1))
                    fn(y4, halves(6), ACT.Copy).then_inc(f2_ready.sem, 1)

                def fourier_out():
                    act.wait_ge(f3_done.sem, f3_done.at(l, 1))
                    fn(pj[:, 2:4, 0:T2], halves(7), ACT.Copy).then_inc(four_cat.sem, 1)

                pair(0)
                pair(1, lambda_exp)
                pair(2)
                pair(3, token_major)
                pair(4, token_sums)
                pair(5, feature_sums)
                pair(6, fourier_out)
                pair(7)

                def exps(hh):
                    act.wait_ge(nm2_ready.sem, nm2_ready.at(l, hh + 1))
                    if hh >= 2:
                        act.wait_ge(a2_ready.sem, a2_ready.at(l, hh - 1))
                    s = hh % 2
                    for j in range(2):
                        for i in range(2):
                            c = 2 * j + i
                            last = fn(prob2[:, s, c, :], ps[:, S2_BANK[hh] + j, 256 * i:256 * i + T2], ACT.Exp,
                                      bias=nmax[:, s, c:c + 1], scale=ATT_SCALE, accum_out=asum[:, s, c:c + 1])
                    last.then_inc(exp2_done.sem, 1)

                def at_copy(hh):
                    act.wait_ge(t2_ready.sem, t2_ready.at(l, hh + 1))
                    if hh >= 2:
                        act.wait_ge(o2_ready.sem, o2_ready.at(l, hh - 1))
                    fn(attn_t[:, hh % 2, :, :], halves(4 + hh % 2), ACT.Copy).then_inc(at2_ready.sem, 1)

                def square_o(pair):
                    act.wait_ge(o2_ready.sem, o2_ready.at(l, 2 * pair + 2))
                    fn(sqo[:, 2 * pair:2 * pair + 2, :], halves(6 + pair), ACT.Square).then_inc(o2_sq.sem, 1)

                def root_o(pair):
                    act.wait_ge(o2_ss.sem, o2_ss.at(l, pair + 1))
                    fn(std4[:, 2 * pair:2 * pair + 2, :], halves(2 + pair), ACT.Sqrt, bias=con("eps2", 1))\
                        .then_inc(o2_std.sem, 1)

                def high(k):
                    fn(x_hi[:, k, 0:T2], pj[:, k, 0:T2], ACT.Copy).then_inc(cat2_hi.sem, 1)

                exps(0)
                exps(1)
                act.wait_ge(pool_cat.sem, pool_cat.at(l, 1))
                for k in range(4):
                    high(k)
                exps(2)
                at_copy(0)
                split_hi(turn0 + IN2 // 4, 1, W_NARROW)
                exps(3)
                at_copy(1)
                at_copy(2)
                square_o(0)
                at_copy(3)
                load_sqrt()
                root_o(0)
                square_o(1)
                root_o(1)
                for hh in range(ATT_HEADS):
                    act.wait_ge(att_cat.sem, att_cat.at(l, hh + 1))
                    high(4 + hh)

            split_hi(0, 0, W_NARROW, wait_slot=False)
            act.wait_ge(h_in, 16)
            for k in range(KD):
                fn(x_hi[:, k, 0:T1], h[:, k, :], ACT.Copy).then_inc(xh_first, 1)
            split_hi(0, 1, W_NARROW, wait_slot=False)
            with act.Fori(0, DEPTH) as l:
                t0, q, r0 = l * TURNS1, l * 2, l * 3
                up(q, t0 + SEC1["ffn1"], T1, True)
                act.wait_ge(consts_in, 16)
                down(t0 + SEC1["ffn1"] + UP_T, r0, False, r0, T1)
                act.wait_ge(prm_in, l * 16 + 16)
                layer_norm(r0, "ln1g", "ln1b", t0 + SEC1["in"])
                mixer1(l, t0 + SEC1["in"])
                out_proj(t0 + SEC1["out"], r0 + 1, False, r0 + 1, T1)
                layer_norm(r0 + 1, "ln2g", "ln2b", t0 + SEC1["ffn2"])
                up(q + 1, t0 + SEC1["ffn2"], T1, True)
                down(t0 + SEC1["ffn2"] + UP_T, r0 + 2, False, r0 + 2, T1)
                layer_norm(r0 + 2, "ln3g", "ln3b", t0 + TURNS1)
            for k in range(KD):
                act.wait_ge(h_ready, (3 * DEPTH - 1) * KD + k + 1 + START)
                fn(pj[:, KD + k, 0:T2], h[:, k, T1 - T2:T1], ACT.Square).then_inc(rms_sq, 1)
                high(P1, "firstg", k, T2)
            root(3 * DEPTH, T2, "eps2")
            with act.Fori(0, DEPTH) as l:
                t0, q, r0 = l * TURNS2 + BLOCK2_TURN, l * 2 + 2 * DEPTH, l * 3 + 3 * DEPTH
                n0, s0 = l * 3 + NORM2, l * 3 + 1
                up(q, t0 + SEC2["ffn1"], T2, False)
                act.wait_ge(prm_in, l * 16 + (16 * DEPTH + 16))
                down(t0 + SEC2["ffn1"] + UP_T, r0, True, s0, T2, "mixg")
                second_pair(t0 + SEC2["in"], 1)
                root(n0, T2, "eps2")
                mixer2(l, t0 + SEC2["in"])
                out_proj(t0 + SEC2["out"], r0 + 1, True, s0 + 1, T2, "ffn2g")
                second_pair(t0 + SEC2["ffn2"], 1)
                root(n0 + 1, T2, "eps2")
                up(q + 1, t0 + SEC2["ffn2"], T2, False)
                down(t0 + SEC2["ffn2"] + UP_T, r0 + 2, True, s0 + 2, T2, "nextg")
                second_pair(t0 + TURNS2, 1)
                root(n0 + 2, T2, "eps2")

        @block.vector
        def _(dve):
            v = nc.vector

            def split_lo(turn, j, width):
                for u in range(2):
                    lo_unit(turn, j, u, width)

            def lo_unit(turn, j, u, width):
                dve.wait_ge(hi_done, turn * 4 + (2 * j + u + 1))
                c = slice(u * width, (u + 1) * width)
                v.tensor_tensor(w_lo[:, j, c], raw[:, j, c], w_hi[:, j, c].bitcast(F32), ALU.subtract)\
                    .then_inc(lo_done, 1)

            def split_next(turn, j, width):
                split_lo(turn + j, 1 - j, width)

            def up(q, turn0, T, biased, *last_waits):
                def turn(it, next_width):
                    first = isinstance(it, int) and it == 0
                    if first:
                        split_next(turn0, 1, W_NARROW)
                    for j in range(2):
                        if not first:
                            split_next(turn0 + it, j, W_NARROW if j == 0 else next_width)
                        gate, upb, half = ps[:, 2 * j, :], ps[:, 2 * j + 1, :], prod[:, j, 0:T]
                        bias_gate, bias_up = wcol[:, 2 * j:2 * j + 1], wcol[:, 2 * j + 1:2 * j + 2]
                        dve.wait_ge(unit_used, turn0 * 4 + it * 4 + (2 * j + 1 + START))
                        if biased:
                            v.tensor_copy(bias_gate, gate[:, T:T + 1])
                        v.tensor_tensor(silu[:, j, 0:T], gate[:, 0:T], rstd[:, 0:T], ALU.mult).then_inc(gate_ready, 1)
                        dve.wait_ge(unit_used, turn0 * 4 + it * 4 + (2 * j + 2 + START))
                        if biased:
                            v.tensor_scalar(bias_up, upb[:, T:T + 1], 0.5, None, ALU.mult)
                        v.scalar_tensor_tensor(out=half, in0=upb[:, 0:T], scalar=0.5, in1=rstd[:, 0:T],
                                               op0=ALU.mult, op1=ALU.mult).then_inc(up_free, 1)
                        dve.drain()
                        dve.wait_ge(silu_done, q * NF + it * 2 + (j + 1))
                        if biased:
                            v.scalar_tensor_tensor(out=half, in0=half, scalar=bias_up, in1=silu[:, j, 0:T],
                                                   op0=ALU.add, op1=ALU.mult)
                        else:
                            v.tensor_tensor(half, half, silu[:, j, 0:T], ALU.mult)
                        f = it * 2 + j
                        f = slice(f, f + 1) if isinstance(f, int) else bass.ds(f, 1)
                        src = prod[:, j:j + 1, 0:T]
                        dve.drain()
                        v.tensor_copy(hid_hi[:, f, 0:T], src)
                        dve.drain()
                        v.tensor_tensor(hid_lo[:, f, 0:T], src, hid_hi[:, f, 0:T].bitcast(F32), ALU.subtract)\
                            .then_inc(hid_ready, 1)

                turn(0, W_NARROW)
                with dve.Fori(1, UP_T - 1) as it:
                    turn(it, W_NARROW)
                for semaphore, value in last_waits:
                    dve.wait_ge(semaphore, value)
                turn(UP_T - 1, W_WIDE)

            def low(number, table, gain, k, T):
                dve.wait_ge(xh_ready, number * KD + (k + 1))
                v.scalar_tensor_tensor(out=x_lo[:, k, 0:T], in0=h[:, k, T1 - T:T1], scalar=par(table, gain, k),
                                       in1=x_hi[:, k, 0:T].bitcast(F32), op0=ALU.mult, op1=ALU.subtract)\
                    .then_inc(x_ready, 1)

            def root(number, T):
                dve.wait_ge(std_ready, number + 1)
                last = v.reciprocal(rstd[:, 0:T], std[:, 0, 0:T])
                if T == T1:
                    last.then_inc(rstd_ready, 1)
                dve.drain()

            def resid(alpha, m, bank, T):
                c = slice(m, m + 1) if isinstance(m, int) else bass.ds(m, 1)
                dst = h[:, c, T1 - T:T1]
                v.scalar_tensor_tensor(out=dst, in0=dst, scalar=alpha, in1=ps[:, bank:bank + 1, 0:T],
                                       op0=ALU.mult, op1=ALU.add).then_inc(resid_ready, 1)

            def down(turn0, alpha, T, number=None, gain=None):
                def turn(it, next_width):
                    for j in range(2):
                        split_next(turn0 + it, j, W_WIDE if j == 0 else next_width)
                        end = next_width == W_NARROW and j == 1
                        if end and gain:
                            for k in range(KD - 1):
                                low(number, P2, gain, k, T)
                        if end:
                            lo_unit(turn0 + DOWN_T, 1, 0, W_NARROW)
                        dve.wait_ge(unit_used, turn0 * 4 + it * 4 + (2 * j + 2 + START))
                        resid(alpha, it * 2 + j, 4 + j, T)

                with dve.Fori(0, DOWN_T - 1) as it:
                    turn(it, W_WIDE)
                turn(DOWN_T - 1, W_NARROW)
                if gain:
                    low(number, P2, gain, KD - 1, T)

            def out_proj(turn0, alpha, T, number=None, gain=None):
                for p in range(OUTB // 2):
                    if p > 0:
                        split_next(turn0 + p // 2, p % 2, W_NARROW)
                    for u in range(2):
                        if p == OUTB // 2 - 1 and u == 1:
                            lo_unit(turn0 + OUTB // 4, 1, 0, W_NARROW)
                        dve.wait_ge(unit_used, turn0 * 4 + (2 * p + u + 1 + START))
                        resid(alpha, 2 * p + u, 4 + u, T)
                if gain:
                    for k in range(KD):
                        low(number, P2, gain, k, T)

            def layer_norm(norm, gain, bias, next_turn):
                def centre(k):
                    v.tensor_tensor(h[:, k, :], h[:, k, :], ps[:, 6, 0:T1], ALU.subtract).then_inc(centered, 1)

                dve.wait_ge(mean_ready, norm + 1)
                centre(0)
                centre(1)
                dve.wait_ge(xh_ready, norm * KD + 1)
                v.tensor_tensor(x_lo[:, :, T1:N1],
                                par(P1, bias, 0, KD).rearrange("p (k a) -> p k a", a=1).broadcast_to([P, KD, 2]),
                                x_hi[:, :, T1:N1].bitcast(F32), ALU.subtract)
                for k in range(KD):
                    low(norm, P1, gain, k, T1)
                    if k + 2 < KD:
                        centre(k + 2)
                lo_unit(next_turn, 1, 1, W_NARROW)
                root(norm, T1)

            def cat_low(l, hi, k0, n, T):
                for k in range(k0, k0 + n):
                    dve.wait_ge(hi.sem, hi.at(l, k + 1))
                    v.tensor_tensor(x_lo[:, k, 0:T], pj[:, k, 0:T], x_hi[:, k, 0:T].bitcast(F32), ALU.subtract)\
                        .then_inc(x_ready, 1)

            def mixer1(l, turn0):
                def row_arguments():
                    dve.wait_ge(proj_ready.sem, proj_ready.at(l, MISC + 1))
                    v.tensor_scalar(row_u[ROWS, :], pj[ROWS, MISC, :], par(P1, "rowbias", rows=ROWS),
                                    par(P1, "rowsign", rows=ROWS), ALU.add, ALU.mult).then_inc(rows_u.sem, 1)
                    v.memset(row_cum[0:ROW0, :], 0.0)

                def row_sums():
                    dve.wait_ge(rows_ln.sem, rows_ln.at(l, 1))
                    v.scalar_tensor_tensor(out=row_sp[ROWS, :], in0=row_u[ROWS, :], scalar=0.0, in1=row_l[ROWS, :],
                                           op0=ALU.max, op1=ALU.add)
                    dve.drain()
                    v.tensor_scalar(row_u[ROWS, :], row_sp[ROWS, :], acoef[ROWS, :], -1.0, ALU.mult, ALU.mult)
                    dve.drain()
                    v.tensor_tensor_scan(row_cum[ROWS, :], con("one", 1, ROWS).broadcast_to([P - ROW0, T1]),
                                         row_u[ROWS, :], 0.0, ALU.mult, ALU.add).then_inc(rows_ready.sem, 1)

                def latents(half):
                    if half == 0:
                        dve.wait_ge(mla_std.sem, mla_std.at(l, 1))
                    v.reciprocal(std[:, half, :], std[:, half, :])
                    dve.drain()
                    for b in ((0, 1), (2,))[half]:
                        src, gain = (CQ0 + b, par(P1, "qg", b)) if b < 2 else (CKV, par(P1, "kvg"))
                        last = v.scalar_tensor_tensor(out=cqn[:, b, :], in0=pj[:, src, :], scalar=gain,
                                                      in1=std[:, half, :], op0=ALU.mult, op1=ALU.mult)
                    last.then_inc((cqn_ready, ckvn_ready)[half].sem, 1)

                def rotate(dst, plain, bank, ready):
                    v.tensor_tensor(rot_t[:, 0, :], plain, con("cos", T1), ALU.mult)
                    v.tensor_tensor(rot_t[:, 1, :], ps[:, bank, 0:T1], con("sin", T1), ALU.mult)
                    dve.drain()
                    v.tensor_tensor(dst, rot_t[:, 0, :], rot_t[:, 1, :], ALU.add).then_inc(ready.sem, 1)

                def rotary_key():
                    dve.wait_ge(kr_raw.sem, kr_raw.at(l, 1))
                    rotate(kr, ps[:, 4, 0:T1], 5, kr_ready)

                def keys_values():
                    dve.wait_ge(ukv_done.sem, ukv_done.at(l, 1))
                    v.tensor_copy(kn, ps[:, 6:8, 0:T1])
                    v.tensor_copy(vmla[:, 0:2, :], ps[:, 5, :].rearrange("p (a b) -> p a b", a=2))
                    v.tensor_copy(vmla[0:16, 2, :], ps[0:16, 4, 0:256]).then_inc(kv_ready.sem, 1)

                def rotary_queries():
                    dve.wait_ge(qrot_done.sem, qrot_done.at(l, 1))
                    rotate(qr, qraw, 6, qr_ready)

                def token_rows():
                    dve.wait_ge(rows_t.sem, rows_t.at(l, 1))
                    rows = ps[:, 7, 0:384].rearrange("p (i r c) -> p i r c", i=3, r=2)
                    v.tensor_scalar(tok_ncum[:, 0:2, :], rows[:, 0:2, 0, :], -1.0, None, ALU.mult)
                    v.tensor_scalar(tok_ncum[0:16, 2, :], rows[0:16, 2, 0, :], -1.0, None, ALU.mult)
                    v.tensor_copy(tok_dt[:, 0:2, :], rows[:, 0:2, 1, :])
                    v.tensor_copy(tok_dt[0:16, 2, :], rows[0:16, 2, 1, :]).then_inc(tokrow_ready.sem, 1)

                def token_inputs():
                    dve.wait_ge(xs_t.sem, xs_t.at(l, 1))
                    v.tensor_copy(xtok[:, 0:2, :], ps[:, 4:6, :])
                    v.tensor_copy(xtok[0:16, 2, :], ps[0:16, 6, :]).then_inc(tok_ready.sem, 1)

                def scale(i):
                    dve.wait_ge(unit_used, turn0 * 4 + (i + 1 + START))
                    v.tensor_copy(wblk[:, i:i + 1], ps[:, i % 4, T1:T1 + 1])
                    v.tensor_tensor(pj[:, i, :], ps[:, i % 4, 0:T1], rstd[:], ALU.mult).then_inc(proj_scaled.sem, 1)

                def pair(p, *steps):
                    if p != 1:
                        nxt = max(p + 1, 2)
                        split_lo(turn0 + nxt // 2, nxt % 2, W_NARROW)
                    scale(2 * p)
                    for step in steps:
                        step()
                    scale(2 * p + 1)

                pair(0, row_arguments)
                pair(1)
                pair(2)
                pair(3, row_sums)
                pair(4)
                latents(0)
                rotary_key()
                pair(5)
                latents(1)
                pair(6, keys_values)
                pair(7, rotary_queries, token_rows)
                pair(8)
                token_inputs()
                scale(IN1 - 2)
                scale(IN1 - 1)
                split_lo(turn0 + IN1 // 4, 0, W_NARROW)
                dve.wait_ge(vf_t.sem, vf_t.at(l, 1))
                v.tensor_copy(vfox[:, 0:2, :], ps[:, 7, :].rearrange("p (a b) -> p a b", a=2))
                v.tensor_copy(vfox[0:16, 2, :], ps[0:16, 6, 0:256]).then_inc(vf_ready.sem, 1)

                def gate(c):
                    dve.wait_ge(y_ready.sem, y_ready.at(l, 2 * c + 2))
                    v.scalar_tensor_tensor(out=xc[:, c, :], in0=xc[:, c, :], scalar=par(P1, "dskip", c),
                                           in1=ps[:, 4 + c % 2, 0:T1], op0=ALU.mult, op1=ALU.add)
                    dve.drain()
                    v.tensor_tensor(xc[:, c, :], xc[:, c, :], pj[:, Z0 + c, :], ALU.mult).then_inc(yz_ready.sem, 1)

                dve.drain()
                for hh in range(SSD_HEADS):
                    dve.wait_ge(g_ready.sem, g_ready.at(l, hh // 4 + 1))
                    dve.wait_ge(decay.sem, decay.at(l, hh + 1))
                    if hh >= 2:
                        dve.wait_ge(y_ready.sem, y_ready.at(l, hh - 1))
                    for i, (t, n) in enumerate(TILES):
                        c = slice(TRI[i], TRI[i] + TRI_W[i])
                        last = v.scalar_tensor_tensor(out=ptr[0:n, hh % 2, c], in0=ps[0:n, hh // 4, c],
                                                      scalar=tok_dt[0:n, i, hh:hh + 1], in1=prob[0:n, hh % 3, c],
                                                      op0=ALU.mult, op1=ALU.mult)
                    last.then_inc(ssd_w.sem, 1)
                    if hh % 2 == 1 and hh >= 3:
                        gate(hh // 2 - 1)
                split_lo(turn0 + IN1 // 4, 1, W_NARROW)
                gate(3)

                def maxima(n_):
                    dve.wait_ge(s_ready.sem, s_ready.at(l, n_ + 1))
                    s = n_ % 3
                    for i, (t, n) in enumerate(QTILES):
                        v.reduce_max(amax[0:n, s, i:i + 1], ps[0:n, S_BANK[s], S_COL[i]:S_COL[i] + KEYS[i]], AX_X)
                    dve.drain()
                    v.tensor_scalar(nmax[:, s, 0:3], amax[:, s, 0:3], -(MLA_SCALE if n_ < MLA_HEADS else FOX_SCALE),
                                    None, ALU.mult).then_inc(nm_ready.sem, 1)

                def normalise(n_):
                    dve.wait_ge(exp_done.sem, exp_done.at(l, n_ + 1))
                    s = n_ % 3
                    v.reciprocal(rsum[:, s, 0:3], asum[:, s, 0:3])
                    dve.drain()
                    for i, (t, n) in enumerate(QTILES):
                        p = prob[0:n, s, S_COL[i]:S_COL[i] + KEYS[i]]
                        last = v.tensor_scalar(p, p, rsum[0:n, s, i:i + 1], None, ALU.mult)
                    last.then_inc(p_ready.sem, 1)

                def o_low(pair):
                    dve.wait_ge(cat_hi.sem, cat_hi.at(l, 4 + pair + 1))
                    v.tensor_tensor(x_lo[:, 4 + pair, 0:T1], ps[:, O_BANK[pair], 0:T1],
                                    x_hi[:, 4 + pair, 0:T1].bitcast(F32), ALU.subtract).then_inc(x_ready, 1)

                maxima(0)
                maxima(1)
                normalise(0)
                for n_ in range(NH):
                    if n_ + 2 < NH:
                        maxima(n_ + 2)
                    if n_ + 1 < NH:
                        normalise(n_ + 1)
                    if n_ in (0, 2):
                        g = n_ // 2
                        if g == 0:
                            dve.wait_ge(ystd_ready.sem, ystd_ready.at(l, 1))
                        v.reciprocal(std[:, g, :], std[:, g, :])
                        dve.drain()
                    if n_ in (1, 3):
                        for c in (n_ - 1, n_):
                            last = v.scalar_tensor_tensor(out=pj[:, c, :], in0=xc[:, c, :], scalar=par(P1, "ssdg", c),
                                                          in1=std[:, c // 2, :], op0=ALU.mult, op1=ALU.mult)
                        last.then_inc(ssd_cat.sem, 1)
                    if n_ in (3, 4):
                        cat_low(l, cat_hi, 2 * (n_ - 3), 2, T1)
                    if n_ in (4, 5, 6):
                        o_low(n_ - 4)
                o_low(NH // 2 - 1)

            def mixer2(l, turn0):
                def lambda_dots():
                    v.tensor_tensor(prod[:, 0, 0:128], par(P2, "lamq", 0, 128), par(P2, "lamk", 0, 128), ALU.mult)
                    dve.drain()
                    v.reduce_sum(lam_s, prod[:, 0, 0:128].rearrange("p (a b) -> p a b", a=2), AX_X)\
                        .then_inc(lam_dot.sem, 1)
                    v.tensor_scalar(g_lam, par(P2, "headg", 0, 4), par(P2, "onemlam"), None, ALU.mult)

                def lambda_sum():
                    dve.wait_ge(lam_exp.sem, lam_exp.at(l, 1))
                    v.tensor_scalar(neg_lam, lam_e[:, 1:2], lam_e[:, 0:1], par(P2, "laminit"), ALU.subtract, ALU.subtract)

                def window_means():
                    dve.wait_ge(pm_done.sem, pm_done.at(l, 1))
                    v.tensor_copy(poolm, ps[:, 6, :].rearrange("p (a t) -> p a t", a=2)).then_inc(pm_ready.sem, 1)

                def pool_out():
                    dve.wait_ge(py_done.sem, py_done.at(l, 1))
                    for b in range(2):
                        last = v.tensor_scalar(pj[:, b, 0:T2], ps[:, 5, 256 * b:256 * b + T2], par(P2, "pscale", b), None,
                                               ALU.mult)
                    last.then_inc(pool_cat.sem, 1)

                def maxima(hh):
                    dve.wait_ge(s2_ready.sem, s2_ready.at(l, hh + 1))
                    s, bank = hh % 2, S2_BANK[hh]
                    v.reduce_max(amax[:, s, :], ps[:, bank:bank + 2, :].rearrange("p j (i k) -> p (j i) k", i=2), AX_X)
                    dve.drain()
                    v.tensor_scalar(nmax[:, s, :], amax[:, s, :], -ATT_SCALE, None, ALU.mult).then_inc(nm2_ready.sem, 1)

                def difference(hh):
                    dve.wait_ge(exp2_done.sem, exp2_done.at(l, hh + 1))
                    if hh >= 2:
                        dve.wait_ge(t2_ready.sem, t2_ready.at(l, hh - 1))
                    s = hh % 2
                    v.reciprocal(rsum[:, s, :], asum[:, s, :])
                    dve.drain()
                    v.tensor_scalar(rlam[:, s, :], rsum[:, s, 2:4], neg_lam, None, ALU.mult)
                    for i in range(2):
                        v.tensor_scalar(prob2[:, s, i, :], prob2[:, s, i, :], rsum[:, s, i:i + 1], None, ALU.mult)
                    dve.drain()
                    for i in range(2):
                        last = v.scalar_tensor_tensor(out=attn[:, s, i, :], in0=prob2[:, s, 2 + i, :],
                                                      scalar=rlam[:, s, i:i + 1], in1=prob2[:, s, i, :],
                                                      op0=ALU.mult, op1=ALU.add)
                    last.then_inc(a2_ready.sem, 1)

                def norm_o(hh):
                    if hh % 2 == 0:
                        dve.wait_ge(o2_std.sem, o2_std.at(l, hh // 2 + 1))
                    v.reciprocal(std4[:, hh, :], std4[:, hh, :])
                    dve.drain()
                    v.scalar_tensor_tensor(out=pj[:, 4 + hh, 0:T2],
                                           in0=ps[:, 6 + hh // 2, 256 * (hh % 2):256 * (hh % 2) + T2],
                                           scalar=g_lam[:, hh:hh + 1], in1=std4[:, hh, :],
                                           op0=ALU.mult, op1=ALU.mult).then_inc(att_cat.sem, 1)

                def scale(i):
                    dve.wait_ge(unit_used, turn0 * 4 + (i + 1 + START))
                    v.tensor_tensor(pj[:, i, 0:T2], ps[:, i % 4, 0:T2], rstd[:, 0:T2], ALU.mult)\
                        .then_inc(proj2_ready.sem, 1)

                def pair(p, *steps):
                    if p != 1:
                        nxt = max(p + 1, 2)
                        split_lo(turn0 + nxt // 2, nxt % 2, W_NARROW)
                    scale(2 * p)
                    for step in steps:
                        step()
                    scale(2 * p + 1)

                pair(0, lambda_dots)
                pair(1)
                pair(2, lambda_sum)
                pair(3)
                pair(4, window_means)
                pair(5, pool_out)
                pair(6)
                pair(7, lambda: maxima(0))
                maxima(1)
                difference(0)
                dve.wait_ge(v_t.sem, v_t.at(l, 1))
                v.tensor_copy(vtok, ps[:, 4:6, :]).then_inc(v_ready.sem, 1)
                maxima(2)
                difference(1)
                cat_low(l, cat2_hi, 0, 4, T2)
                maxima(3)
                difference(2)
                difference(3)
                split_lo(turn0 + IN2 // 4, 1, W_NARROW)
                for hh in range(ATT_HEADS):
                    norm_o(hh)
                    if hh > 0:
                        cat_low(l, cat2_hi, 4 + hh - 1, 1, T2)
                cat_low(l, cat2_hi, 4 + ATT_HEADS - 1, 1, T2)

            v.memset(small[:], 1.0)
            dve.nop().then_inc(up_free, CREDIT)
            dve.nop().then_inc(resid_ready, CREDIT)
            v.memset(rstd[:], 1.0)
            zeros = std[:, 0, 0:2 * KD]
            v.memset(zeros, 0.0)
            dve.drain()
            for part in (x_hi, x_lo):
                v.tensor_copy(part[:, :, T1:N1], zeros.rearrange("p (k a) -> p k a", k=KD))
            split_lo(0, 0, W_NARROW)
            dve.wait_ge(h_in, 16)
            for k in range(KD):
                dve.wait_ge(xh_first, k + 1)
                v.tensor_tensor(x_lo[:, k, 0:T1], h[:, k, :], x_hi[:, k, 0:T1].bitcast(F32), ALU.subtract)\
                    .then_inc(x_ready, 1)
            split_lo(0, 1, W_NARROW)
            with dve.Fori(0, DEPTH) as l:
                t0, q, r0 = l * TURNS1, l * 2, l * 3
                up(q, t0 + SEC1["ffn1"], T1, True, (h_ready, l * (3 * KD) + START))
                down(t0 + SEC1["ffn1"] + UP_T, ALPHA, T1)
                dve.wait_ge(prm_in, l * 16 + 16)
                layer_norm(r0, "ln1g", "ln1b", t0 + SEC1["in"])
                dve.wait_ge(consts_in, 16)
                mixer1(l, t0 + SEC1["in"])
                dve.wait_ge(h_ready, l * (3 * KD) + (KD + START))
                out_proj(t0 + SEC1["out"], ALPHA, T1)
                layer_norm(r0 + 1, "ln2g", "ln2b", t0 + SEC1["ffn2"])
                up(q + 1, t0 + SEC1["ffn2"], T1, True, (h_ready, l * (3 * KD) + (2 * KD + START)))
                down(t0 + SEC1["ffn2"] + UP_T, ALPHA, T1)
                layer_norm(r0 + 2, "ln3g", "ln3b", t0 + TURNS1)
            for k in range(KD):
                low(3 * DEPTH, P1, "firstg", k, T2)
            dve.drain().then_inc(prm_free, 1)
            root(3 * DEPTH, T2)
            with dve.Fori(0, DEPTH) as l:
                t0, q = l * TURNS2 + BLOCK2_TURN, l * 2 + 2 * DEPTH
                n0 = l * 3 + NORM2
                up(q, t0 + SEC2["ffn1"], T2, False, (prm_in, l * 16 + (16 * DEPTH + 16)))
                down(t0 + SEC2["ffn1"] + UP_T, 1.0, T2, n0, "mixg")
                lo_unit(t0 + SEC2["in"], 1, 1, W_NARROW)
                root(n0, T2)
                mixer2(l, t0 + SEC2["in"])
                out_proj(t0 + SEC2["out"], 1.0, T2, n0 + 1, "ffn2g")
                lo_unit(t0 + SEC2["ffn2"], 1, 1, W_NARROW)
                root(n0 + 1, T2)
                up(q + 1, t0 + SEC2["ffn2"], T2, False)
                down(t0 + SEC2["ffn2"] + UP_T, 1.0, T2, n0 + 2, "nextg")
                lo_unit(t0 + TURNS2, 1, 1, W_NARROW)
                root(n0 + 2, T2)
                dve.drain().then_inc(prm_free, 1)
            for k in range(KD):
                v.scalar_tensor_tensor(out=pj[:, k, 0:T2], in0=h[:, k, T1 - T2:T1], scalar=par(P2, "nextg", k),
                                       in1=rstd[:, 0:T2], op0=ALU.mult, op1=ALU.mult).then_inc(out_ready, 1)

        @block.gpsimd
        def _(pool):
            def sum_chunks(dst, chunk, ready, before, done, T):
                for k in range(1, KD - 1):
                    pool.wait_ge(ready, before + (k + 1))
                    last = nc.gpsimd.tensor_tensor(dst[:, 0:T], chunk(0) if k == 1 else dst[:, 0:T], chunk(k), ALU.add)
                    if k < KD - 2:
                        pool.drain()
                last.then_inc(done, 1)

            def residual_sums(norm):
                sum_chunks(h_sum, lambda k: h[:, k, :], resid_ready, norm * KD + CREDIT, h_summed, T1)

            def layer_norm_sums(norm):
                sum_chunks(sq_sum, lambda k: pj[:, KD + k, 0:T1], ln_sq, norm * KD, sq_summed, T1)

            def rms_norm_sums(norm):
                sum_chunks(sq_sum, lambda k: pj[:, KD + k, 0:T2], rms_sq, norm * KD, sq_summed, T2)

            def residual(l, n, gain, bias):
                event = l * 4 + (1, 3, 4)[n]
                pool.wait_ge(x_ready, event * KD + KD)
                pool.wait_ge(rstd_ready, l * 3 + (n + 1))
                for k in range(KD):
                    nc.gpsimd.tensor_tensor(h[:, k, :], h[:, k, :], rstd[:], ALU.mult)
                pool.drain()
                for k in range(KD):
                    nc.gpsimd.tensor_scalar(h[:, k, :], h[:, k, :], par(P1, gain, k), par(P1, bias, k), ALU.mult, ALU.add)\
                        .then_inc(h_ready, 1)

            def convolution(l):
                for c0 in (0, 2, 4):
                    pool.wait_ge(conv_seed.sem, conv_seed.at(l, c0 + 2))
                    for d in range(1, CONV):
                        for c in (c0, c0 + 1):
                            tap = par(P1, "convw", CONV * c + CONV - 1 - d).broadcast_to([P, T1 - d])
                            nc.gpsimd.tensor_tensor(prod[:, c - c0, d:T1], pj[:, XBC0 + c, 0:T1 - d], tap, ALU.mult)
                        pool.drain()
                        last = nc.gpsimd.tensor_tensor(xc[:, c0:c0 + 2, d:T1], xc[:, c0:c0 + 2, d:T1],
                                                       prod[:, 0:2, d:T1], ALU.add)
                        pool.drain()
                last.then_inc(conv_done.sem, 1)

            pool.nop().then_inc(h_ready, START)
            pool.wait_ge(hid_ready, 2)
            nc.gpsimd.dma_start(cst[:, 0:CC_FIRST], consts[:, 0:CC_FIRST]).then_inc(consts_in, 16)
            pool.wait_ge(consts_in, 16)
            nc.gpsimd.tensor_copy(masks[:], con("ident", 3 * P)).then_inc(masks_ready, 1)
            with pool.Fori(0, DEPTH) as l:
                nc.gpsimd.dma_start(prm[:, 0:P1_W], prm1[l]).then_inc(prm_in, 16)
                residual_sums(l * 3)
                layer_norm_sums(l * 3)
                residual(l, 0, "ln1g", "ln1b")
                convolution(l)
                residual_sums(l * 3 + 1)
                layer_norm_sums(l * 3 + 1)
                residual(l, 1, "ln2g", "ln2b")
                residual_sums(l * 3 + 2)
                residual(l, 2, "ln3g", "ln3b")
                pool.drain()
            rms_norm_sums(0)
            nc.gpsimd.dma_start(cst[:, CC_FIRST:], consts[:, CC_FIRST:]).then_inc(consts_in, 16)
            pool.wait_ge(consts_in, 32)
            nc.gpsimd.tensor_copy(alibi[:], con("absd", 2 * T2 + ATT_HEADS * P)).then_inc(masks_ready, 1)
            with pool.Fori(0, DEPTH) as l:
                pool.wait_ge(prm_free, l * 1 + 1)
                pool.wait_ge(masks_ready, 2)
                nc.gpsimd.dma_start(prm[:, 0:P2_W], prm2[l]).then_inc(prm_in, 16)
                for n in range(1, 4):
                    rms_norm_sums(l * 3 + n)


def blocks_of(w, n_chunks):
    k, n = w.shape
    return w.reshape(n_chunks, P, n // P, P).transpose(2, 1, 0, 3).reshape(n // P, P, n_chunks * P)


def in_pairs(b):
    n, p, w = b.shape
    return b.reshape(n // 2, 2, p, w).transpose(0, 2, 1, 3).reshape(n // 2, p, 2 * w)


def columns(v):
    return v.reshape(-1, P).T


def kernel(**inputs):
    import concourse.bacc as bacc
    from concourse.bass_utils import run_bass_kernel_spmd

    a = {k: np.asarray(v) for k, v in inputs.items()}
    f32 = np.float32
    ffn = [(s, f, l) for s in ("", "_2") for l in range(DEPTH) for f in ("ffn1", "ffn2")]
    w_up = np.zeros((len(ffn) * NF + PAD_PAIRS, P, 2 * W_NARROW), f32)
    w_down = np.zeros((len(ffn) * KD, P, 2 * W_WIDE), f32)
    for n, (s, f, l) in enumerate(ffn):
        w_up[n * NF:(n + 1) * NF, :, 0:W_NARROW] = blocks_of(a[f"{f}_w_gate{s}"][l], KD)
        w_up[n * NF:(n + 1) * NF, :, W_NARROW:] = blocks_of(a[f"{f}_w_up{s}"][l], KD)
        w_down[n * KD:(n + 1) * KD] = blocks_of(a[f"{f}_w_down{s}"][l], NF)
    hd2 = HD + ROPE
    w_in1, prm1, prm2 = [], np.zeros((DEPTH, P, P1_W), f32), np.zeros((DEPTH, P, P2_W), f32)
    for l in range(DEPTH):
        w = a["w_in"][l]
        z, xbc, dt, fq, fk, fv, fr, cq, ckv, kr = np.split(w, np.cumsum([512, 768, 8, 256, 256, 256, 4, 256, 128])
                                                           .tolist(), axis=1)
        misc = np.zeros((D, P), f32)
        misc[:, 0:ROPE], misc[:, ROW0:ROW0 + 8], misc[:, FROW0:FROW0 + 4] = kr, dt, fr
        w_in1.append(in_pairs(blocks_of(np.concatenate([misc, ckv, cq, xbc, z, fq, fk, fv], axis=1), KD)))

        p = prm1[l]

        def put(table, dst, name, v):
            dst[:, table[name]:table[name] + v.shape[1]] = v

        for name, key in (("ln1g", "ln1_g"), ("ln1b", "ln1_b"), ("ln2g", "ln2_g"), ("ln2b", "ln2_b"), ("ln3g", "ln3_g"),
                          ("ln3b", "ln3_b"), ("convb", "conv_b"), ("ssdg", "ssd_norm_g"), ("qg", "mla_q_norm_g"),
                          ("kvg", "mla_kv_norm_g")):
            put(P1, p, name, columns(a[key][l]))
        put(P1, p, "firstg", columns(a["ffn1_norm_2"][0]))
        put(P1, p, "convw", a["conv_w"][l].reshape(CONV, 6, P).transpose(2, 1, 0).reshape(P, 6 * CONV))
        put(P1, p, "dskip", columns(np.repeat(a["d_skip"][l], HD)))
        p[ROW0:ROW0 + 8, P1["rowbias"]] = a["dt_bias"][l]
        p[FROW0:FROW0 + 4, P1["rowbias"]] = a["fox_f_b"][l]
        p[ROW0:ROW0 + 8, P1["rowsign"]] = 1.0
        p[FROW0:FROW0 + 4, P1["rowsign"]] = -1.0
        p[ROW0:ROW0 + 8, P1["alog"]] = a["a_log"][l]
        uq = a["mla_w_uq"][l].reshape(256, MLA_HEADS, hd2)
        uq = np.concatenate([uq[:, :, :HD].reshape(256, -1), uq[:, :, HD:].reshape(256, -1)], axis=1)
        put(P1, p, "uq", uq.reshape(2, P, 384).transpose(1, 0, 2).reshape(P, -1))
        ukv = a["mla_w_ukv"][l].reshape(P, MLA_HEADS, 2 * HD)
        put(P1, p, "ukv", np.concatenate([ukv[:, :, :HD].reshape(P, -1), ukv[:, :, HD:].reshape(P, -1)], axis=1))

        p = prm2[l]
        last = l == DEPTH - 1
        put(P2, p, "mixg", columns(a["mix_norm_2"][l]))
        put(P2, p, "ffn2g", columns(a["ffn2_norm_2"][l]))
        put(P2, p, "nextg", columns(a["final_norm_2"] if last else a["ffn1_norm_2"][l + 1]))
        put(P2, p, "pscale", columns(a["pool_scale_2"][l]))
        put(P2, p, "headg", columns(a["attn_head_norm_2"][l]))
        lam_init = 0.8 - 0.6 * np.exp(-0.3 * l)
        p[:, P2["laminit"]] = lam_init
        p[:, P2["onemlam"]] = 1.0 - lam_init
        put(P2, p, "lamq", np.broadcast_to(np.concatenate([a["lam_q1_2"][l], a["lam_q2_2"][l]]), (P, 128)))
        put(P2, p, "lamk", np.broadcast_to(np.concatenate([a["lam_k1_2"][l], a["lam_k2_2"][l]]), (P, 128)))
        put(P2, p, "poolw", a["pool_w_2"][l].reshape(2, P, 64).transpose(1, 0, 2).reshape(P, -1))
        put(P2, p, "fourw", a["fourier_w_2"][l].reshape(2, P, 256).transpose(1, 0, 2).reshape(P, -1))
    mixed = np.concatenate([np.arange(512), np.arange(768, 1024), np.arange(512, 768)])
    w_out1 = [in_pairs(blocks_of(a["w_out"][l][mixed], KD)) for l in range(DEPTH)]
    w_in2 = [in_pairs(blocks_of(a["w_in_2"][l], KD)) for l in range(DEPTH)]
    w_out2 = [in_pairs(blocks_of(a["w_out_2"][l], KD)) for l in range(DEPTH)]
    hidden = np.concatenate([a["meta"], a["x"][0]], axis=0)
    arrays = {
        "hidden0": np.ascontiguousarray(hidden.T.reshape(KD, P, T1).transpose(1, 0, 2)),
        "w_up": w_up,
        "w_down": w_down,
        "w_in1": np.concatenate(w_in1),
        "w_out1": np.concatenate(w_out1),
        "w_in2": np.concatenate(w_in2),
        "w_out2": np.concatenate(w_out2),
        "prm1": prm1,
        "prm2": prm2,
        "consts": shape_constants(),
    }
    nc = bacc.Bacc("TRN2", target_bir_lowering=False, num_devices=1)
    args = [nc.dram_tensor(f"in_{n}", v.shape, mybir.dt.from_np(v.dtype), kind="ExternalInput").ap()
            for n, v in arrays.items()]
    args.append(nc.dram_tensor("out_0", (P, KD, T2), F32, kind="ExternalOutput").ap())
    build(nc, *args)
    r = run_bass_kernel_spmd(nc, [{f"in_{n}": v for n, v in arrays.items()}], core_ids=[0])
    y = np.asarray(r.results[0]["out_0"])
    return np.ascontiguousarray(y.transpose(1, 0, 2).reshape(D, T2).T)[None]
```
